# Optimizing a Trainium2 kernel written in Bass

```python
import jax, jax.numpy as jnp
from jax import lax
import numpy as np
import math

D_MODEL = 1024
BATCH = 1
SEQ = 256
DEPTH = 2

GRID_W = 64
CTX_LEN = 256
N_MIXERS = 2
N_HEADS = 16
N_KV_HEADS = 4
HEAD_DIM = D_MODEL // N_HEADS
GROUP = N_HEADS // N_KV_HEADS
Q_DIM = N_HEADS * HEAD_DIM
KV_DIM = N_KV_HEADS * HEAD_DIM
WINDOW = 128
BLOCK = 128
ROPE_THETA = 10000.0
ROPE_QUARTER = HEAD_DIM // 4
CONV_WIDTH = 3
D_FF = 2816
N_MOD = 9
RMS_EPS = 1e-6
NEG_INF = -1e30
HALF_STEP = 0.5


def rmsnorm(x, g):
    xf = x.astype(jnp.float32)
    y = xf * lax.rsqrt(jnp.mean(xf * xf, axis=-1, keepdims=True) + RMS_EPS)
    return (y * g.astype(jnp.float32)).astype(x.dtype)

def adaln_in(x, g, shift, scale):
    return rmsnorm(x, g) * (1 + scale) + shift

def adaln_out(x, y, g, gate, weight):
    return x + weight * gate * rmsnorm(y, g)

def swiglu(h, w_gu, w_down):
    gu = h @ w_gu
    return (jax.nn.silu(gu[..., :D_FF]) * gu[..., D_FF:]) @ w_down

def ffn_sublayer(x, mod, k, g_pre, g_post, w_gu, w_down):
    h = adaln_in(x, g_pre, mod[k], mod[k + 1])
    return adaln_out(x, swiglu(h, w_gu, w_down), g_post, mod[k + 2], HALF_STEP)

def short_conv_mixer(h, w_in, w_conv, w_out):
    bcu = h @ w_in
    b, cg, u = bcu[..., :D_MODEL], bcu[..., D_MODEL:2 * D_MODEL], bcu[..., 2 * D_MODEL:]
    up = jnp.pad(cg * u, ((0, 0), (1, 1), (0, 0)))
    y = w_conv[0] * up[:, :-2] + w_conv[1] * up[:, 1:-1] + w_conv[2] * up[:, 2:]
    return (b * y) @ w_out

def axial_rope_tables(n_tokens, dtype):
    rows = n_tokens // GRID_W
    row = jnp.broadcast_to(jnp.arange(rows)[:, None], (rows, GRID_W)).reshape(-1).astype(jnp.float32)
    col = jnp.broadcast_to(jnp.arange(GRID_W)[None, :], (rows, GRID_W)).reshape(-1).astype(jnp.float32)
    inv_freq = ROPE_THETA ** (-jnp.arange(ROPE_QUARTER, dtype=jnp.float32) / ROPE_QUARTER)
    ang = jnp.stack([row[:, None] * inv_freq, col[:, None] * inv_freq], axis=1)
    return jnp.cos(ang)[:, None].astype(dtype), jnp.sin(ang)[:, None].astype(dtype)

def apply_rope(t, cos, sin):
    t4 = t.reshape(t.shape[:-1] + (2, 2, ROPE_QUARTER))
    x1, x2 = t4[..., 0, :], t4[..., 1, :]
    out = jnp.stack([x1 * cos - x2 * sin, x2 * cos + x1 * sin], axis=-2)
    return out.reshape(t.shape)

def banded_blocks(t, nb):
    B = t.shape[0]
    tp = jnp.pad(t, ((0, 0), (BLOCK, BLOCK), (0, 0), (0, 0)))
    tp = tp.reshape(B, nb + 2, BLOCK, N_KV_HEADS, HEAD_DIM)
    return jnp.concatenate([tp[:, :-2], tp[:, 1:-1], tp[:, 2:]], axis=2)

def band_mask(nb, n_tokens):
    a = jnp.arange(BLOCK)[:, None]
    b = jnp.arange(3 * BLOCK)[None, :]
    off = b - a
    in_win = (off >= BLOCK - WINDOW) & (off <= BLOCK + WINDOW)
    key_pos = (jnp.arange(nb)[:, None] - 1) * BLOCK + b
    valid = (key_pos >= 0) & (key_pos < n_tokens)
    return in_win[None] & valid[:, None, :]

def window_attention_mixer(hx, hz, w_qkv, w_o, sink, cos, sin, ctx_queries):
    B, S, _ = hx.shape
    C = hz.shape[1]
    nb = S // BLOCK
    nk = 3 * BLOCK
    scale = HEAD_DIM ** -0.5
    qkv = hx @ w_qkv
    q = apply_rope(qkv[..., :Q_DIM].reshape(B, S, N_HEADS, HEAD_DIM), cos, sin) * scale
    k = apply_rope(qkv[..., Q_DIM:Q_DIM + KV_DIM].reshape(B, S, N_KV_HEADS, HEAD_DIM), cos, sin)
    v = qkv[..., Q_DIM + KV_DIM:].reshape(B, S, N_KV_HEADS, HEAD_DIM)
    kvz = hz @ w_qkv[:, Q_DIM:]
    kz = kvz[..., :KV_DIM].reshape(B, C, N_KV_HEADS, HEAD_DIM)
    vz = kvz[..., KV_DIM:].reshape(B, C, N_KV_HEADS, HEAD_DIM)
    sink_l = sink.reshape(N_KV_HEADS, GROUP).astype(jnp.float32)

    qb = q.reshape(B, nb, BLOCK, N_KV_HEADS, GROUP, HEAD_DIM)
    kb = banded_blocks(k, nb)
    vb = banded_blocks(v, nb)
    s_win = jnp.einsum('bnqhgd,bnkhd->bnhgqk', qb, kb).astype(jnp.float32)
    s_win = jnp.where(band_mask(nb, S)[None, :, None, None], s_win, NEG_INF)
    s_ctx = jnp.einsum('bnqhgd,bchd->bnhgqc', qb, kz).astype(jnp.float32)
    s_sink = jnp.broadcast_to(sink_l[None, None, :, :, None, None], s_win.shape[:-1] + (1,))
    p = jax.nn.softmax(jnp.concatenate([s_win, s_ctx, s_sink], axis=-1), axis=-1).astype(v.dtype)
    o = (jnp.einsum('bnhgqk,bnkhd->bnqhgd', p[..., :nk], vb)
         + jnp.einsum('bnhgqc,bchd->bnqhgd', p[..., nk:nk + C], vz))
    yx = o.reshape(B, S, Q_DIM) @ w_o

    yz = None
    if ctx_queries:
        qz = (hz @ w_qkv[:, :Q_DIM]).reshape(B, C, N_KV_HEADS, GROUP, HEAD_DIM) * scale
        sz = jnp.einsum('bqhgd,bkhd->bhgqk', qz, kz).astype(jnp.float32)
        sz_sink = jnp.broadcast_to(sink_l[None, :, :, None, None], sz.shape[:-1] + (1,))
        pz = jax.nn.softmax(jnp.concatenate([sz, sz_sink], axis=-1), axis=-1).astype(vz.dtype)
        oz = jnp.einsum('bhgqk,bkhd->bqhgd', pz[..., :C], vz)
        yz = oz.reshape(B, C, Q_DIM) @ w_o
    return yx, yz

def first_inputs(seed: int = 0) -> dict:
    key = jax.random.key(seed)
    ks = jax.random.split(key, 16)
    n_conv = (DEPTH + 1) // N_MIXERS
    n_attn = DEPTH // N_MIXERS

    def w(k, shape, fan_in, gain=1.0):
        return gain * fan_in ** -0.5 * jax.random.normal(k, shape, jnp.float32)

    return {
        'x': jax.random.normal(ks[0], (BATCH, SEQ, D_MODEL), jnp.float32),
        'c': jax.random.normal(ks[1], (BATCH, D_MODEL), jnp.float32),
        'ctx': jax.random.normal(ks[2], (BATCH, CTX_LEN, D_MODEL), jnp.float32),
        'c_ctx': jax.random.normal(ks[3], (D_MODEL,), jnp.float32),
        'w_mod': w(ks[4], (DEPTH, D_MODEL, N_MOD * D_MODEL), D_MODEL, 0.5),
        'b_mod': 0.02 * jax.random.normal(ks[5], (DEPTH, N_MOD * D_MODEL), jnp.float32),
        'norm_g': 1.0 + 0.05 * jax.random.normal(ks[6], (DEPTH, 6, D_MODEL), jnp.float32),
        'ffn_w_gu': w(ks[7], (DEPTH, 2, D_MODEL, 2 * D_FF), D_MODEL),
        'ffn_w_down': w(ks[8], (DEPTH, 2, D_FF, D_MODEL), D_FF),
        'conv_w_in': w(ks[9], (n_conv, D_MODEL, 3 * D_MODEL), D_MODEL),
        'conv_w': w(ks[10], (n_conv, CONV_WIDTH, D_MODEL), CONV_WIDTH),
        'conv_w_out': w(ks[11], (n_conv, D_MODEL, D_MODEL), D_MODEL),
        'attn_w_qkv': w(ks[12], (n_attn, D_MODEL, Q_DIM + 2 * KV_DIM), D_MODEL),
        'attn_w_o': w(ks[13], (n_attn, Q_DIM, D_MODEL), Q_DIM),
        'attn_sink': 0.5 * jax.random.normal(ks[14], (n_attn, N_HEADS), jnp.float32),
    }

def first_block(x, c, ctx, c_ctx, w_mod, b_mod, norm_g, ffn_w_gu, ffn_w_down,
              conv_w_in, conv_w, conv_w_out, attn_w_qkv, attn_w_o, attn_sink):
    B, S, D = x.shape
    cos, sin = axial_rope_tables(S, x.dtype)
    z = ctx
    for i in range(DEPTH):
        last = i == DEPTH - 1
        use_attn = (i % N_MIXERS) == 1
        j = i // N_MIXERS
        g = norm_g[i]
        mx = (jax.nn.silu(c) @ w_mod[i] + b_mod[i]).reshape(B, N_MOD, 1, D).transpose(1, 0, 2, 3)
        mz = (jax.nn.silu(c_ctx) @ w_mod[i] + b_mod[i]).reshape(N_MOD, D)
        ctx_needed = (not last) or use_attn

        x = ffn_sublayer(x, mx, 0, g[0], g[1], ffn_w_gu[i, 0], ffn_w_down[i, 0])
        if ctx_needed:
            z = ffn_sublayer(z, mz, 0, g[0], g[1], ffn_w_gu[i, 0], ffn_w_down[i, 0])

        hx = adaln_in(x, g[2], mx[3], mx[4])
        if use_attn:
            hz = adaln_in(z, g[2], mz[3], mz[4])
            yx, yz = window_attention_mixer(hx, hz, attn_w_qkv[j], attn_w_o[j], attn_sink[j],
                                            cos, sin, not last)
        else:
            yx = short_conv_mixer(hx, conv_w_in[j], conv_w[j], conv_w_out[j])
            yz = None
            if not last:
                hz = adaln_in(z, g[2], mz[3], mz[4])
                yz = short_conv_mixer(hz, conv_w_in[j], conv_w[j], conv_w_out[j])
        x = adaln_out(x, yx, g[3], mx[5], 1.0)

        x = ffn_sublayer(x, mx, 6, g[4], g[5], ffn_w_gu[i, 1], ffn_w_down[i, 1])
        if not last:
            z = adaln_out(z, yz, g[3], mz[5], 1.0)
            z = ffn_sublayer(z, mz, 6, g[4], g[5], ffn_w_gu[i, 1], ffn_w_down[i, 1])
    return x


GROUP_WIDTH = 256
MIX_WIDTH = 4 * GROUP_WIDTH
Q_BLOCK = 128
EPS = 1e-6

A_HEADS = 4
A_HEAD_DIM = 64
IDX_HEADS = 8
IDX_DIM = 32
TOPK_MAX = 256
REL_BUCKETS = 32
REL_MAX_DIST = 128

B_HEADS = 4
B_KEY_DIM = 32
B_VAL_DIM = 64
B_GATE_RANK = 16
B_GATE_TAU = 16.0
B_CHUNK = 64

C_CHANNELS = 256
C_KERNEL = 31

D_HEADS = 4
D_Q_RANK = 256
D_KV_RANK = 128
D_NOPE = 64
D_ROPE = 32
D_V = 64
D_QK = D_NOPE + D_ROPE

IN_WIDTHS = (
    A_HEADS * A_HEAD_DIM, A_HEADS * A_HEAD_DIM, A_HEADS * A_HEAD_DIM,
    IDX_HEADS * IDX_DIM, IDX_DIM, IDX_HEADS,
    B_HEADS * B_KEY_DIM, B_HEADS * B_KEY_DIM, B_HEADS * B_VAL_DIM,
    B_GATE_RANK, B_HEADS * B_VAL_DIM,
    2 * C_CHANNELS,
    D_Q_RANK, D_KV_RANK, D_ROPE,
)
IN_WIDTH = sum(IN_WIDTHS)


def rmsnorm_2(x, g):
    x32 = x.astype(jnp.float32)
    y = x32 * lax.rsqrt(jnp.mean(x32 * x32, axis=-1, keepdims=True) + EPS)
    return (y * g.astype(jnp.float32)).astype(x.dtype)

def swiglu_2(x, w_gate, w_up, w_down):
    return (jax.nn.silu(x @ w_gate) * (x @ w_up)) @ w_down

def t5_bucket(dist):
    max_exact = REL_BUCKETS // 2
    d = jnp.maximum(dist, 0)
    df = jnp.maximum(d, 1).astype(jnp.float32)
    large = max_exact + (jnp.log(df / max_exact) / math.log(REL_MAX_DIST / max_exact)
                         * (REL_BUCKETS - max_exact)).astype(jnp.int32)
    large = jnp.minimum(large, REL_BUCKETS - 1)
    return jnp.where(d < max_exact, d, large)

def rope(x, pos):
    half = x.shape[-1] // 2
    freqs = ROPE_THETA ** (-jnp.arange(half, dtype=jnp.float32) / half)
    ang = pos.astype(jnp.float32)[:, None] * freqs[None, :]
    cos = jnp.cos(ang)[:, None, :]
    sin = jnp.sin(ang)[:, None, :]
    x32 = x.astype(jnp.float32)
    x1, x2 = x32[..., :half], x32[..., half:]
    return jnp.concatenate([x1 * cos - x2 * sin, x2 * cos + x1 * sin], axis=-1).astype(x.dtype)

def dsa_mixer(q, k, v, iq, ik, iw, g_q, g_k, rel_bias):
    bsz, L = q.shape[0], q.shape[1]
    topk = min(TOPK_MAX, L // 4)
    q = rmsnorm_2(q, g_q)
    k = rmsnorm_2(k, g_k)
    scale = A_HEAD_DIM ** -0.5
    idx_scale = IDX_DIM ** -0.5
    w = iw.astype(jnp.float32) * (IDX_HEADS ** -0.5)
    key_pos = jnp.arange(L)

    def block(i):
        t0 = i * Q_BLOCK
        qb = lax.dynamic_slice_in_dim(q, t0, Q_BLOCK, axis=1)
        iqb = lax.dynamic_slice_in_dim(iq, t0, Q_BLOCK, axis=1)
        wb = lax.dynamic_slice_in_dim(w, t0, Q_BLOCK, axis=1)
        qpos = t0 + jnp.arange(Q_BLOCK)
        causal = key_pos[None, :] <= qpos[:, None]
        s = jax.nn.relu(jnp.einsum('bthd,bsd->bths', iqb, ik).astype(jnp.float32) * idx_scale)
        score = jnp.einsum('bths,bth->bts', s, wb)
        score = jnp.where(causal[None], score, -jnp.inf)
        _, sel = lax.top_k(score, topk)
        ks = jax.vmap(lambda kb, ib: kb[ib])(k, sel)
        vs = jax.vmap(lambda vb, ib: vb[ib])(v, sel)
        valid = sel <= qpos[None, :, None]
        bias = rel_bias[t5_bucket(qpos[None, :, None] - sel)]
        logits = (jnp.einsum('bthd,btkhd->bthk', qb, ks).astype(jnp.float32) * scale
                  + jnp.swapaxes(bias, 2, 3).astype(jnp.float32))
        logits = jnp.where(valid[:, :, None, :], logits, -jnp.inf)
        p = jax.nn.softmax(logits, axis=-1)
        return jnp.einsum('bthk,btkhd->bthd', p.astype(v.dtype), vs)

    out = lax.map(block, jnp.arange(L // Q_BLOCK))
    return jnp.moveaxis(out, 0, 1).reshape(bsz, L, A_HEADS * A_HEAD_DIM)

def gla_mixer(q, k, v, g_lat, r, w_gate_up, b_gate, g_out):
    bsz, L = q.shape[0], q.shape[1]
    f32 = jnp.float32
    log_a = jax.nn.log_sigmoid((g_lat @ w_gate_up + b_gate).astype(f32)) / B_GATE_TAU
    log_a = log_a.reshape(bsz, L, B_HEADS, B_KEY_DIM)
    qf = q.astype(f32) * (B_KEY_DIM ** -0.5)
    kf = k.astype(f32)
    vf = v.astype(f32)
    n = L // B_CHUNK

    def to_chunks(t):
        return jnp.moveaxis(t.reshape(bsz, n, B_CHUNK, t.shape[2], t.shape[3]), 1, 0)

    tri = jnp.tril(jnp.ones((B_CHUNK, B_CHUNK), dtype=bool))

    def step(S, inp):
        qc, kc, vc, gc = inp
        b = jnp.cumsum(gc, axis=1)
        o_inter = jnp.einsum('bchk,bhkv->bchv', qc * jnp.exp(b), S)
        diff = b[:, :, None] - b[:, None, :]
        decay = jnp.exp(jnp.where(tri[None, :, :, None, None], diff, -jnp.inf))
        A = jnp.einsum('bihk,bjhk,bijhk->bhij', qc, kc, decay)
        o_intra = jnp.einsum('bhij,bjhv->bihv', A, vc)
        b_last = b[:, -1]
        k_dec = kc * jnp.exp(b_last[:, None] - b)
        S = jnp.exp(b_last)[..., None] * S + jnp.einsum('bchk,bchv->bhkv', k_dec, vc)
        return S, o_inter + o_intra

    S0 = jnp.zeros((bsz, B_HEADS, B_KEY_DIM, B_VAL_DIM), f32)
    _, o = lax.scan(step, S0, (to_chunks(qf), to_chunks(kf), to_chunks(vf), to_chunks(log_a)))
    o = jnp.moveaxis(o, 0, 1).reshape(bsz, L, B_HEADS, B_VAL_DIM)
    o = rmsnorm_2(o, g_out).reshape(bsz, L, B_HEADS * B_VAL_DIM)
    return (o * jax.nn.silu(r.astype(f32))).astype(q.dtype)

def conv_mixer(u, w_dw, b_dw, g_norm):
    a, gate = jnp.split(u, 2, axis=-1)
    h = a * jax.nn.sigmoid(gate)
    h = lax.conv_general_dilated(h, w_dw.astype(h.dtype), window_strides=(1,),
                                 padding=[(C_KERNEL - 1, 0)],
                                 dimension_numbers=('NWC', 'WIO', 'NWC'),
                                 feature_group_count=C_CHANNELS) + b_dw
    return jax.nn.silu(rmsnorm_2(h, g_norm))

def mla_mixer(c_q, c_kv, k_pe, g_qa, w_uq, g_kva, w_ukv, g_q, g_k, pos):
    bsz, L = c_q.shape[0], c_q.shape[1]
    q = (rmsnorm_2(c_q, g_qa) @ w_uq).reshape(bsz, L, D_HEADS, D_QK)
    kv = (rmsnorm_2(c_kv, g_kva) @ w_ukv).reshape(bsz, L, D_HEADS, D_NOPE + D_V)
    k_nope, v = kv[..., :D_NOPE], kv[..., D_NOPE:]
    k = jnp.concatenate([k_nope, jnp.broadcast_to(k_pe[:, :, None, :], (bsz, L, D_HEADS, D_ROPE))], axis=-1)
    q = rmsnorm_2(q, g_q)
    k = rmsnorm_2(k, g_k)
    q = jnp.concatenate([q[..., :D_NOPE], rope(q[..., D_NOPE:], pos)], axis=-1)
    k = jnp.concatenate([k[..., :D_NOPE], rope(k[..., D_NOPE:], pos)], axis=-1)
    scale = D_QK ** -0.5
    key_pos = jnp.arange(L)

    def block(i):
        t0 = i * Q_BLOCK
        qb = lax.dynamic_slice_in_dim(q, t0, Q_BLOCK, axis=1)
        qpos = t0 + jnp.arange(Q_BLOCK)
        causal = key_pos[None, :] <= qpos[:, None]
        logits = jnp.einsum('bthd,bshd->bhts', qb, k).astype(jnp.float32) * scale
        logits = jnp.where(causal[None, None], logits, -jnp.inf)
        p = jax.nn.softmax(logits, axis=-1)
        return jnp.einsum('bhts,bshd->bthd', p.astype(v.dtype), v)

    out = lax.map(block, jnp.arange(L // Q_BLOCK))
    return jnp.moveaxis(out, 0, 1).reshape(bsz, L, D_HEADS * D_V)

def hybrid_layer(x, ffn1_norm, ffn1_gate, ffn1_up, ffn1_down, mix_norm, w_in,
                 a_q_norm, a_k_norm, rel_bias, b_gate_up, b_gate_bias, b_out_norm,
                 c_dw_w, c_dw_b, c_norm, d_qa_norm, d_uq, d_kva_norm, d_ukv, d_q_norm, d_k_norm,
                 w_out, ffn2_norm, ffn2_gate, ffn2_up, ffn2_down, pos):
    bsz, L = x.shape[0], x.shape[1]
    x = x + 0.5 * swiglu_2(rmsnorm_2(x, ffn1_norm), ffn1_gate, ffn1_up, ffn1_down)

    z = rmsnorm_2(x, mix_norm) @ w_in
    (aq, ak, av, iq, ik, iw, bq, bk, bv, bg, br, cu, dcq, dckv, dkpe) = jnp.split(
        z, np.cumsum(IN_WIDTHS)[:-1].tolist(), axis=-1)

    y_a = dsa_mixer(aq.reshape(bsz, L, A_HEADS, A_HEAD_DIM), ak.reshape(bsz, L, A_HEADS, A_HEAD_DIM),
                    av.reshape(bsz, L, A_HEADS, A_HEAD_DIM), iq.reshape(bsz, L, IDX_HEADS, IDX_DIM),
                    ik, iw, a_q_norm, a_k_norm, rel_bias)
    y_b = gla_mixer(bq.reshape(bsz, L, B_HEADS, B_KEY_DIM), bk.reshape(bsz, L, B_HEADS, B_KEY_DIM),
                    bv.reshape(bsz, L, B_HEADS, B_VAL_DIM), bg, br, b_gate_up, b_gate_bias, b_out_norm)
    y_c = conv_mixer(cu, c_dw_w, c_dw_b, c_norm)
    y_d = mla_mixer(dcq, dckv, dkpe, d_qa_norm, d_uq, d_kva_norm, d_ukv, d_q_norm, d_k_norm, pos)

    y = jnp.concatenate([y_a, y_b.astype(x.dtype), y_c.astype(x.dtype), y_d], axis=-1) @ w_out
    x = x + y

    x = x + 0.5 * swiglu_2(rmsnorm_2(x, ffn2_norm), ffn2_gate, ffn2_up, ffn2_down)
    return x

def second_inputs(seed: int = 0) -> dict:
    key = jax.random.key(seed)
    ks = iter(jax.random.split(key, 40))
    f32 = jnp.float32

    def w(shape, fan_in):
        return jax.random.normal(next(ks), shape, f32) * (fan_in ** -0.5)

    def gain(shape):
        return 1.0 + 0.05 * jax.random.normal(next(ks), shape, f32)

    def small(shape, s):
        return s * jax.random.normal(next(ks), shape, f32)

    Ld = DEPTH
    return {
        "x": jax.random.normal(next(ks), (BATCH, SEQ, D_MODEL), f32),
        "ffn1_norm": gain((Ld, D_MODEL)),
        "ffn1_gate": w((Ld, D_MODEL, D_FF), D_MODEL),
        "ffn1_up": w((Ld, D_MODEL, D_FF), D_MODEL),
        "ffn1_down": w((Ld, D_FF, D_MODEL), D_FF),
        "mix_norm": gain((Ld, D_MODEL)),
        "w_in": w((Ld, D_MODEL, IN_WIDTH), D_MODEL),
        "a_q_norm": gain((Ld, A_HEAD_DIM)),
        "a_k_norm": gain((Ld, A_HEAD_DIM)),
        "rel_bias": small((REL_BUCKETS, A_HEADS), 0.2),
        "b_gate_up": w((Ld, B_GATE_RANK, B_HEADS * B_KEY_DIM), B_GATE_RANK),
        "b_gate_bias": small((Ld, B_HEADS * B_KEY_DIM), 0.1),
        "b_out_norm": gain((Ld, B_VAL_DIM)),
        "c_dw_w": w((Ld, C_KERNEL, 1, C_CHANNELS), C_KERNEL),
        "c_dw_b": small((Ld, C_CHANNELS), 0.02),
        "c_norm": gain((Ld, C_CHANNELS)),
        "d_qa_norm": gain((Ld, D_Q_RANK)),
        "d_uq": w((Ld, D_Q_RANK, D_HEADS * D_QK), D_Q_RANK),
        "d_kva_norm": gain((Ld, D_KV_RANK)),
        "d_ukv": w((Ld, D_KV_RANK, D_HEADS * (D_NOPE + D_V)), D_KV_RANK),
        "d_q_norm": gain((Ld, D_QK)),
        "d_k_norm": gain((Ld, D_QK)),
        "w_out": w((Ld, MIX_WIDTH, D_MODEL), MIX_WIDTH),
        "ffn2_norm": gain((Ld, D_MODEL)),
        "ffn2_gate": w((Ld, D_MODEL, D_FF), D_MODEL),
        "ffn2_up": w((Ld, D_MODEL, D_FF), D_MODEL),
        "ffn2_down": w((Ld, D_FF, D_MODEL), D_FF),
    }

def second_block(x, ffn1_norm, ffn1_gate, ffn1_up, ffn1_down, mix_norm, w_in, a_q_norm, a_k_norm,
              rel_bias, b_gate_up, b_gate_bias, b_out_norm, c_dw_w, c_dw_b, c_norm,
              d_qa_norm, d_uq, d_kva_norm, d_ukv, d_q_norm, d_k_norm, w_out,
              ffn2_norm, ffn2_gate, ffn2_up, ffn2_down):
    pos = jnp.arange(x.shape[1])
    for l in range(DEPTH):
        x = hybrid_layer(x, ffn1_norm[l], ffn1_gate[l], ffn1_up[l], ffn1_down[l], mix_norm[l], w_in[l],
                         a_q_norm[l], a_k_norm[l], rel_bias, b_gate_up[l], b_gate_bias[l], b_out_norm[l],
                         c_dw_w[l], c_dw_b[l], c_norm[l], d_qa_norm[l], d_uq[l], d_kva_norm[l], d_ukv[l],
                         d_q_norm[l], d_k_norm[l], w_out[l], ffn2_norm[l], ffn2_gate[l], ffn2_up[l],
                         ffn2_down[l], pos)
    return x


def setup_inputs(seed=0):
    out = dict(first_inputs(seed))
    for name, value in second_inputs(seed + 1).items():
        if name != "x":
            out[name + "_2"] = value
    return out


def reference(
    x, c, ctx, c_ctx, w_mod, b_mod, norm_g, ffn_w_gu, ffn_w_down, conv_w_in, conv_w, conv_w_out,
    attn_w_qkv, attn_w_o, attn_sink, ffn1_norm_2, ffn1_gate_2, ffn1_up_2, ffn1_down_2,
    mix_norm_2, w_in_2, a_q_norm_2, a_k_norm_2, rel_bias_2, b_gate_up_2, b_gate_bias_2,
    b_out_norm_2, c_dw_w_2, c_dw_b_2, c_norm_2, d_qa_norm_2, d_uq_2, d_kva_norm_2, d_ukv_2,
    d_q_norm_2, d_k_norm_2, w_out_2, ffn2_norm_2, ffn2_gate_2, ffn2_up_2, ffn2_down_2,
):
    x = first_block(
        x, c, ctx, c_ctx, w_mod, b_mod, norm_g, ffn_w_gu, ffn_w_down, conv_w_in, conv_w,
        conv_w_out, attn_w_qkv, attn_w_o, attn_sink,
    )
    return second_block(
        x, ffn1_norm_2, ffn1_gate_2, ffn1_up_2, ffn1_down_2, mix_norm_2, w_in_2, a_q_norm_2,
        a_k_norm_2, rel_bias_2, b_gate_up_2, b_gate_bias_2, b_out_norm_2, c_dw_w_2, c_dw_b_2,
        c_norm_2, d_qa_norm_2, d_uq_2, d_kva_norm_2, d_ukv_2, d_q_norm_2, d_k_norm_2, w_out_2,
        ffn2_norm_2, ffn2_gate_2, ffn2_up_2, ffn2_down_2,
    )


_drawn_inputs = setup_inputs


def setup_inputs(seed=0):
    import zlib

    import numpy as np

    out = dict(_drawn_inputs(seed))
    spreads = {}
    factors = {'attn_sink': 8.0,
     'a_q_norm_2': 8.0,
     'a_k_norm_2': 8.0,
     'b_gate_bias_2': 3.088,
     'b_out_norm_2': 3.081,
     'd_qa_norm_2': 8.0,
     'd_kva_norm_2': 4.753,
     'd_q_norm_2': 8.0,
     'd_k_norm_2': 8.0,
     'rel_bias_2': 2.851}
    for name, (base, spread) in spreads.items():
        noise = np.random.default_rng([zlib.crc32(name.encode()), seed]).standard_normal(out[name].shape)
        drawn = base * np.exp(spread * noise) if base else spread * noise
        out[name] = __import__('jax').numpy.asarray(drawn.astype(out[name].dtype))
    for name, factor in factors.items():
        out[name] = (out[name] * factor).astype(out[name].dtype)
    return out
```

```python
from contextlib import ExitStack

import numpy as np
import concourse.bass as bass
from concourse import mybir

F32 = mybir.dt.float32
F32R = mybir.dt.float32r
U32 = mybir.dt.uint32
ACT = mybir.ActivationFunctionType
ALU = mybir.AluOpType
AXX = mybir.AxisListType.X

P = 128
D = 1024
DC = D // P
T = 256
TT = T // P
DFF = 2816
FC = DFF // P
RAW = 4
SPLIT = 2
EPS = 1e-6
NMOD = 9
NEG = -1.0e30

def out_bank(d):
    return (d + 4) % 8

C_A, C_G = 0, 2
B_Q, B_K, B_V, B_G, B_R = 4, 5, 6, 8, 9
D_Q, D_KV, D_PE = 11, 13, 14
A_Q, A_K, A_V, I_Q, I_K, I_W = 15, 17, 19, 21, 23, 24
N_IN = 25
KTAPS = 31
LEVELS = 6

def make_plan():
    plan = []
    c = dict(unit=0, norm=0, post=0, post_n=0, ffn=0, hid=0, h=0)

    def add(kind, **k):
        plan.append((kind, dict(c) | k))

    def pre(N, coef):
        add("pre", N=N, coef=coef)
        c["norm"] += 1
        c["h"] += DC

    def gu(N):
        add("gu", N=N)
        c["unit"] += 2 * FC
        c["ffn"] += 1
        c["hid"] += FC

    def out(N, nk):
        add("out", N=N, nk=nk)
        c["unit"] += nk

    def post(N, coef):
        add("post", N=N, coef=coef)
        c["norm"] += 1
        c["post"] += 1
        c["post_n"] += 1

    for l in range(2):
        for part in range(3):
            N = T if (l, part) == (1, 2) else 2 * T
            pre(2 * T if (l, part) == (1, 1) else N, (l, part))
            if part != 1:
                gu(N)
                out(N, FC)
            elif l == 0:
                add("conv", N=N)
                c["unit"] += 3 * DC
                c["hid"] += DC
                out(N, DC)
            else:
                add("attn", N=N)
                c["unit"] += 12
                c["hid"] += DC
                out(T, DC)
                N = T
            post(N, (l, part))
    for l in range(2):
        for part in range(3):
            pre(T, (2 + l, part))
            if part != 1:
                gu(T)
                out(T, FC)
            else:
                add("mix", l=l)
                c["unit"] += N_IN + 2
                c["hid"] += DC
                out(T, DC)
            add("add", weight=1.0 if part == 1 else 0.5)
            c["post"] += 1
    return plan, c["unit"], c["post"]


PLAN, UNITS, NPOST = make_plan()
DO = ("mod",)

VEC = {}


def vec_columns():
    at = 0
    for name, n in [("g1", 12 * DC), ("g2", 6 * DC), ("convw", 3 * DC), ("bmod", 2 * NMOD * DC), ("sink", 16)] + [
            (f"{name}{l}", n) for l in range(2) for name, n in
            [("aq", 1), ("ak", 1), ("bg", 1), ("bo", 1), ("cw", 62), ("cb", 2), ("cn", 2), ("dqa", 2), ("dkva", 1),
             ("dq", 1), ("dk", 1)]]:
        VEC[name] = at
        at += n
    return at


NVEC = vec_columns()


def build(nc, xin, wst, wmod, cvec, vecs, ctabs, attabs, mixtabs, bup, relb, onehot, out):
    es = ExitStack()
    with es:
        def sb(name, shape, dt=F32, ctx=es):
            return ctx.enter_context(nc.sbuf_tensor(name, shape, dt))

        sems = {}

        def S(name):
            if name not in sems:
                sems[name] = es.enter_context(nc.semaphore(name))
            return sems[name]

        xT = sb("xT", [P, DC, 2 * T])
        h_hi = sb("h_hi", [P, DC, 2 * T], F32R)
        h_lo = sb("h_lo", [P, DC, 2 * T], F32R)
        raw = sb("raw", [P, RAW, D])
        w_hi = sb("w_hi", [P, SPLIT, D], F32R)
        w_lo = sb("w_lo", [P, SPLIT, D], F32R)
        gt = sb("gt", [P, 2, 2 * T])
        ut = sb("ut", [P, 2, 2 * T])
        sq = sb("sq", [P, 2, 2 * T])
        y0 = sb("y0", [P, 2 * T])
        rt = sb("rt", [P, 2 * T])
        rstd = sb("rstd", [P, 2 * T])
        tabs = sb("tabs", [P, 6 * P + 3 * T])
        vec = sb("vec", [P, vecs.shape[1]])
        cv = sb("cv", [P, DC, 2])
        MOD = sb("MOD", [P, 2, NMOD * DC, 2])
        CA = sb("CA", [P, 2, 3, DC, 2])
        CG = sb("CG", [P, 2, 3, DC, 2])
        epsc = sb("epsc", [P, 1])
        zc = sb("zc", [P, 1])
        stepper = sb("stepper", [P, 2])

        ones, ident, bones64, ones96, permW, permD = (tabs[:, P * i:P * (i + 1)] for i in range(6))
        caus1, caus0, bmask = (tabs[:, 6 * P + T * i:6 * P + T * (i + 1)] for i in range(3))

        biasA = sb("biasA", [P, 4, T])
        bupt = sb("bupt", [16, 2, P])

        with ExitStack() as c1:
            u_hi = sb("u_hi", [P, FC, 2 * T], F32R, c1)
            u_lo = sb("u_lo", [P, FC, 2 * T], F32R, c1)
        with ExitStack() as c1:
            mraw = sb("mraw", [P, RAW, D], F32, c1)
            sqb = sb("sqb", [P, 4, 384], F32, c1)
            rbb = sb("rbb", [32, 4, P], F32, c1)
            oh = sb("oh", [32, 384], F32, c1)
            rl = sb("rl", [32, 4], F32, c1)
        with ExitStack() as c1:
            sb("conv_pad", [P, DC, 2 * T], F32, c1)
            cu = sb("cu", [P, 2, 2, T + 2], F32, c1)
            cy = sb("cy", [P, 2, 2, T], F32, c1)
        with ExitStack() as c1:
            AK = sb("AK", [P, 2, 2 * T], F32, c1)
            AV = sb("AV", [P, 2, 2 * T], F32, c1)
            AQ = sb("AQ", [P, DC, T], F32, c1)
            VV = sb("VV", [P, 4, 2 * P], F32, c1)
            atab = sb("atab", [P, attabs.shape[1]], F32, c1)
            rp1 = sb("rp1", [P, 2, 2, T], F32, c1)
            rp2 = sb("rp2", [P, 2, 2, T], F32, c1)
            sw = sb("sw", [P, 2, 2 * T], F32, c1)
            pw = sb("pw", [P, 2, 2 * T], F32, c1)
            pn = sb("pn", [P, 2, 2 * T], F32, c1)
            PTw = sb("PTw", [P, 2, 4, T], F32, c1)
            aw = sb("aw", [P, 2, 8], F32, c1)
        with ExitStack() as c1:
            Z = sb("Z", [P, N_IN, T], F32, c1)
            mtab = sb("mtab", [P, mixtabs.shape[1]], F32, c1)
            sqm = sb("sqm", [P, 8, T], F32, c1)
            rm = sb("rm", [P, 8 * T], F32, c1)
            cnf = sb("cnf", [P, 3, T], F32, c1)
            cn_hi = sb("cn_hi", [P, 3, T], F32R, c1)
            cn_lo = sb("cn_lo", [P, 3, T], F32R, c1)
            with ExitStack() as c2:
                hp = sb("hp", [P, 2, KTAPS - 1 + T], F32, c2)
                hc = sb("hc", [P, 2, T], F32, c2)
            with ExitStack() as c2:
                OB = sb("OB", [P, 2, T], F32, c2)
                G1, G2 = OB[:, 0, :], OB[:, 1, :]
                EB = sb("EB", [P, LEVELS + 2, T], F32, c2)
                QP = sb("QP", [P, LEVELS + 1, T], F32, c2)
                KP = sb("KP", [P, LEVELS + 1, T], F32, c2)
                AT = sb("AT", [P, 4, T], F32, c2)
                kdT = sb("kdT", [P, TT, P], F32, c2)
                VB = sb("VB", [P, TT, 2 * P], F32, c2)
                ST = sb("ST", [P, 3, 2 * P], F32, c2)
            with ExitStack() as c2:
                DQ = sb("DQ", [P, 4, T], F32, c2)
                DK = sb("DK", [P, 4, T], F32, c2)
                DV = sb("DV", [P, 4, T], F32, c2)
                dt1 = sb("dt1", [P, 4, T], F32, c2)
                QA = sb("QA", [P, 4, T], F32, c2)
                VT = sb("VT", [P, TT, 4, P], F32, c2)
                LG = dt1
                PR = DV
                PTm = sb("PTm", [P, TT, 4, T], F32, c2)
                am = sb("am", [P, 16], F32, c2)
            with ExitStack() as c2:
                RI = sb("RI", [P, 2, T], F32, c2)
                SCI = sb("SCI", [P, T], F32, c2)
                WK = sb("WK", [P, 2, T], F32, c2)
                SEL = sb("SEL", [P, T], F32, c2)
                m8 = sb("m8", [P, 2, 8], F32, c2)
                iw = sb("iw", [P, TT, 8], F32, c2)
        CD, SD, scanm = (mtab[:, T * i:T * (i + 1)] for i in range(3))
        levm = mtab[:, 3 * T:(3 + LEVELS + 1) * T].rearrange("p (l k) -> p l k", l=LEVELS + 1)
        bandW = atab[:, 0:4 * T].rearrange("p (b k) -> p b k", b=2)
        skew = nc.dram_tensor("skew", (P, 4, 384), F32).ap()
        skewed = bass.AP(skew.tensor, 127, [[4 * 384 - 1, P], [384, 4], [1, T]])
        ropeW = [atab[:, 4 * T + T * i:4 * T + T * (i + 1)] for i in range(4)]

        ps = es.enter_context(nc.psum_tensor("ps", [P, 8, 512], F32))

        def unit(b, i):
            return b + 4 * i, b % 4, 16 * (b // 4 + 1) + 16 * i

        def split_hi(act, b, i=0):
            if isinstance(i, int) and b + 4 * i >= UNITS:
                return
            u, s, landed = unit(b, i)
            act.wait_ge(S(f"raw_landed{s}"), landed)
            if not (isinstance(i, int) and b + 4 * i < SPLIT):
                act.wait_ge(S("unit_done"), u - 1)
            act.activation(w_hi[:, s % 2, :], raw[:, s, :], ACT.Copy).then_inc(S("hi_ready"), 1)

        def split_lo(dve, b, i=0):
            if isinstance(i, int) and b + 4 * i >= UNITS:
                return
            u, s, _ = unit(b, i)
            dve.wait_ge(S("hi_ready"), u + 1)
            dve.tensor_tensor(w_lo[:, s % 2, :], raw[:, s, :], w_hi[:, s % 2, :],
                              ALU.subtract).then_inc(S("lo_ready"), 1)

        def tile(pe, s, k, psum, hi, lo, start, stop):
            wh, wl = w_hi[:, s, P * k:P * (k + 1)], w_lo[:, s, P * k:P * (k + 1)]
            pe.matmul(psum, wh, hi, start=start, stop=False)
            pe.matmul(psum, wh, lo, start=False, stop=False)
            return pe.matmul(psum, wl, hi, start=False, stop=stop)

        def in_unit(pe, b, i, bank, N, hi=h_hi, lo=h_lo):
            u, s, _ = unit(b, i)
            pe.wait_ge(S("lo_ready"), u + 1)
            for k in range(DC):
                mm = tile(pe, s % 2, k, ps[:, bank, 0:N], hi[:, k, 0:N], lo[:, k, 0:N], k == 0, k == DC - 1)
            mm.then_inc(S("unit_done"), 1)

        def halves(N):
            return [(v, slice(T * v, T * (v + 1))) for v in range(N // T)]

        def coef(c, t, v):
            l, part = c
            if l < 2:
                return CA[:, l, part, t, v:v + 1], MOD[:, l, 3 * part * DC + t, v:v + 1]
            at = VEC["g2"] + ((l - 2) * 3 + part) * DC + t
            return vec[:, at:at + 1], zc[:, 0:1]

        S_STEP = [0]
        block = es.enter_context(nc.Block())

        @block.sync
        def _(sp):
            for s in range(RAW):
                sp.dma_start(raw[:, s, :], wst[s]).then_inc(S(f"raw_landed{s}"), 16)
            sp.dma_start(xT[:, :, :], xin).then_inc(S("x_loaded"), 16)
            with sp.Fori(1, UNITS // 4) as i:
                for s in range(RAW):
                    sp.wait_ge(S("lo_ready"), 4 * i + (s - 3))
                    sp.dma_start(raw[:, s, :], wst[4 * i + s]).then_inc(S(f"raw_landed{s}"), 16)
            for u in range(UNITS // 4 * 4, UNITS):
                sp.wait_ge(S("lo_ready"), u - 3)
                sp.dma_start(raw[:, u % 4, :], wst[u]).then_inc(S(f"raw_landed{u % 4}"), 16)
            sp.wait_ge(S("x_ready"), DC * NPOST)
            sp.dma_start(out, xT[:, :, 0:T]).then_inc(S("stored"), 16)
            sp.wait_ge(S("stored"), 16)

        @block.tensor
        def _(pe):
            def mod_pe():
                pe.wait_ge(S("cs_ready"), 1)
                with pe.Fori(0, 2 * NMOD * DC // 4) as i:
                    for s in range(RAW):
                        pe.wait_ge(S(f"mod_landed{s}"), 16 * i + 16)
                        for k in range(DC):
                            mm = pe.matmul(ps[:, 0, bass.ds(8 * i + 2 * s, 2)], mraw[:, s, P * k:P * (k + 1)],
                                           cv[:, k, :], start=(k == 0), stop=(k == DC - 1))
                        mm.then_inc(S("mod_done"), 1)

            def stats(c, N):
                for t in range(DC):
                    pe.wait_ge(S("sq_ready"), DC * c["norm"] + t + 1)
                    pe.matmul(ps[:, 4, 0:N], ones, sq[:, t % 2, 0:N], start=(t == 0),
                              stop=(t == DC - 1)).then_inc(S("ss_done"), 1)

            def gu_pe(c):
                N, b = c["N"], c["unit"]
                pe.wait_ge(S("h_ready"), c["h"])
                with pe.Fori(0, FC // 2) as i:
                    for j in range(2):
                        in_unit(pe, b + 2 * j, i, j, N)
                        in_unit(pe, b + 2 * j + 1, i, 2 + j, N)

            def out_pe(c, kind):
                N, b, nk = c["N"], c["unit"], c["nk"]
                hi, lo = (h_hi, h_lo) if kind in ("attn", "mix") else (u_hi, u_lo)

                def one(j, i, k, start, stop):
                    u, s, _ = unit(b + j, i)
                    pe.wait_ge(S("lo_ready"), u + 1)
                    pe.wait_ge(S("ulo_ready"), c["hid"] - nk + k + 3)
                    for d in range(DC):
                        if start and d == 4:
                            pe.wait_ge(S("gated"), c["hid"])
                        mm = tile(pe, s % 2, d, ps[:, out_bank(d), 0:N], hi[:, k, 0:N], lo[:, k, 0:N], start, stop)
                    mm.then_inc(S("unit_done"), 1)

                if kind != "gu":
                    pe.wait_ge(S("gated"), c["hid"])
                for k in range(2):
                    one(k, 0, k, k == 0, False)
                if nk == FC:
                    with pe.Fori(0, (nk - 4) // 4) as i:
                        for j in range(4):
                            one(2 + j, i, 4 * i + (2 + j), False, False)
                    first = 2 + (nk - 4) // 4 * 4
                else:
                    first = 2
                for k in range(first, nk):
                    one(k, 0, k, False, k == nk - 1)

            def conv_pe(c):
                N, b = c["N"], c["unit"]
                pe.wait_ge(S("h_ready"), c["h"])
                for i in range(2):
                    for j in range(4):
                        n = 4 * i + j
                        if n >= 2:
                            pe.wait_ge(S("gated"), c["hid"] + n - 1)
                        for m in range(3):
                            in_unit(pe, b + 12 * i + 3 * j + m, 0, 3 * (j % 2) + m, N)

            def attn_pe(c):
                b, l = c["unit"], 0
                pe.wait_ge(S("h_ready"), c["h"])
                for n in range(12):
                    if n >= 4:
                        pe.wait_ge(S("w_evac"), n - 3)
                    in_unit(pe, b + n, 0, n % 4, 2 * T if n < 4 else T)
                pe.wait_ge(S("w_evac"), 12)
                for n in range(10):
                    src = AK[:, n, 0:T] if n < 2 else AQ[:, n - 2, :]
                    mm = pe.matmul(ps[:, n // 2, T * (n % 2):T * (n % 2 + 1)], permW, src, start=True, stop=True)
                mm.then_inc(S("w_perm"), 1)
                for n in range(2):
                    for t in range(4):
                        mm = pe.transpose(ps[:, 5 + n, P * t:P * (t + 1)], AV[:, n, P * t:P * (t + 1)], ident)
                mm.then_inc(S("w_vt"), 1)
                pe.wait_ge(S("w_rope"), 5)
                pe.wait_ge(S("w_vv"), 2)

                def scores(n):
                    cc, hf, qb = n // 4, n // 2 % 2, n % 2
                    r = slice(64 * hf, 64 * hf + 64)
                    if n >= 2:
                        pe.wait_ge(S("w_sb"), n - 1)
                    pe.matmul(ps[:, n % 2, 0:512], AQ[r, cc, P * qb:P * (qb + 1)], AK[r, cc // 4, :],
                              start=True, stop=True).then_inc(S("w_s"), 1)

                def values(n):
                    cc, hf, qb = n // 4, n // 2 % 2, n % 2
                    pe.wait_ge(S("w_pn"), n + 1)
                    if n >= 2:
                        pe.wait_ge(S("w_pt"), n - 1)
                    for t in range(4):
                        mm = pe.transpose(ps[:, 2 + n % 2, P * t:P * (t + 1)], pn[:, n % 2, P * t:P * (t + 1)], ident)
                    mm.then_inc(S("w_tr"), 1)
                    if qb == 1:
                        pe.wait_ge(S("w_pt"), n + 1)
                        if hf == 0 and cc >= 2:
                            pe.wait_ge(S("gated"), c["hid"] + cc - 1)
                        r = slice(64 * hf, 64 * hf + 64)
                        for t in range(4):
                            v0 = P * (cc // 4) + 64 * hf
                            mm = pe.matmul(ps[r, 4 + cc % 2, 0:T], VV[:, t, v0:v0 + 64], PTw[:, hf, t, :],
                                           start=(t == 0), stop=(t == 3))
                        mm.then_inc(S("w_pv"), 1)

                scores(0)
                for n in range(32):
                    if n + 1 < 32:
                        scores(n + 1)
                    values(n)


            def pair_slot(h):
                return 2 * (h % 2) + h // 2

            def mix_pe(c):
                b, l = c["unit"], c["l"]

                def need(name, per, k):
                    pe.wait_ge(S(name), per * l + k)

                pe.wait_ge(S("h_ready"), c["h"])
                for n in range(N_IN):
                    if n >= 4:
                        need("m_evac", N_IN, n - 3)
                    in_unit(pe, b + n, 0, n % 4, T)
                need("m_evac", N_IN, N_IN)
                need("m_sq1", 1, 1)
                for n in range(2):
                    pe.matmul(ps[:, 0, 0:T], ones, sqm[:, n, :], start=(n == 0), stop=(n == 1))
                pe.matmul(ps[:, 0, T:2 * T], ones, sqm[:, 2, :], start=True, stop=True)
                for n in range(2):
                    mm = pe.matmul(ps[:, 1 + n, :], bones64, sqm[:, 4 + 2 * n:6 + 2 * n, :].rearrange("p a t -> p (a t)"),
                                   start=True, stop=True)
                mm.then_inc(S("m_ss1"), 1)
                need("m_sqc", 1, 1)
                for n in range(2):
                    mm = pe.matmul(ps[:, 3, 0:T], ones, sqm[:, n, :], start=(n == 0), stop=(n == 1))
                mm.then_inc(S("m_ssc"), 1)

                pe.matmul(ps[:, 4, 0:T], bupt[:, l, :], Z[0:16, B_G, :], start=True, stop=True).then_inc(S("b_gate"), 1)
                for m in range(2):
                    for t in range(TT):
                        mm = pe.transpose(ps[:, 5, P * (2 * t + m):P * (2 * t + m + 1)], Z[:, B_V + m, P * t:P * (t + 1)],
                                          ident)
                mm.then_inc(S("b_vt"), 1)
                need("b_qk", 1, 1)
                for t in range(TT):
                    mm = pe.transpose(ps[:, 6, P * t:P * (t + 1)], KP[:, LEVELS, P * t:P * (t + 1)], ident)
                mm.then_inc(S("b_kt"), 1)
                need("b_vb", 2, 2)
                for k in range(3):
                    r = slice(64 * (k % 2), 64 * (k % 2) + 64)
                    mm = pe.matmul(ps[:, 7, 0:2 * P] if k == 0 else ps[:, 3 + k, 0:2 * P] if k == 1 else ps[:, 5, 0:2 * P],
                                   kdT[r, k // 2, :], VB[r, k // 2, :], start=True, stop=True)
                mm.then_inc(S("b_st"), 1)
                need("m_rt", 2, 2)
                for v in range(LEVELS + 1):
                    if v >= 1:
                        need("b_at", LEVELS + 1, v)
                    for h in range(4):
                        r = slice(32 * h, 32 * h + 32)
                        for t in range(TT):
                            kk = KP[r, v, P * t:P * (t + 1)] if v < LEVELS else Z[r, B_K, P * t:P * (t + 1)]
                            qq = QP[r, v, P * t:P * (t + 1)] if v < LEVELS else Z[r, B_Q, P * t:P * (t + 1)]
                            mm = pe.matmul(ps[:, h, P * t:P * (t + 1)], kk, qq, start=True, stop=True)
                    mm.then_inc(S("b_lv"), 1)
                need("b_at", LEVELS + 1, LEVELS + 1)
                need("b_s", 2, 2)
                for h in range(4):
                    for t in range(TT):
                        r = slice(64 * (h % 2), 64 * (h % 2) + 64)
                        pe.matmul(ps[r, 4, T * (h // 2) + P * t:T * (h // 2) + P * (t + 1)],
                                  VB[:, t, 64 * h:64 * h + 64], AT[:, h, P * t:P * (t + 1)], start=True, stop=True)
                for m in range(2):
                    for k in range(1, 4):
                        mm = pe.matmul(ps[:, 5, T * m + 64 * k:T * m + 64 * (k + 1)], ST[:, k - 1, P * m:P * (m + 1)],
                                       QP[:, LEVELS, 64 * k:64 * (k + 1)], start=True, stop=True)
                mm.then_inc(S("b_o"), 1)
                need("b_sq", 1, 1)
                pe.matmul(ps[:, 6, :], bones64, sqm[:, 0:2, :].rearrange("p a t -> p (a t)"), start=True,
                          stop=True).then_inc(S("b_ss"), 1)

                need("d_cn", 1, 1)
                pe.wait_ge(S("lo_ready"), b + N_IN + 1)
                s = (b + N_IN) % 2
                for h in range(4):
                    for k in range(2):
                        mm = tile(pe, s, 4 * k + h, ps[:, h // 2, T * (h % 2):T * (h % 2 + 1)], cn_hi[:, k, :],
                                  cn_lo[:, k, :], k == 0, k == 1)
                mm.then_inc(S("unit_done"), 1)
                pe.wait_ge(S("lo_ready"), b + N_IN + 2)
                for h in range(4):
                    mm = tile(pe, 1 - s, h, ps[:, 2 + h // 2, T * (h % 2):T * (h % 2 + 1)], cn_hi[:, 2, :],
                              cn_lo[:, 2, :], True, True)
                mm.then_inc(S("unit_done"), 1)
                need("d_sq", 1, 1)
                for n in range(4):
                    mm = pe.matmul(ps[0:96, n, :], ones[0:96, 0:96], sqm[0:96, 2 * n:2 * n + 2, :].rearrange("p a t -> p (a t)"),
                                   start=True, stop=True)
                mm.then_inc(S("d_ss"), 1)
                need("d_n", 2, 2)
                for n in range(4):
                    src = (DQ if n < 2 else DK)[0:96, 2 * (n % 2):2 * (n % 2) + 2, :].rearrange("p a t -> p (a t)")
                    mm = pe.matmul(ps[0:96, n, :], permD[0:96, 0:96], src, start=True, stop=True)
                mm.then_inc(S("d_perm"), 1)
                need("d_e", 4, 4)
                for t in range(TT):
                    for h in range(4):
                        mm = pe.transpose(ps[:, 4 + t, P * h:P * (h + 1)], DV[:, h, P * t:P * (t + 1)], ident)
                mm.then_inc(S("d_vt"), 1)

                def attend(slot, q, k, v, q0, qb):
                    kc = P * (qb + 1)
                    for h in range(4):
                        g = slot(h)
                        mm = pe.matmul(ps[:, g // 2, T * (g % 2):T * (g % 2) + kc], q(h)[:, P * qb:P * (qb + 1)],
                                       k(h)[:, 0:kc], start=True, stop=True)
                    mm.then_inc(S("s_s"), 1)
                    pe.wait_ge(S("s_p"), 4 * l + q0 + qb + 1)
                    for t in range(qb + 1):
                        for h in range(4):
                            mm = pe.transpose(ps[:, 2 + t, P * h:P * (h + 1)], PR[:, h, P * t:P * (t + 1)], ident)
                    mm.then_inc(S("s_tr"), 1)
                    pe.wait_ge(S("s_pt"), 4 * l + q0 + qb + 1)
                    for h in range(4):
                        r = slice(64 * (h % 2), 64 * (h % 2) + 64)
                        for t in range(qb + 1):
                            mm = pe.matmul(ps[r, 6, T * (h // 2) + P * qb:T * (h // 2) + P * (qb + 1)], v(t, h),
                                           PTm[:, t, slot(h), P * qb:P * (qb + 1)], start=(t == 0), stop=(t == qb))
                    mm.then_inc(S("s_pv"), 1)

                need("d_r", 2, 2)
                need("d_vt2", 2, 2)
                for qb in range(TT):
                    attend(lambda h: h, lambda h: DQ[0:96, h, :], lambda h: DK[0:96, h, :], lambda t, h: VT[:, t, h, 64:128], 0, qb)

                for t in range(TT):
                    mm = pe.transpose(ps[:, 7, 8 * t:8 * t + 8], Z[0:8, I_W, P * t:P * (t + 1)], ident[0:8, 0:8])
                mm.then_inc(S("i_wt"), 1)
                for m in range(2):
                    for t in range(TT):
                        mm = pe.transpose(ps[:, 5, P * (2 * t + m):P * (2 * t + m + 1)], Z[:, A_V + m, P * t:P * (t + 1)],
                                          ident)
                mm.then_inc(S("a_vt"), 1)
                for qb in range(TT):
                    kc = P * (qb + 1)
                    if qb == 1:
                        pass
                    for h in range(8):
                        r = slice(32 * (h % 4), 32 * (h % 4) + 32)
                        n = 8 * qb + h
                        if n >= 2:
                            need("i_r", 16, n - 1)
                        pe.matmul(ps[:, 2 + n % 2, 0:kc], Z[r, I_Q + h // 4, P * qb:P * (qb + 1)], Z[r, I_K, 0:kc],
                                  start=True, stop=True).then_inc(S("i_s"), 1)
                need("a_vt2", 1, 1)
                need("i_r", 16, 16)
                for qb in range(TT):
                    attend(pair_slot, lambda h: QA[64 * (h % 2):64 * (h % 2) + 64, h // 2, :],
                           lambda h: QA[64 * (h % 2):64 * (h % 2) + 64, 2 + h // 2, :],
                           lambda t, h: VT[:, t, h // 2, 64 * (h % 2):64 * (h % 2) + 64], 2, qb)

            if any(k == "mix" for k, _ in PLAN):
                pe.wait_ge(S("rbb_ready"), 1)
                for h in range(4):
                    mm = pe.matmul(ps[:, 1 + pair_slot(h), 0:384], rbb[:, h, :], oh[:, :], start=True, stop=True)
                mm.then_inc(S("bias_rows"), 1)
            if "mod" in DO:
                mod_pe()
            prev = None
            for kind, c in PLAN:
                if kind == "pre":
                    stats(c, c["N"])
                elif kind == "gu":
                    gu_pe(c)
                elif kind == "out":
                    out_pe(c, prev)
                elif kind == "post":
                    pe.wait_ge(S("y0_ready"), c["post_n"] + 1)
                    stats(c, c["N"])
                elif kind == "conv":
                    conv_pe(c)
                elif kind == "attn":
                    attn_pe(c)
                elif kind == "mix":
                    mix_pe(c)
                prev = kind

        @block.scalar
        def _(act):
            def root(c, N, scale):
                act.wait_ge(S("ss_done"), DC * (c["norm"] + 1))
                act.activation(rt[:, 0:N], ps[:, 4, 0:N], ACT.Sqrt, bias=epsc[:, 0:1],
                               scale=scale).then_inc(S("rt_ready"), 1)

            def pre_act(c):
                N, n = c["N"], c["norm"]
                for t in range(DC):
                    if c["post"]:
                        act.wait_ge(S("x_ready"), DC * (c["post"] - 1) + t + 1)
                    else:
                        act.wait_ge(S("x_loaded"), 16)
                    if DC * n + t - 1 > 0:
                        act.wait_ge(S("ss_done"), DC * n + t - 1)
                    act.activation(sq[:, t % 2, 0:N], xT[:, t, 0:N], ACT.Square).then_inc(S("sq_ready"), 1)
                root(c, N, 1.0 / D)
                for t in range(DC):
                    act.wait_ge(S("tn_ready"), c["h"] + t + 1)
                    if c["h"] + t - 1 > 0:
                        act.wait_ge(S("h_ready"), c["h"] + t - 1)
                    for v, r in halves(N):
                        a, s = coef(c["coef"], t, v)
                        ins = act.activation(gt[:, t % 2, r], ut[:, t % 2, r], ACT.Identity, bias=s, scale=a)
                    ins.then_inc(S("hf_ready"), 1)

            def gu_act(c):
                N, b = c["N"], c["unit"]
                with act.Fori(0, FC // 2) as i:
                    for j in range(2):
                        split_hi(act, b + 2 * j + 2, i)
                        act.wait_ge(S("unit_done"), b + 2 * j + 1 + 4 * i)
                        act.activation(gt[:, j, 0:N], ps[:, j, 0:N], ACT.Silu).then_inc(S("silu_done"), 1)
                        split_hi(act, b + 2 * j + 3, i)

            def out_act(c):
                b, nk = c["unit"], c["nk"]
                full = (nk // 4) if b + nk + 2 <= UNITS else nk // 4 - 1
                with act.Fori(0, full) as i:
                    for j in range(4):
                        split_hi(act, b + 2 + j, i)
                for k in range(4 * full, nk):
                    split_hi(act, b + 2 + k)

            def post_act(c):
                N, n = c["N"], c["norm"]
                act.wait_ge(S("unit_done"), c["unit"])
                act.activation(y0[:, 0:N], ps[:, 4, 0:N], ACT.Copy).then_inc(S("y0_ready"), 1)
                for t in range(DC):
                    if t == 0:
                        act.wait_ge(S("y0_ready"), c["post_n"] + 1)
                    act.wait_ge(S("ss_done"), DC * n + t - 1)
                    src = y0[:, 0:N] if t == 0 else ps[:, out_bank(t), 0:N]
                    act.activation(sq[:, t % 2, 0:N], src, ACT.Square).then_inc(S("sq_ready"), 1)
                root(c, N, 1.0 / D)

            def conv_act(c):
                b = c["unit"]
                for n in range(DC):
                    split_hi(act, b + 3 * n + 2)
                    split_hi(act, b + 3 * n + 3)
                    act.wait_ge(S("unit_done"), b + 3 * n + 2)
                    if n >= 2:
                        act.wait_ge(S("cu_ready"), n - 1)
                    act.activation(gt[:, n % 2, :], ps[:, 3 * (n % 2) + 1, :], ACT.Copy).then_inc(S("cg_ready"), 1)
                    split_hi(act, b + 3 * n + 4)
                    act.wait_ge(S("cu_ready"), n + 1)
                    if n >= 2:
                        act.wait_ge(S("gated"), c["hid"] + n - 1)
                    w = VEC["convw"] + DC + n
                    act.activation(cy[:, n % 2, :, :], cu[:, n % 2, :, 1:T + 1], ACT.Copy,
                                   scale=vec[:, w:w + 1]).then_inc(S("cy_ready"), 1)

            def attn_act(c):
                b = c["unit"]
                act.wait_ge(S("unit_done"), b)
                act.dma_start(atab[:, :], attabs).then_inc(S("atab_loaded"), 16)
                for n in range(12):
                    split_hi(act, b + n + 2)
                    act.wait_ge(S("unit_done"), b + n + 1)
                    dst = AK[:, n, :] if n < 2 else AV[:, n - 2, :] if n < 4 else AQ[:, n - 4, :]
                    act.activation(dst, ps[:, n % 4, 0:2 * T if n < 4 else T], ACT.Copy).then_inc(S("w_evac"), 1)
                act.wait_ge(S("w_vt"), 1)
                for n in range(2):
                    act.activation(VV[:, :, P * n:P * (n + 1)],
                                   ps[:, 5 + n, :].rearrange("p (t v) -> p t v", t=4), ACT.Copy).then_inc(S("w_vv"), 1)

                def pt(n):
                    hf, qb = n // 2 % 2, n % 2
                    act.wait_ge(S("w_tr"), n + 1)
                    if n >= 4:
                        act.wait_ge(S("w_pv"), n // 2 - 1)
                    act.activation(PTw[:, hf, :, P * qb:P * (qb + 1)],
                                   ps[:, 2 + n % 2, :].rearrange("p (t q) -> p t q", t=4), ACT.Copy).then_inc(S("w_pt"), 1)

                for n in range(32):
                    head = 2 * (n // 4) + n // 2 % 2
                    sk = VEC["sink"] + head
                    act.wait_ge(S("w_nm"), n + 1)
                    if n >= 2:
                        act.wait_ge(S("w_pn"), n - 1)
                    act.activation(pw[:, n % 2, :], sw[:, n % 2, :], ACT.Exp, bias=aw[:, n % 2, 1:2],
                                   accum_out=aw[:, n % 2, 2:3]).then_inc(S("w_e"), 1)
                    act.activation(aw[:, n % 2, 3:4], vec[:, sk:sk + 1], ACT.Exp,
                                   bias=aw[:, n % 2, 1:2]).then_inc(S("w_e"), 1)
                    if n >= 1:
                        pt(n - 1)
                pt(31)


            def mix_act(c):
                b, l = c["unit"], c["l"]

                def need(name, per, k):
                    act.wait_ge(S(name), per * l + k)

                act.wait_ge(S("unit_done"), b)
                act.dma_start(mtab[:, :], mixtabs).then_inc(S("mtab_loaded"), 16)
                for n in range(N_IN):
                    split_hi(act, b + n + 2)
                    act.wait_ge(S("unit_done"), b + n + 1)
                    if n in (C_G, C_G + 1):
                        act.activation(Z[:, n, :], ps[:, n % 4, 0:T], ACT.Sigmoid).then_inc(S("m_evac"), 1)
                    elif n == B_Q:
                        act.activation(Z[:, n, :], ps[:, n % 4, 0:T], ACT.Copy, scale=32 ** -0.5).then_inc(S("m_evac"), 1)
                    else:
                        act.activation(Z[:, n, :], ps[:, n % 4, 0:T], ACT.Copy).then_inc(S("m_evac"), 1)
                need("m_evac", N_IN, N_IN)
                act.activation(sqm[:, :, :], Z[:, D_Q:D_Q + 8, :], ACT.Square).then_inc(S("m_sq1"), 1)
                need("m_ss1", 1, 1)
                act.activation(rm[:, 0:T], ps[:, 0, 0:T], ACT.Sqrt, bias=epsc[:, 0:1], scale=1 / 256)
                act.activation(rm[:, T:2 * T], ps[:, 0, T:2 * T], ACT.Sqrt, bias=epsc[:, 0:1], scale=1 / 128)
                act.activation(rm[:, 2 * T:6 * T], ps[:, 1:3, :].rearrange("p a t -> p (a t)"), ACT.Sqrt,
                               bias=epsc[:, 0:1], scale=1 / 64).then_inc(S("m_rt"), 1)
                need("c_tap", 2 * KTAPS, 2 * KTAPS)
                act.activation(sqm[:, 0:2, :], hc[:, :, :], ACT.Square).then_inc(S("m_sqc"), 1)
                need("m_ssc", 1, 1)
                act.activation(rm[:, 6 * T:7 * T], ps[:, 3, 0:T], ACT.Sqrt, bias=epsc[:, 0:1],
                               scale=1 / 256).then_inc(S("m_rt"), 1)
                need("c_n", 1, 1)
                act.activation(hc[:, :, :], hc[:, :, :], ACT.Silu).then_inc(S("c_silu"), 1)
                act.wait_ge(S("gated"), c["hid"] + 2)
                need("b_vt", 1, 1)
                act.activation(VB[:, :, :].rearrange("p a t -> p (a t)"), ps[:, 5, :], ACT.Copy).then_inc(S("b_vb"), 1)
                need("b_g", 1, 1)
                act.activation(G2, G1, ACT.Abs).then_inc(S("b_a"), 1)
                need("b_a", 3, 1)
                act.activation(G2, G2, ACT.Exp, scale=-1.0).then_inc(S("b_a"), 1)
                need("b_a", 3, 2)
                act.activation(G2, G2, ACT.Ln, bias=1.0).then_inc(S("b_a"), 1)
                need("b_e", 1, 1)
                act.activation(EB[:, :, :], EB[:, :, :], ACT.Exp, scale=1 / 16).then_inc(S("b_p"), 1)
                need("b_kt", 1, 1)
                act.activation(kdT[:, :, :].rearrange("p a t -> p (a t)"), ps[:, 6, 0:2 * P], ACT.Copy).then_inc(S("b_vb"), 1)
                need("b_o", 1, 1)
                act.activation(OB[:, :, :].rearrange("p a t -> p (a t)"), ps[:, 4, :], ACT.Copy).then_inc(S("b_oc"), 1)
                need("b_oi", 1, 1)
                act.activation(sqm[:, 0:2, :], OB[:, :, :], ACT.Square).then_inc(S("b_sq"), 1)
                need("b_ss", 1, 1)
                act.activation(rm[:, 0:2 * T], ps[:, 6, :], ACT.Sqrt, bias=epsc[:, 0:1], scale=1 / 64).then_inc(S("b_rt"), 1)
                act.activation(Z[:, B_R:B_R + 2, :], Z[:, B_R:B_R + 2, :], ACT.Silu).then_inc(S("b_silu"), 1)
                act.wait_ge(S("gated"), c["hid"] + 4)
                act.wait_ge(S("unit_done"), b + N_IN + 2)
                act.activation(DQ[:, :, :], ps[:, 0:2, :].rearrange("p a (b t) -> p (a b) t", b=2), ACT.Copy).then_inc(S("d_e"), 1)
                act.activation(DV[:, :, :], ps[:, 2:4, :].rearrange("p a (b t) -> p (a b) t", b=2), ACT.Copy).then_inc(S("d_e"), 1)
                act.activation(DK[0:64, :, :], ps[0:64, 2:4, :].rearrange("p a (b t) -> p (a b) t", b=2),
                               ACT.Copy).then_inc(S("d_e"), 1)
                act.activation(DK[64:96, :, :], Z[64:96, D_PE, :].unsqueeze(1).broadcast_to([32, 4, T]),
                               ACT.Copy).then_inc(S("d_e"), 1)
                split_hi(act, b + N_IN + 2)
                split_hi(act, b + N_IN + 3)
                need("d_e", 4, 4)
                act.activation(sqm[0:96, 0:4, :], DQ[0:96, :, :], ACT.Square)
                act.activation(sqm[0:96, 4:8, :], DK[0:96, :, :], ACT.Square).then_inc(S("d_sq"), 1)
                need("d_ss", 1, 1)
                act.activation(rm[0:96, :], ps[0:96, 0:4, :].rearrange("p a t -> p (a t)"), ACT.Sqrt,
                               bias=epsc[0:96, 0:1], scale=1 / 96).then_inc(S("d_rt"), 1)
                need("d_vt", 1, 1)
                for t in range(TT):
                    act.activation(VT[:, t, :, :], ps[:, 4 + t, :].rearrange("p (h v) -> p h v", h=4),
                                   ACT.Copy).then_inc(S("d_vt2"), 1)

                def attend(q0, qb):
                    kc, n = P * (qb + 1), 4 * l + q0 + qb + 1
                    act.wait_ge(S("s_nm"), n)
                    for h in range(4):
                        ins = act.activation(PR[:, h, 0:kc], LG[:, h, 0:kc], ACT.Exp, bias=am[:, 4 + h:5 + h],
                                             accum_out=am[:, 8 + h:9 + h])
                    ins.then_inc(S("s_e"), 1)
                    act.wait_ge(S("s_tr"), n)
                    for t in range(qb + 1):
                        ins = act.activation(PTm[:, t, :, P * qb:P * (qb + 1)],
                                             ps[:, 2 + t, :].rearrange("p (h q) -> p h q", h=4), ACT.Copy)
                    ins.then_inc(S("s_pt"), 1)

                for qb in range(TT):
                    attend(0, qb)
                need("i_wt", 1, 1)
                act.activation(iw[:, :, :].rearrange("p a t -> p (a t)"), ps[:, 7, 0:16], ACT.Copy,
                               scale=8 ** -0.5).then_inc(S("i_w"), 1)
                need("a_vt", 1, 1)
                act.activation(VT[:, :, 0:2, :].rearrange("p t a v -> p t (a v)"),
                               ps[:, 5, :].rearrange("p (t v) -> p t v", t=2), ACT.Copy).then_inc(S("a_vt2"), 1)
                for n in range(16):
                    kc = P * (n // 8 + 1)
                    need("i_s", 16, n + 1)
                    if n >= 2:
                        need("i_a", 16, n - 1)
                    act.activation(RI[:, n % 2, 0:kc], ps[:, 2 + n % 2, 0:kc], ACT.Relu,
                                   scale=32 ** -0.5).then_inc(S("i_r"), 1)
                for qb in range(TT):
                    attend(2, qb)

            act.dma_start(cv[:, :, :], cvec).then_inc(S("small_loaded"), 16)
            act.dma_start(vec[:, :], vecs).then_inc(S("small_loaded"), 16)
            act.dma_start(tabs[:, :], ctabs).then_inc(S("small_loaded"), 16)
            act.dma_start(bupt[:, :, :], bup).then_inc(S("small_loaded"), 16)
            act.dma_start(rl[:, :], relb).then_inc(S("small_loaded"), 16)
            act.dma_start(oh[:, :], onehot).then_inc(S("small_loaded"), 16)
            act.wait_ge(S("small_loaded"), 96)
            act.wait_ge(S("init"), 1)
            act.activation(cv[:, :, :], cv[:, :, :], ACT.Silu).then_inc(S("cs_ready"), 1)
            if "mod" in DO:
                for s in range(RAW):
                    act.dma_start(mraw[:, s, :], wmod[s]).then_inc(S(f"mod_landed{s}"), 16)
                with act.Fori(1, 2 * NMOD * DC // 4) as i:
                    for s in range(RAW):
                        act.wait_ge(S("mod_done"), 4 * i + (s - 3))
                        act.dma_start(mraw[:, s, :], wmod[4 * i + s]).then_inc(S(f"mod_landed{s}"), 16)
            if any(k == "mix" for k, _ in PLAN):
                act.wait_ge(S("bias_rows"), 1)
                act.activation(sqb[:, :, :], ps[:, 1:5, 0:384], ACT.Copy).then_inc(S("bias_copied"), 1)
                act.wait_ge(S("bias_copied"), 1)
                act.dma_start(skew, sqb[:, :, :]).then_inc(S("skew_stored"), 16)
                act.wait_ge(S("skew_stored"), 16)
                act.dma_start(biasA[:, :, :], skewed).then_inc(S("bias_loaded"), 16)
            split_hi(act, 0)
            split_hi(act, 1)
            for kind, c in PLAN:
                if kind == "pre":
                    pre_act(c)
                elif kind == "gu":
                    gu_act(c)
                elif kind == "out":
                    out_act(c)
                elif kind == "post":
                    post_act(c)
                elif kind == "conv":
                    conv_act(c)
                elif kind == "attn":
                    attn_act(c)
                elif kind == "mix":
                    mix_act(c)

        @block.vector
        def _(dve):
            def recip(c, N):
                dve.wait_ge(S("rt_ready"), c["norm"] + 1)
                dve.reciprocal(rstd[:, 0:N], rt[:, 0:N]).then_inc(S("rstd_ready"), 1)
                dve.wait_ge(S("rstd_ready"), c["norm"] + 1)

            def pre_dve(c):
                N, h = c["N"], c["h"]
                recip(c, N)

                def lo(t):
                    dve.wait_ge(S("h_hi_ready"), h + t + 1)
                    dve.tensor_tensor(h_lo[:, t, 0:N], gt[:, t % 2, 0:N], h_hi[:, t, 0:N],
                                      ALU.subtract).then_inc(S("h_ready"), 1)

                for t in range(DC):
                    if h + t - 1 > 0:
                        dve.wait_ge(S("hf_ready"), h + t - 1)
                    dve.tensor_tensor(ut[:, t % 2, 0:N], xT[:, t, 0:N], rstd[:, 0:N],
                                      ALU.mult).then_inc(S("tn_ready"), 1)
                    if t >= 1:
                        lo(t - 1)
                lo(DC - 1)

            def gu_dve(c):
                N, b, hid = c["N"], c["unit"], c["hid"]
                with dve.Fori(0, FC // 2) as i:
                    for j in range(2):
                        split_lo(dve, b + 2 * j + 2, i)
                        split_lo(dve, b + 2 * j + 3, i)
                        dve.wait_ge(S("silu_done"), FC * c["ffn"] + 2 * i + (j + 1))
                        dve.wait_ge(S("unit_done"), b + 2 * j + 2 + 4 * i)
                        dve.wait_ge(S("ulo_ready"), hid + 2 * i + (j + 1))
                        dve.tensor_tensor(ut[:, j, 0:N], gt[:, j, 0:N], ps[:, 2 + j, 0:N],
                                          ALU.mult).then_inc(S("gated"), 1)

            def out_dve(c):
                b, nk = c["unit"], c["nk"]
                full = (nk // 4) if b + nk + 2 <= UNITS else nk // 4 - 1
                with dve.Fori(0, full) as i:
                    for j in range(4):
                        split_lo(dve, b + 2 + j, i)
                for k in range(4 * full, nk):
                    split_lo(dve, b + 2 + k)

            def post_dve(c):
                N = c["N"]
                l, part = c["coef"]
                recip(c, N)

                def scaled(t):
                    src = y0[:, 0:N] if t == 0 else ps[:, out_bank(t), 0:N]
                    dve.tensor_tensor(ut[:, t % 2, 0:N], src, rstd[:, 0:N], ALU.mult).then_inc(S("yn_ready"), 1)

                scaled(0)
                for t in range(DC):
                    if t + 1 < DC:
                        if t >= 1:
                            dve.wait_ge(S("x_ready"), DC * c["post"] + t)
                        scaled(t + 1)
                    dve.wait_ge(S("yn_ready"), DC * c["post_n"] + t + 1)
                    for v, r in halves(N):
                        ins = dve.scalar_tensor_tensor(xT[:, t, r], ut[:, t % 2, r], CG[:, l, part, t, v:v + 1],
                                                       xT[:, t, r], ALU.mult, ALU.add)
                    ins.then_inc(S("x_ready"), 1)

            def add_dve(c):
                dve.wait_ge(S("unit_done"), c["unit"])
                for t in range(DC):
                    dve.scalar_tensor_tensor(xT[:, t, 0:T], ps[:, out_bank(t), 0:T], c["weight"], xT[:, t, 0:T],
                                             ALU.mult, ALU.add).then_inc(S("x_ready"), 1)

            def conv_dve(c):
                b, hid = c["unit"], c["hid"]
                for n in range(DC):
                    for m in range(2, 5):
                        split_lo(dve, b + 3 * n + m)
                    if n == 0:
                        dve.memset(cu[:, :, :, 0:1], 0.0)
                        dve.memset(cu[:, :, :, T + 1:T + 2], 0.0).then_inc(S("cu_zero"), 1)
                        dve.wait_ge(S("cu_zero"), 1)
                    dve.wait_ge(S("cg_ready"), n + 1)
                    dve.wait_ge(S("unit_done"), b + 3 * n + 3)
                    dve.tensor_tensor(cu[:, n % 2, :, 1:T + 1], gt[:, n % 2, :].rearrange("p (v t) -> p v t", v=2),
                                      ps[:, 3 * (n % 2) + 2, :].rearrange("p (v t) -> p v t", v=2),
                                      ALU.mult).then_inc(S("cu_ready"), 1)
                    dve.wait_ge(S("cy_ready"), n + 1)
                    dve.wait_ge(S("cu_ready"), n + 1)
                    for m, o in ((0, 0), (2, 2)):
                        w = VEC["convw"] + DC * m + n
                        dve.scalar_tensor_tensor(cy[:, n % 2, :, :], cu[:, n % 2, :, o:o + T], vec[:, w:w + 1],
                                                 cy[:, n % 2, :, :], ALU.mult, ALU.add).then_inc(S("cy_tap"), 1)
                        dve.wait_ge(S("cy_tap"), 2 * n + (1 if o == 0 else 2))
                    dve.wait_ge(S("ulo_ready"), hid + n + 1)
                    dve.tensor_tensor(ut[:, n % 2, :], cy[:, n % 2, :, :].rearrange("p v t -> p (v t)"),
                                      ps[:, 3 * (n % 2), :], ALU.mult).then_inc(S("gated"), 1)

            def attn_dve(c):
                b, hid = c["unit"], c["hid"]
                for n in range(12):
                    split_lo(dve, b + n + 2)
                dve.wait_ge(S("w_perm"), 1)
                dve.wait_ge(S("atab_loaded"), 16)
                for n in range(5):
                    dst = AK[:, :, 0:T] if n == 0 else AQ[:, 2 * n - 2:2 * n, :]
                    cs = ropeW[0 if n == 0 else 2].unsqueeze(1).broadcast_to([P, 2, T])
                    sn = ropeW[1 if n == 0 else 3].unsqueeze(1).broadcast_to([P, 2, T])
                    dve.tensor_tensor(rp1[:, n % 2], dst, cs, ALU.mult).then_inc(S("w_rp"), 1)
                    dve.tensor_tensor(rp2[:, n % 2], ps[:, n, :].rearrange("p (a t) -> p a t", a=2), sn,
                                      ALU.mult).then_inc(S("w_rp"), 1)
                    dve.wait_ge(S("w_rp"), 2 * n + 2)
                    dve.tensor_tensor(dst, rp1[:, n % 2], rp2[:, n % 2], ALU.add).then_inc(S("w_rope"), 1)

                def top(n):
                    qb = n % 2
                    sk = VEC["sink"] + 2 * (n // 4) + n // 2 % 2
                    dve.wait_ge(S("w_s"), n + 1)
                    if n >= 2:
                        dve.wait_ge(S("w_e"), 2 * (n - 1))
                    dve.tensor_tensor(sw[:, n % 2, :], ps[:, n % 2, :], bandW[:, qb, :], ALU.add).then_inc(S("w_sb"), 1)
                    dve.wait_ge(S("w_sb"), n + 1)
                    dve.tensor_reduce(aw[:, n % 2, 0:1], sw[:, n % 2, :], AXX, ALU.max).then_inc(S("w_mx"), 1)
                    dve.wait_ge(S("w_mx"), n + 1)
                    dve.tensor_scalar(aw[:, n % 2, 1:2], aw[:, n % 2, 0:1], vec[:, sk:sk + 1], -1.0, ALU.max,
                                      ALU.mult).then_inc(S("w_nm"), 1)

                def norm(n):
                    dve.wait_ge(S("w_e"), 2 * n + 2)
                    dve.tensor_tensor(aw[:, n % 2, 4:5], aw[:, n % 2, 2:3], aw[:, n % 2, 3:4],
                                      ALU.add).then_inc(S("w_sum"), 1)
                    dve.wait_ge(S("w_sum"), n + 1)
                    dve.reciprocal(aw[:, n % 2, 5:6], aw[:, n % 2, 4:5]).then_inc(S("w_rec"), 1)
                    dve.wait_ge(S("w_rec"), n + 1)
                    if n >= 2:
                        dve.wait_ge(S("w_tr"), n - 1)
                    dve.tensor_scalar(pn[:, n % 2, :], pw[:, n % 2, :], aw[:, n % 2, 5:6], None,
                                      ALU.mult).then_inc(S("w_pn"), 1)

                def head_out(cc):
                    dve.wait_ge(S("w_pv"), 2 * cc + 2)
                    dve.wait_ge(S("ulo_ready"), hid + cc + 1)
                    dve.tensor_copy(ut[:, cc % 2, 0:T], ps[:, 4 + cc % 2, 0:T]).then_inc(S("gated"), 1)

                top(0)
                for n in range(32):
                    if n + 1 < 32:
                        top(n + 1)
                    norm(n)
                    if n % 4 == 1 and n > 4:
                        head_out(n // 4 - 1)
                head_out(7)


            def mix_dve(c):
                b, l, hid = c["unit"], c["l"], c["hid"]
                V = lambda name, i=0: vec[:, VEC[f"{name}{l}"] + i:VEC[f"{name}{l}"] + i + 1]

                def need(name, per, k):
                    dve.wait_ge(S(name), per * l + k)

                step = [S_STEP[0]]

                def then(ins):
                    ins.then_inc(S("dve_step"), 1)
                    step[0] += 1
                    dve.wait_ge(S("dve_step"), step[0])

                taps = [(k, ch) for k in range(1, KTAPS) for ch in range(2)]

                def tap():
                    k, ch = taps.pop(0)
                    n = 2 * k + ch
                    need("c_tap", 2 * KTAPS, n - 1)
                    dve.scalar_tensor_tensor(hc[:, ch, :], hp[:, ch, k:k + T], V("cw", n), hc[:, ch, :],
                                             ALU.mult, ALU.add).then_inc(S("c_tap"), 1)

                for n in range(N_IN):
                    split_lo(dve, b + n + 2)
                    if n == 5:
                        need("m_evac", N_IN, 4)
                        dve.memset(hp[:, :, 0:KTAPS - 1], 0.0)
                        then(dve.tensor_tensor(hp[:, :, KTAPS - 1:], Z[:, C_A:C_A + 2, :], Z[:, C_G:C_G + 2, :], ALU.mult))
                        for ch in range(2):
                            dve.tensor_scalar(hc[:, ch, :], hp[:, ch, 0:T], V("cw", ch), V("cb", ch), ALU.mult,
                                              ALU.add).then_inc(S("c_tap"), 1)
                    if n > 5:
                        for _ in range(3):
                            tap()
                while len(taps) > 1:
                    tap()
                tap()
                need("c_tap", 2 * KTAPS, 2 * KTAPS)
                need("m_rt", 2, 1)
                then(dve.reciprocal(rm[:, 0:6 * T], rm[:, 0:6 * T]))
                for n in range(3):
                    r = rm[:, T:2 * T] if n == 2 else rm[:, 0:T]
                    g = V("dkva") if n == 2 else V("dqa", n)
                    ins = dve.scalar_tensor_tensor(cnf[:, n, :], Z[:, D_Q + n, :], g, r, ALU.mult, ALU.mult)
                then(ins)
                then(dve.tensor_copy(cn_hi[:, :, :], cnf[:, :, :]))
                dve.tensor_tensor(cn_lo[:, :, :], cnf[:, :, :], cn_hi[:, :, :], ALU.subtract).then_inc(S("d_cn"), 1)
                for n in range(2):
                    ins = dve.scalar_tensor_tensor(Z[:, A_Q + 2 * n:A_Q + 2 * n + 2, :], Z[:, A_Q + 2 * n:A_Q + 2 * n + 2, :],
                                                   V("ak") if n else V("aq"),
                                                   rm[:, (2 + 2 * n) * T:(4 + 2 * n) * T].rearrange("p (a t) -> p a t", a=2),
                                                   ALU.mult, ALU.mult)
                then(ins)

                def hand_over(k, src, name, wait_first=None):
                    dve.wait_ge(S("ulo_ready"), hid + k + 1)
                    return src

                need("m_rt", 2, 2)
                then(dve.reciprocal(rm[:, 6 * T:7 * T], rm[:, 6 * T:7 * T]))
                for ch in range(2):
                    ins = dve.scalar_tensor_tensor(hc[:, ch, :], hc[:, ch, :], V("cn", ch), rm[:, 6 * T:7 * T], ALU.mult,
                                                   ALU.mult)
                ins.then_inc(S("c_n"), 1)
                need("c_silu", 1, 1)
                for ch in range(2):
                    dve.wait_ge(S("ulo_ready"), hid + ch + 1)
                    dve.tensor_copy(ut[:, ch, 0:T], hc[:, ch, :]).then_inc(S("gated"), 1)
                dve.wait_ge(S("gated"), hid + 2)
                then(dve.memset(AT[:, :, :], 0.0))

                need("b_gate", 1, 1)
                dve.tensor_scalar(G1, ps[:, 4, 0:T], V("bg"), None, ALU.add).then_inc(S("b_g"), 1)
                need("b_g", 1, 1)
                need("b_a", 3, 3)
                then(dve.tensor_scalar(G1, G1, 0.0, None, ALU.min))
                then(dve.tensor_tensor(G1, G1, G2, ALU.subtract))
                dve.wait_ge(S("mtab_loaded"), 16 * (l + 1))
                bb = EB[:, LEVELS, :]
                then(dve.tensor_tensor_scan(bb, scanm, G1, 0.0, ALU.mult, ALU.add))
                for v in range(LEVELS):
                    s = 32 >> v
                    w = bb.rearrange("p (n a s) -> p n a s", a=2, s=s)
                    e = EB[:, v, :].rearrange("p (n a s) -> p n a s", a=2, s=s)
                    mid = w[:, :, 0, s - 1:s].broadcast_to([P, T // (2 * s), s])
                    dve.tensor_tensor(e[:, :, 0, :], mid, w[:, :, 0, :], ALU.subtract)
                    dve.tensor_tensor(e[:, :, 1, :], w[:, :, 1, :], mid, ALU.subtract)
                w = bb.rearrange("p (n s) -> p n s", s=64)
                dve.tensor_tensor(EB[:, LEVELS + 1, :].rearrange("p (n s) -> p n s", s=64),
                                  w[:, :, 63:64].broadcast_to([P, 4, 64]), w, ALU.subtract).then_inc(S("b_e"), 1)
                need("b_p", 1, 1)
                q6 = Z[:, B_Q:B_Q + 1, :].broadcast_to([P, LEVELS + 1, T])
                k6 = Z[:, B_K:B_K + 1, :].broadcast_to([P, LEVELS, T])
                dve.tensor_tensor(QP[:, :, :], q6, EB[:, 0:LEVELS + 1, :], ALU.mult)
                dve.tensor_tensor(KP[:, 0:LEVELS, :], k6, EB[:, 0:LEVELS, :], ALU.mult)
                dve.tensor_tensor(KP[:, LEVELS, :], Z[:, B_K, :], EB[:, LEVELS + 1, :], ALU.mult).then_inc(S("b_qk"), 1)
                need("b_st", 1, 1)
                for k in range(3):
                    src = ps[:, 7, 0:2 * P] if k == 0 else ps[:, 4, 0:2 * P] if k == 1 else ps[:, 5, 0:2 * P]
                    ins = dve.tensor_tensor(ST[:, k, :], src, bmask, ALU.mult)
                then(ins)
                for k in (1, 2):
                    e = EB[:, LEVELS, 64 * k + 63:64 * k + 64]
                    dve.scalar_tensor_tensor(ST[:, k, :], ST[:, k - 1, :], e, ST[:, k, :], ALU.mult,
                                             ALU.add).then_inc(S("b_s"), 1)
                    need("b_s", 2, k)
                for v in range(LEVELS + 1):
                    need("b_lv", LEVELS + 1, v + 1)
                    if v:
                        need("b_at", LEVELS + 1, v)
                    mask = levm[:, v:v + 1, :].bitcast(U32).broadcast_to([P, 4, T])
                    dve.copy_predicated(AT[:, :, :], mask, ps[:, 0:4, 0:T]).then_inc(S("b_at"), 1)
                need("b_oc", 1, 1)
                dve.tensor_tensor(OB[:, :, 64:T], OB[:, :, 64:T], ps[:, 5, :].rearrange("p (a t) -> p a t", a=2)[:, :, 64:T],
                                  ALU.add).then_inc(S("b_oi"), 1)
                need("b_rt", 1, 1)
                need("b_oi", 1, 1)
                then(dve.reciprocal(rm[:, 0:2 * T], rm[:, 0:2 * T]))
                then(dve.scalar_tensor_tensor(OB[:, :, :], OB[:, :, :], V("bo"),
                                              rm[:, 0:2 * T].rearrange("p (a t) -> p a t", a=2), ALU.mult, ALU.mult))
                need("b_silu", 1, 1)
                for ch in range(2):
                    dve.wait_ge(S("ulo_ready"), hid + 2 + ch + 1)
                    dve.tensor_tensor(ut[:, ch, 0:T], OB[:, ch, :], Z[:, B_R + ch, :], ALU.mult).then_inc(S("gated"), 1)
                dve.wait_ge(S("gated"), hid + 4)

                split_lo(dve, b + N_IN + 2)
                split_lo(dve, b + N_IN + 3)
                need("d_rt", 1, 1)
                then(dve.reciprocal(rm[0:96, :], rm[0:96, :]))
                for n, x in enumerate((DQ, DK)):
                    dve.scalar_tensor_tensor(x[0:96, :, :].rearrange("p a t -> p (a t)"),
                                             x[0:96, :, :].rearrange("p a t -> p (a t)"),
                                             (V("dk") if n else V("dq"))[0:96, :], rm[0:96, 4 * T * n:4 * T * (n + 1)],
                                             ALU.mult, ALU.mult).then_inc(S("d_n"), 1)
                need("d_n", 2, 2)
                need("d_perm", 1, 1)
                for n, x in enumerate((DQ, DK)):
                    then(dve.tensor_tensor(dt1[0:96, :, :], ps[0:96, 2 * n:2 * n + 2, :].rearrange("p a (b t) -> p (a b) t", b=2),
                                           SD[0:96, :].unsqueeze(1).broadcast_to([96, 4, T]), ALU.mult))
                    then(dve.tensor_tensor(x[0:96, :, :], x[0:96, :, :], CD[0:96, :].unsqueeze(1).broadcast_to([96, 4, T]),
                                           ALU.mult))
                    dve.tensor_tensor(x[0:96, :, :], x[0:96, :, :], dt1[0:96, :, :], ALU.add).then_inc(S("d_r"), 1)
                    need("d_r", 2, n + 1)

                def attend(q0, qb, scale, bias):
                    kc, n = P * (qb + 1), 4 * l + q0 + qb + 1
                    dve.wait_ge(S("s_s"), n)
                    src = ps[:, 0:2, :].rearrange("p a (b t) -> p (a b) t", b=2)[:, :, 0:kc]
                    if bias is None:
                        cz = (caus0[:, P * (1 - qb):P * (1 - qb) + kc] if qb == 0 else caus0[:, 0:kc])
                        then(dve.scalar_tensor_tensor(LG[:, :, 0:kc], src, scale, cz.unsqueeze(1).broadcast_to([P, 4, kc]),
                                                      ALU.mult, ALU.add))
                    else:
                        k0 = P if qb == 0 else 0
                        then(dve.scalar_tensor_tensor(LG[:, :, 0:kc], src, scale, biasA[:, :, k0:k0 + kc], ALU.mult, ALU.add))
                        then(dve.tensor_tensor(LG[:, :, 0:kc], LG[:, :, 0:kc], bias[:, 0:kc].unsqueeze(1).broadcast_to([P, 4, kc]),
                                               ALU.add))
                    then(dve.tensor_reduce(am[:, 0:4], LG[:, :, 0:kc], AXX, ALU.max))
                    dve.tensor_scalar(am[:, 4:8], am[:, 0:4], -1.0, None, ALU.mult).then_inc(S("s_nm"), 1)
                    dve.wait_ge(S("s_e"), n)
                    then(dve.reciprocal(am[:, 12:16], am[:, 8:12]))
                    for h in range(4):
                        ins = dve.tensor_scalar(PR[:, h, 0:kc], PR[:, h, 0:kc], am[:, 12 + h:13 + h], None, ALU.mult)
                    ins.then_inc(S("s_p"), 1)
                    dve.wait_ge(S("s_p"), n)

                def values_out(q0, k0):
                    dve.wait_ge(S("s_pv"), 4 * l + q0 + 2)
                    for ch in range(2):
                        dve.wait_ge(S("ulo_ready"), hid + k0 + ch + 1)
                        dve.tensor_copy(ut[:, ch, 0:T], ps[:, 6, T * ch:T * (ch + 1)]).then_inc(S("gated"), 1)
                    dve.wait_ge(S("gated"), hid + k0 + 2)

                for qb in range(TT):
                    attend(0, qb, 96 ** -0.5, None)
                values_out(0, 4)
                then(dve.tensor_copy(QA[:, :, :], Z[:, A_Q:A_Q + 4, :]))
                need("i_w", 1, 1)
                sel = []
                for qb in range(TT):
                    kc = P * (qb + 1)
                    acc = SCI[:, 0:kc]
                    for h in range(8):
                        n = 8 * qb + h
                        need("i_r", 16, n + 1)
                        wcol = iw[:, qb, h:h + 1]
                        if h == 0:
                            dve.tensor_scalar(acc, RI[:, n % 2, 0:kc], wcol, None, ALU.mult).then_inc(S("i_a"), 1)
                        else:
                            dve.scalar_tensor_tensor(acc, RI[:, n % 2, 0:kc], wcol, acc, ALU.mult, ALU.add).then_inc(S("i_a"), 1)
                        need("i_a", 16, n + 1)
                    k0 = P if qb == 0 else 0
                    then(dve.tensor_tensor(acc, acc, caus1[:, k0:k0 + kc], ALU.mult))
                    then(dve.tensor_tensor(WK[:, 0, 0:kc], acc, caus0[:, k0:k0 + kc], ALU.add))
                    cur = 0
                    for it in range(8):
                        then(dve.max(m8[:, it % 2, :], WK[:, cur, 0:kc]))
                        then(dve.match_replace(WK[:, 1 - cur, 0:kc], m8[:, it % 2, :], WK[:, cur, 0:kc], -3.3e38))
                        cur = 1 - cur
                    bias = sqm[:, qb, :]
                    then(dve.tensor_scalar(SEL[:, 0:kc], WK[:, cur, 0:kc], -3.3e38, None, ALU.is_equal))
                    then(dve.tensor_tensor(SEL[:, 0:kc], SEL[:, 0:kc], caus1[:, k0:k0 + kc], ALU.mult))
                    then(dve.tensor_scalar(bias[:, 0:kc], SEL[:, 0:kc], 1.0, -NEG, ALU.subtract, ALU.mult))
                for qb in range(TT):
                    attend(2, qb, 0.125, sqm[:, qb, :])
                values_out(2, 6)
                S_STEP[0] = step[0]

            dve.memset(epsc[:, :], EPS)
            dve.memset(zc[:, :], 0.0).then_inc(S("init"), 1)
            dve.wait_ge(S("small_loaded"), 96)
            dve.tensor_copy(rbb[:, :, :], rl[:, :].unsqueeze(2).broadcast_to([32, 4, P])).then_inc(S("rbb_ready"), 1)
            if "mod" in DO:
                dve.wait_ge(S("mod_done"), 2 * NMOD * DC)
                dve.wait_ge(S("small_loaded"), 96)
                bm = vec[:, VEC["bmod"]:VEC["bmod"] + 2 * NMOD * DC]
                dve.tensor_tensor(MOD[:, :, :, :].rearrange("p l n v -> p (l n) v"),
                                  ps[:, 0, 0:4 * NMOD * DC].rearrange("p (n v) -> p n v", v=2),
                                  bm.unsqueeze(2).broadcast_to([P, 2 * NMOD * DC, 2]), ALU.add).then_inc(S("mod_ready"), 1)
                dve.wait_ge(S("mod_ready"), 1)
                for l in range(2):
                    for part in range(3):
                        for v in range(2):
                            g = VEC["g1"] + (l * 6 + 2 * part) * DC
                            m = 3 * part * DC
                            dve.scalar_tensor_tensor(CA[:, l, part, :, v], MOD[:, l, m + DC:m + 2 * DC, v], 1.0,
                                                     vec[:, g:g + DC], ALU.add, ALU.mult)
                            ins = dve.scalar_tensor_tensor(CG[:, l, part, :, v], MOD[:, l, m + 2 * DC:m + 3 * DC, v],
                                                           1.0 if part == 1 else 0.5, vec[:, g + DC:g + 2 * DC],
                                                           ALU.mult, ALU.mult)
                ins.then_inc(S("coef_ready"), 1)
                dve.wait_ge(S("coef_ready"), 1)
            split_lo(dve, 0)
            split_lo(dve, 1)
            for kind, c in PLAN:
                if kind == "pre":
                    pre_dve(c)
                elif kind == "gu":
                    gu_dve(c)
                elif kind == "out":
                    out_dve(c)
                elif kind == "post":
                    post_dve(c)
                elif kind == "add":
                    add_dve(c)
                elif kind == "conv":
                    conv_dve(c)
                elif kind == "attn":
                    attn_dve(c)
                elif kind == "mix":
                    mix_dve(c)

        @block.gpsimd
        def _(pool):
            pool.memset(stepper[:, 0:1], 0.0).then_inc(S("ulo_ready"), 1)
            pool.memset(stepper[:, 1:2], 0.0).then_inc(S("ulo_ready"), 1)

            def pre_pool(c):
                N, h = c["N"], c["h"]
                for t in range(DC):
                    pool.wait_ge(S("hf_ready"), h + t + 1)
                    pool.tensor_copy(h_hi[:, t, 0:N], gt[:, t % 2, 0:N]).then_inc(S("h_hi_ready"), 1)

            def split_hidden(c, k, par, N, hi, lo):
                pool.wait_ge(S("gated"), c["hid"] + k + 1)
                pool.tensor_copy(hi[:, k, 0:N], ut[:, par, 0:N]).then_inc(S("uhi_ready"), 1)
                pool.wait_ge(S("uhi_ready"), c["hid"] + k + 1)
                pool.tensor_tensor(lo[:, k, 0:N], ut[:, par, 0:N], hi[:, k, 0:N],
                                   ALU.subtract).then_inc(S("ulo_ready"), 1)

            for kind, c in PLAN:
                if kind == "pre":
                    pre_pool(c)
                elif kind == "gu":
                    with pool.Fori(0, FC // 2) as i:
                        for j in range(2):
                            split_hidden(c, 2 * i + j, j, c["N"], u_hi, u_lo)
                elif kind == "conv":
                    for k in range(DC):
                        split_hidden(c, k, k % 2, c["N"], u_hi, u_lo)
                elif kind == "attn":
                    for k in range(DC):
                        split_hidden(c, k, k % 2, T, h_hi, h_lo)
                elif kind == "mix":
                    for k in range(DC):
                        split_hidden(c, k, k % 2, T, h_hi, h_lo)


def cols(v):
    v = np.asarray(v)
    return np.ascontiguousarray(v.reshape(-1, P).T)


def in_units(w, heads=None):
    k, n = w.shape
    return w.reshape(k // P, P, n // P, P).transpose(2, 1, 0, 3).reshape(n // P, P, k)


def out_units(w):
    return w.reshape(-1, P, D)


def head_of(chunk, half):
    return (2 * (chunk // 4) + half) * 4 + chunk % 4


def weight_stream(a):
    units = []
    HD = 64

    def ffn(gu, down):
        g, u = in_units(gu[:, :DFF]), in_units(gu[:, DFF:])
        units.extend([np.stack([g, u], 1).reshape(2 * FC, P, D), out_units(down)])

    def ffn3(gate, up, down):
        units.extend([np.stack([in_units(gate), in_units(up)], 1).reshape(2 * FC, P, D), out_units(down)])

    for l in range(2):
        ffn(a["ffn_w_gu"][l, 0], a["ffn_w_down"][l, 0])
        if l == 0:
            w = in_units(a["conv_w_in"][0]).reshape(3, DC, P, D).transpose(1, 0, 2, 3).reshape(3 * DC, P, D)
            units.extend([w, out_units(a["conv_w_out"][0])])
        else:
            w = a["attn_w_qkv"][0]
            order = [head_of(c, h) for c in range(8) for h in range(2)]
            q = w[:, :1024].reshape(D, 16, HD)[:, order].reshape(D, 1024)
            wo = a["attn_w_o"][0].reshape(16, HD, D)[order].reshape(1024, D)
            units.extend([in_units(w[:, 1024:]), in_units(q), out_units(wo)])
        ffn(a["ffn_w_gu"][l, 1], a["ffn_w_down"][l, 1])
    for l in range(2):
        ffn3(a["ffn1_gate_2"][l], a["ffn1_up_2"][l], a["ffn1_down_2"][l])
        w = a["w_in_2"][l]
        z = np.zeros((D, P), w.dtype)

        def put(at, first, width, n=1):
            m = z.copy()
            for j in range(n):
                m[:, at + j * width:at + (j + 1) * width] = w[:, first:first + width]
            return m

        parts = [w[:, 1848:2360], w[:, 1064:1576], put(0, 1576, 16), w[:, 1592:1848], w[:, 2360:2744],
                 put(64, 2744, 32), w[:, 0:1024], put(0, 1024, 32, 4), put(0, 1056, 8)]
        units.append(in_units(np.concatenate(parts, 1)))
        uq = np.zeros((2, P, 4, P), w.dtype)
        uq[..., :96] = a["d_uq_2"][l].reshape(2, P, 4, 96)
        units.append(uq.transpose(1, 0, 2, 3).reshape(1, P, D))
        ukv = np.zeros((P, D), w.dtype)
        ukv[:, :512] = a["d_ukv_2"][l]
        units.append(ukv[None])
        units.append(out_units(a["w_out_2"][l].reshape(4, 256, D)[ORDER].reshape(1024, D)))
        ffn3(a["ffn2_gate_2"][l], a["ffn2_up_2"][l], a["ffn2_down_2"][l])
    return np.concatenate(units, 0)


ORDER = [2, 1, 3, 0]


def vectors(a):
    v = np.zeros((P, NVEC), np.float32)

    def put(name, m):
        v[:, VEC[name]:VEC[name] + m.shape[1]] = m

    put("g1", cols(a["norm_g"]))
    put("g2", cols(np.stack([a["ffn1_norm_2"], a["mix_norm_2"], a["ffn2_norm_2"]], 1)))
    put("convw", cols(a["conv_w"][0]))
    put("bmod", cols(a["b_mod"]))
    put("sink", np.broadcast_to(a["attn_sink"][0][[head_of(c, h) for c in range(8) for h in range(2)]], (P, 16)))
    for l in range(2):
        put(f"aq{l}", np.tile(a["a_q_norm_2"][l], 2)[:, None])
        put(f"ak{l}", np.tile(a["a_k_norm_2"][l], 2)[:, None])
        put(f"bg{l}", a["b_gate_bias_2"][l][:, None])
        put(f"bo{l}", np.tile(a["b_out_norm_2"][l], 2)[:, None])
        put(f"cw{l}", cols(a["c_dw_w_2"][l][:, 0]))
        put(f"cb{l}", cols(a["c_dw_b_2"][l]))
        put(f"cn{l}", cols(a["c_norm_2"][l]))
        put(f"dqa{l}", cols(a["d_qa_norm_2"][l]))
        put(f"dkva{l}", cols(a["d_kva_norm_2"][l]))
        for n in "qk":
            v[:96, VEC[f"d{n}{l}"]] = a[f"d_{n}_norm_2"][l]
    return v


def rotation(first, n, half):
    r = np.zeros((P, P), np.float32)
    for g in range(n):
        for i in range(half):
            p = first + 2 * half * g + i
            r[p + half, p] = -1.0
            r[p, p + half] = 1.0
    return r


def tables():
    f = np.float32
    one = np.ones((P, P), f)
    p = np.arange(P)
    b64 = (p[:, None] // 64 == p[None] // 64).astype(f)
    o96 = np.zeros((P, P), f)
    o96[:96] = 1.0
    k = np.arange(T)
    caus = ((p[:, None] + P) >= k[None]).astype(f)
    bmask = (p[:, None] // 32 == k[None] // 64).astype(f)
    ctabs = np.concatenate([one, np.eye(P, dtype=f), b64, o96, rotation(0, 4, 16), rotation(64, 1, 16),
                            caus, ((caus - 1) * f(3e38)).astype(f), bmask], 1)
    band = np.zeros((P, 2, 2 * T), f)
    for b in range(2):
        band[:, b, :T] = np.where(np.abs(P * b + p[:, None] - k[None]) <= 128, f(0), f(NEG))
    tok = np.arange(T)
    inv = (f(10000.0) ** (-np.arange(16, dtype=f) / f(16))).astype(f)
    ang = np.stack([(tok // 64).astype(f)[:, None] * inv, (tok % 64).astype(f)[:, None] * inv], 0)
    ang = ang[(p // 32) % 2, :, p % 16]
    C, Sn = np.cos(ang).astype(f), np.sin(ang).astype(f)
    att = np.concatenate([band.reshape(P, -1), C, Sn, C * f(0.125), Sn * f(0.125)], 1)
    ang = tok.astype(f)[None] * inv[p % 16][:, None]
    on = ((p >= 64) & (p < 96))[:, None]
    CD, SD = np.where(on, np.cos(ang), 1).astype(f), np.where(on, np.sin(ang), 0).astype(f)
    lev = []
    j, i = p[:, None], (k % P)[None]
    for s in (32, 16, 8, 4, 2, 1):
        lev.append((j // (2 * s) == i // (2 * s)) & (j // s % 2 == 0) & (i // s % 2 == 1))
    lev.append(j == i)
    lev = np.stack(lev, 1).astype(f).reshape(P, -1)
    scan = np.broadcast_to((k % 64 != 0).astype(f), (P, T))
    mix = np.concatenate([CD, SD, scan, lev], 1)
    dist = np.maximum(255 - np.arange(384), 0)
    large = 16 + (np.log(np.maximum(dist, 1).astype(f) / f(16)) / f(np.log(8.0)) * f(16)).astype(np.int32)
    buck = np.where(dist < 16, dist, np.minimum(large, 31))
    onehot = (np.arange(32)[:, None] == buck[None]).astype(f)
    return [np.ascontiguousarray(m.astype(f)) for m in (ctabs, att, mix, onehot)]


def chunked(x):
    return x.T.reshape(DC, P, -1).transpose(1, 0, 2)


def host(a):
    a = {k: np.asarray(v) for k, v in a.items()}
    ctabs, att, mix, onehot = tables()
    wm = np.concatenate([in_units(a["w_mod"][l]) for l in range(2)], 0)
    return dict(
        xin=np.ascontiguousarray(np.concatenate([chunked(a["x"][0]), chunked(a["ctx"][0])], 2)),
        wst=weight_stream(a), wmod=wm,
        cvec=np.ascontiguousarray(np.stack([cols(a["c"]), cols(a["c_ctx"])], 2)),
        vecs=vectors(a), ctabs=ctabs, attabs=att, mixtabs=mix,
        bup=np.ascontiguousarray(a["b_gate_up_2"].transpose(1, 0, 2)), relb=a["rel_bias_2"], onehot=onehot)


def kernel(**inputs):
    from concourse import bacc
    from concourse.bass_utils import run_bass_kernel_spmd

    arrays = host(inputs)
    nc = bacc.Bacc("TRN2", target_bir_lowering=False, num_devices=1)
    args = [nc.dram_tensor(n, v.shape, mybir.dt.from_np(v.dtype), kind="ExternalInput").ap() for n, v in arrays.items()]
    out = nc.dram_tensor("out", (P, DC, T), F32, kind="ExternalOutput").ap()
    build(nc, *args, out)
    r = run_bass_kernel_spmd(nc, [arrays], core_ids=[0]).results[0]["out"]
    return np.ascontiguousarray(r.transpose(1, 0, 2).reshape(D, T).T)[None]
```

```python
from contextlib import ExitStack

import numpy as np
import concourse.bass as bass
from concourse import mybir

F32 = mybir.dt.float32
F32R = mybir.dt.float32r
U32 = mybir.dt.uint32
ACT = mybir.ActivationFunctionType
ALU = mybir.AluOpType
AXX = mybir.AxisListType.X

P = 128
D = 1024
DC = D // P
T = 256
TT = T // P
DFF = 2816
FC = DFF // P
RING = 4
EPS = 1e-6
NMOD = 9
NEG = -1.0e30

def out_bank(d):
    return (d + 4) % 8

C_A, C_G = 0, 2
B_Q, B_K, B_V, B_G, B_R = 4, 5, 6, 8, 9
D_Q, D_KV, D_PE = 11, 13, 14
A_Q, A_K, A_V, I_Q, I_K, I_W = 15, 17, 19, 21, 23, 24
N_IN = 25
KTAPS = 31
SCORE_BANK = (0, 1, 6, 7)
LEVELS = 6

POOL_X = 2
X_ORDER = [0, 1, 6, 2, 3, 7, 4, 5]
MB = NMOD * D // 512
MOD_CONV = MB - FC // 2

def make_plan():
    plan = []
    c = dict(unit=0, norm=0, x=0, xp=0, out=0, post=0, ffn=0, fin=0, hid=0, h=0)

    def add(kind, **k):
        plan.append((kind, dict(c) | k))

    def pre(N, coef):
        add("pre", N=N, coef=coef)
        c["norm"] += 1
        c["h"] += DC

    def gu(N, late=False):
        add("gu", N=N, late=late)
        c["unit"] += 2 * FC
        c["ffn"] += 1
        c["fin"] += late
        c["hid"] += FC

    def out(N, nk):
        add("out", N=N, nk=nk)
        c["unit"] += nk
        c["out"] += 1

    def post(N, coef):
        add("post", N=N, coef=coef)
        c["norm"] += 1
        c["post"] += 1
        c["x"] += DC - POOL_X
        c["xp"] += POOL_X

    add("mod")
    c["unit"] += 4 * MB
    for l in range(2):
        for part in range(3):
            N = T if (l, part) == (1, 2) else 2 * T
            pre(2 * T if (l, part) == (1, 1) else N, (l, part))
            if (l, part) == (0, 0):
                add("gu_mod", N=N)
                c["unit"] += 4 * FC
                c["ffn"] += 1
                c["hid"] += FC
                out(N, FC)
            elif part != 1:
                gu(N)
                out(N, FC)
            elif l == 0:
                add("conv", N=N)
                c["unit"] += 3 * DC + 4 * MOD_CONV
                c["hid"] += DC
                out(N, DC)
            else:
                add("attn", N=N)
                c["unit"] += 12
                c["hid"] += DC
                out(T, DC)
                N = T
            post(N, (l, part))
    for l in range(2):
        for part in range(3):
            if (l, part) == (0, 0):
                add("pre2", coef=(2, 0), update=None)
                c["norm"] += 1
                c["h"] += DC
            if part != 1:
                gu(T, late=True)
                out(T, FC)
            else:
                add("mix", l=l)
                c["unit"] += N_IN + 2
                c["hid"] += DC
                out(T, DC)
            weight = 1.0 if part == 1 else 0.5
            if (l, part) == (1, 2):
                add("add", weight=weight)
                c["x"] += DC
            else:
                add("pre2", coef=(2 + l + (part == 2), (part + 1) % 3), update=weight)
                c["x"] += DC
                c["norm"] += 1
                c["h"] += DC
    return plan, c["unit"], c["x"]


PLAN, UNITS, NX = make_plan()

VEC = {}


def vec_columns():
    at = 0
    for name, n in [("g1", 12 * DC), ("g2", 6 * DC), ("convw", 3 * DC), ("bmod", 2 * NMOD * DC), ("sink", 16)] + [
            (f"{name}{l}", n) for l in range(2) for name, n in
            [("aq", 1), ("ak", 1), ("bg", 1), ("bo", 1), ("cw", 62), ("cb", 2), ("cn", 2), ("dqa", 2), ("dkva", 1),
             ("dq", 1), ("dk", 1)]]:
        VEC[name] = at
        at += n
    return at


NVEC = vec_columns()


def build(nc, xin, wst, cvec, vecs, ctabs, attabs, mixtabs, bup, relb, onehot, out):
    es = ExitStack()
    with es:
        def sb(name, shape, dt=F32, ctx=es):
            return ctx.enter_context(nc.sbuf_tensor(name, shape, dt))

        sems = {}

        def S(name):
            if name not in sems:
                sems[name] = es.enter_context(nc.semaphore(name))
            return sems[name]

        xT = sb("xT", [P, DC, 2 * T])
        h_hi = sb("h_hi", [P, DC, 2 * T], F32R)
        h_lo = sb("h_lo", [P, DC, 2 * T], F32R)
        w_hi = sb("w_hi", [P, RING, D], F32R)
        gt = sb("gt", [P, 2, 2 * T])
        ut = sb("ut", [P, 2, 2 * T])
        sq = sb("sq", [P, 2, 2 * T])
        modb = sb("modb", [4, 512])
        rt = sb("rt", [P, 2 * T])
        rstd = sb("rstd", [P, 2 * T])
        tabs = sb("tabs", [P, 6 * P + 3 * T])
        vec = sb("vec", [P, vecs.shape[1]])
        cv = sb("cv", [P, DC, 2])
        cs = sb("cs", [P, DC, 4], F32R)
        MOD = sb("MOD", [P, 2, NMOD * DC, 2])
        CA = sb("CA", [P, 2, 3, DC, 2])
        CG = sb("CG", [P, 2, 3, DC, 2])
        epsc = sb("epsc", [P, 1])
        zc = sb("zc", [P, 1])
        stepper = sb("stepper", [P, 4])

        ones, ident, bones64, ones96, permW, permD = (tabs[:, P * i:P * (i + 1)] for i in range(6))
        caus1, caus0, bmask = (tabs[:, 6 * P + T * i:6 * P + T * (i + 1)] for i in range(3))

        with ExitStack() as c1:
            raw = sb("raw", [P, RING, D], F32, c1)
        w_lo = sb("w_lo", [P, RING, D], F32R)

        biasA = sb("biasA", [P, 4, T])
        bupt = sb("bupt", [16, 2, P])

        with ExitStack() as c1:
            u_hi = sb("u_hi", [P, FC, 2 * T], F32R, c1)
            u_lo = sb("u_lo", [P, FC, 2 * T], F32R, c1)
        with ExitStack() as c1:
            sb("norm_pad", [P, DC, 2 * T], F32, c1)
            gy = sb("gy", [P, DC, 2 * T], F32, c1)
            tn = sb("tn", [P, DC, 2 * T], F32, c1)
            hf = sb("hf", [P, DC, 2 * T], F32, c1)
        with ExitStack() as c1:
            sqb = sb("sqb", [P, 4, 384], F32, c1)
            rbb = sb("rbb", [32, 4, P], F32, c1)
            oh = sb("oh", [32, 384], F32, c1)
            rl = sb("rl", [32, 4], F32, c1)
        with ExitStack() as c1:
            sb("conv_pad", [P, DC, 2 * T], F32, c1)
            cu = sb("cu", [P, 2, 2, T + 2], F32, c1)
            cy = sb("cy", [P, 2, 2, T], F32, c1)
        with ExitStack() as c1:
            AK = sb("AK", [P, 2, 2 * T], F32, c1)
            AV = sb("AV", [P, 2, 2 * T], F32, c1)
            AQ = sb("AQ", [P, DC, T], F32, c1)
            VV = sb("VV", [P, 4, 2 * P], F32, c1)
            atab = sb("atab", [P, attabs.shape[1]], F32, c1)
            rp1 = sb("rp1", [P, 2, 2, T], F32, c1)
            rp2 = sb("rp2", [P, 2, 2, T], F32, c1)
            sw = sb("sw", [P, 2, 2 * T], F32, c1)
            pw = sb("pw", [P, 2, 2 * T], F32, c1)
            pn = sb("pn", [P, 2, 2 * T], F32, c1)
            PTw = sb("PTw", [P, 2, 4, T], F32, c1)
            aw = sb("aw", [P, 2, 8], F32, c1)
        with ExitStack() as c1:
            Z = sb("Z", [P, N_IN, T], F32, c1)
            mtab = sb("mtab", [P, mixtabs.shape[1]], F32, c1)
            sqm = sb("sqm", [P, 8, T], F32, c1)
            rm = sb("rm", [P, 8 * T], F32, c1)
            cnf = sb("cnf", [P, 3, T], F32, c1)
            cn_hi = sb("cn_hi", [P, 3, T], F32R, c1)
            cn_lo = sb("cn_lo", [P, 3, T], F32R, c1)
            with ExitStack() as c2:
                hp = sb("hp", [P, 2, KTAPS - 1 + T], F32, c2)
                hc = sb("hc", [P, 2, T], F32, c2)
            with ExitStack() as c2:
                OB = sb("OB", [P, 2, T], F32, c2)
                G1, G2 = OB[:, 0, :], OB[:, 1, :]
                EB = sb("EB", [P, LEVELS + 2, T], F32, c2)
                QP = sb("QP", [P, LEVELS + 1, T], F32, c2)
                KP = sb("KP", [P, LEVELS + 1, T], F32, c2)
                AT = sb("AT", [P, 4, T], F32, c2)
                kdT = sb("kdT", [P, TT, P], F32, c2)
                VB = sb("VB", [P, TT, 2 * P], F32, c2)
                ST = sb("ST", [P, 3, 2 * P], F32, c2)
            with ExitStack() as c2:
                DQ = sb("DQ", [P, 4, T], F32, c2)
                DK = sb("DK", [P, 4, T], F32, c2)
                DV = sb("DV", [P, 4, T], F32, c2)
                dt1 = sb("dt1", [P, 4, T], F32, c2)
                QA = sb("QA", [P, 4, T], F32, c2)
                VT = sb("VT", [P, TT, 4, P], F32, c2)
                LG = dt1
                PR = DV
                PTm = sb("PTm", [P, TT, 4, T], F32, c2)
                am = sb("am", [P, 16], F32, c2)
            with ExitStack() as c2:
                RI = sb("RI", [P, 2, T], F32, c2)
                SCI = sb("SCI", [P, T], F32, c2)
                WK = sb("WK", [P, 2, T], F32, c2)
                SEL = sb("SEL", [P, T], F32, c2)
                m8 = sb("m8", [P, 2, 8], F32, c2)
                iw = sb("iw", [P, TT, 8], F32, c2)
        CD, SD, scanm = (mtab[:, T * i:T * (i + 1)] for i in range(3))
        levm = mtab[:, 3 * T:(3 + LEVELS + 1) * T].rearrange("p (l k) -> p l k", l=LEVELS + 1)
        bandW = atab[:, 0:4 * T].rearrange("p (b k) -> p b k", b=2)
        skew = nc.dram_tensor("skew", (P, 4, 384), F32).ap()
        mod_rows = nc.dram_tensor("mod_rows", (2, 4, NMOD * D), F32).ap()
        skewed = bass.AP(skew.tensor, 127, [[4 * 384 - 1, P], [384, 4], [1, T]])
        ropeW = [atab[:, 4 * T + T * i:4 * T + T * (i + 1)] for i in range(4)]

        ps = es.enter_context(nc.psum_tensor("ps", [P, 8, 512], F32))

        def unit(b, i, step=4):
            return b + step * i, b % 4, 16 * (b // 4 + 1) + 4 * step * i

        def split_hi(act, b, i=0, step=4):
            if isinstance(i, int) and b + step * i >= UNITS:
                return
            u, s, landed = unit(b, i, step)
            act.wait_ge(S(f"raw_landed{s}"), landed)
            act.activation(w_hi[:, s, :], raw[:, s, :], ACT.Copy).then_inc(S("hi_ready"), 1)

        def split_lo(dve, b, i=0, step=4):
            if isinstance(i, int) and b + step * i >= UNITS:
                return
            u, s, _ = unit(b, i, step)
            dve.wait_ge(S("hi_ready"), u + 1)
            dve.tensor_tensor(w_lo[:, s, :], raw[:, s, :], w_hi[:, s, :],
                              ALU.subtract).then_inc(S("lo_ready"), 1)

        def tile(pe, s, k, psum, hi, lo, start, stop):
            wh, wl = w_hi[:, s, P * k:P * (k + 1)], w_lo[:, s, P * k:P * (k + 1)]
            pe.matmul(psum, wh, hi, start=start, stop=False)
            pe.matmul(psum, wh, lo, start=False, stop=False)
            return pe.matmul(psum, wl, hi, start=False, stop=stop)

        def mod_unit(pe, b, i, step, q, m):
            u, s, _ = unit(b, i, step)
            if q == 0:
                pe.wait_ge(S("mod_evac"), m + 1)
            pe.wait_ge(S("lo_ready"), u + 1)
            for k in range(2):
                for part, w in enumerate((w_hi, w_lo)):
                    mm = pe.matmul(ps[0:4, 6, :], cs[:, 2 * q + k, :], w[:, s, 512 * k:512 * (k + 1)],
                                   start=(q + k + part == 0), stop=(q == 3 and k == 1 and part == 1))
            mm.then_inc(S("unit_done"), 1)

        def mod_evacuate(act, done, l, m, col):
            act.wait_ge(S("unit_done"), done)
            act.wait_ge(S("mod_stored"), 16 * m + 1)
            act.activation(modb[:, :], ps[0:4, 6, :], ACT.Copy).then_inc(S("mod_evac"), 1)
            act.wait_ge(S("mod_evac"), m + 2)
            act.dma_start(mod_rows[l, :, col], modb[:, :]).then_inc(S("mod_stored"), 16)

        def mod_reload(act, l):
            act.wait_ge(S("mod_stored"), 16 * MB * (l + 1) + 1)
            act.dma_start(rstd[0:NMOD * DC, :].rearrange("n (r p) -> n r p", r=4),
                          mod_rows[l].rearrange("r (n p) -> n r p", p=P)).then_inc(S("mod_loaded"), 16)

        def mod_transpose(pe, l):
            n = NMOD * DC
            pe.wait_ge(S("mod_loaded"), 16 * (l + 1))
            for r in range(4):
                mm = pe.transpose(ps[:, 7, n * r:n * (r + 1)], rstd[0:n, P * r:P * (r + 1)], ident[0:n, 0:n])
            mm.then_inc(S("mod_turned"), 1)

        def mod_finish(dve, l):
            n = NMOD * DC
            dve.wait_ge(S("mod_turned"), l + 1)
            by_part = ps[:, 7, 0:4 * n].rearrange("p (r n) -> p n r", r=4)
            bm = vec[:, VEC["bmod"] + n * l:VEC["bmod"] + n * (l + 1)].unsqueeze(2).broadcast_to([P, n, 2])
            dve.tensor_tensor(MOD[:, l], by_part[:, :, 0:2], bm, ALU.add).then_inc(S("mod_ready"), 1)
            dve.wait_ge(S("mod_ready"), 2 * l + 1)
            dve.tensor_tensor(MOD[:, l], MOD[:, l], by_part[:, :, 2:4], ALU.add).then_inc(S("mod_ready"), 1)
            dve.wait_ge(S("mod_ready"), 2 * l + 2)
            for part in range(3):
                for v in range(2):
                    g = VEC["g1"] + (l * 6 + 2 * part) * DC
                    m = 3 * part * DC
                    dve.scalar_tensor_tensor(CA[:, l, part, :, v], MOD[:, l, m + DC:m + 2 * DC, v], 1.0,
                                             vec[:, g:g + DC], ALU.add, ALU.mult)
                    ins = dve.scalar_tensor_tensor(CG[:, l, part, :, v], MOD[:, l, m + 2 * DC:m + 3 * DC, v],
                                                   1.0 if part == 1 else 0.5, vec[:, g + DC:g + 2 * DC],
                                                   ALU.mult, ALU.mult)
            ins.then_inc(S("coef_ready"), 1)
            dve.wait_ge(S("coef_ready"), l + 1)

        def in_unit(pe, b, i, bank, N, step=4, h=None, hi=h_hi, lo=h_lo):
            u, s, _ = unit(b, i, step)
            pe.wait_ge(S("lo_ready"), u + 1)
            for k in range(DC):
                if h is not None:
                    pe.wait_ge(S("h_ready"), h + k + 1)
                mm = tile(pe, s, k, ps[:, bank, 0:N], hi[:, k, 0:N], lo[:, k, 0:N], k == 0, k == DC - 1)
            mm.then_inc(S("unit_done"), 1)

        def wait_y(eng, c, t):
            if t < DC - 1:
                eng.wait_ge(S("y_done"), (DC - 1) * (c["out"] - 1) + t + 1)
            else:
                eng.wait_ge(S("unit_done"), c["unit"])

        def halves(N):
            return [(v, slice(T * v, T * (v + 1))) for v in range(N // T)]

        def coef(c, t, v):
            l, part = c
            if l < 2:
                return CA[:, l, part, t, v:v + 1], MOD[:, l, 3 * part * DC + t, v:v + 1]
            at = VEC["g2"] + ((l - 2) * 3 + part) * DC + t
            return vec[:, at:at + 1], zc[:, 0:1]

        S_STEP = [0]
        block = es.enter_context(nc.Block())

        @block.sync
        def _(sp):
            for s in range(RING):
                sp.dma_start(raw[:, s, :], wst[s]).then_inc(S(f"raw_landed{s}"), 16)
            with sp.Fori(1, UNITS // 4) as i:
                for s in range(RING):
                    sp.wait_ge(S("unit_done"), 4 * i + (s - 3))
                    sp.dma_start(raw[:, s, :], wst[4 * i + s]).then_inc(S(f"raw_landed{s}"), 16)
            for u in range(UNITS // 4 * 4, UNITS):
                sp.wait_ge(S("unit_done"), u - 3)
                sp.dma_start(raw[:, u % 4, :], wst[u]).then_inc(S(f"raw_landed{u % 4}"), 16)
            sp.wait_ge(S("x_ready"), NX)
            sp.dma_start(out, xT[:, :, 0:T]).then_inc(S("stored"), 16)
            sp.wait_ge(S("stored"), 16)

        @block.tensor
        def _(pe):
            def mod_pe(c):
                pe.wait_ge(S("cs_ready"), 2)
                with pe.Fori(0, MB) as i:
                    for q in range(4):
                        mod_unit(pe, c["unit"] + q, i, 4, q, i)
                mod_transpose(pe, 0)

            def stat(c, N, n):
                pe.wait_ge(S("sq_ready"), DC * c["norm"] + n + 1)
                pe.matmul(ps[:, 4, 0:N], ones, sq[:, n % 2, 0:N], start=(n == 0),
                          stop=(n == DC - 1)).then_inc(S("ss_done"), 1)

            def gu_pe(c):
                N, b = c["N"], c["unit"]
                with pe.Fori(0, FC // 2) as i:
                    for j in range(2):
                        in_unit(pe, b + 2 * j, i, j, N, h=c["h"] - DC if j == 0 else None)
                        in_unit(pe, b + 2 * j + 1, i, 2 + j, N)

            def gu_mod_pe(c):
                N, b = c["N"], c["unit"]
                with pe.Fori(0, FC // 2) as i:
                    for j in range(2):
                        for q in range(2):
                            in_unit(pe, b + 4 * j + 2 * q, i, 2 * q + j, N, 8, c["h"] - DC if j + q == 0 else None)
                            mod_unit(pe, b + 4 * j + 2 * q + 1, i, 8, 2 * j + q, MB + i)

            def out_pe(c, kind, follower):
                N, b, nk = c["N"], c["unit"], c["nk"]
                hi, lo = (h_hi, h_lo) if kind in ("attn", "mix") else (u_hi, u_lo)

                def one(j, i, k, start, stop):
                    u, s, _ = unit(b + j, i)
                    pe.wait_ge(S("lo_ready"), u + 1)
                    pe.wait_ge(S("ulo_ready"), c["hid"] - nk + k + 3)
                    for d in range(DC):
                        if start and d == 4:
                            pe.wait_ge(S("gated"), c["hid"])
                        mm = tile(pe, s, d, ps[:, out_bank(d), 0:N], hi[:, k, 0:N], lo[:, k, 0:N], start, stop)
                        if stop:
                            mm.then_inc(S("unit_done" if d == DC - 1 else "y_done"), 1)
                            if d == 2 and follower[0] == "post":
                                pe.wait_ge(S("gy_ready"), DC * follower[1]["post"] + 1)
                            elif d == 2 and follower[0] == "pre2":
                                pe.wait_ge(S("x_ready"), follower[1]["x"] + 1)
                            if d >= 2 and follower[0] != "add":
                                stat(follower[1], N, d - 2)
                    if stop and follower[0] != "add":
                        stat(follower[1], N, DC - 2)
                        stat(follower[1], N, DC - 1)
                    if not stop:
                        mm.then_inc(S("unit_done"), 1)

                if kind in ("gu_mod", "conv"):
                    pe.wait_ge(S("mod_evac"), (MB + FC // 2 if kind == "gu_mod" else 2 * MB) + 1)
                if kind not in ("gu", "gu_mod"):
                    pe.wait_ge(S("gated"), c["hid"])
                for k in range(2):
                    one(k, 0, k, k == 0, False)
                if nk == FC:
                    with pe.Fori(0, (nk - 4) // 4) as i:
                        for j in range(4):
                            one(2 + j, i, 4 * i + (2 + j), False, False)
                    first = 2 + (nk - 4) // 4 * 4
                else:
                    first = 2
                for k in range(first, nk):
                    one(k, 0, k, False, k == nk - 1)

            def conv_pe(c):
                N, b = c["N"], c["unit"]
                for n in range(DC):
                    if n >= 2:
                        pe.wait_ge(S("gated"), c["hid"] + n - 1)
                    for m in range(3):
                        in_unit(pe, b + 7 * n + (2 * m if n < MOD_CONV else m), 0, 3 * (n % 2) + m, N,
                                h=c["h"] - DC if n + m == 0 else None)
                        if n < MOD_CONV:
                            for q in ((0,), (1,), (2, 3))[m]:
                                mod_unit(pe, b + 7 * n + m + 1 + q, 0, 4, q, 2 * MB - MOD_CONV + n)
                mod_transpose(pe, 1)
                pe.wait_ge(S("mod_ready"), 4)

            def attn_pe(c):
                b = c["unit"]
                for n in range(12):
                    if n >= 4:
                        pe.wait_ge(S("w_evac"), n - 3)
                    in_unit(pe, b + n, 0, n % 4, 2 * T if n < 4 else T, h=c["h"] - DC if n == 0 else None)
                pe.wait_ge(S("w_evac"), 12)
                for n in range(10):
                    src = AK[:, n, 0:T] if n < 2 else AQ[:, n - 2, :]
                    mm = pe.matmul(ps[:, n // 2, T * (n % 2):T * (n % 2 + 1)], permW, src, start=True, stop=True)
                mm.then_inc(S("w_perm"), 1)
                for n in range(2):
                    for t in range(4):
                        mm = pe.transpose(ps[:, 5 + n, P * t:P * (t + 1)], AV[:, n, P * t:P * (t + 1)], ident)
                mm.then_inc(S("w_vt"), 1)
                pe.wait_ge(S("w_rope"), 5)
                pe.wait_ge(S("w_vv"), 2)

                def scores(n):
                    cc, hf, qb = n // 4, n // 2 % 2, n % 2
                    r = slice(64 * hf, 64 * hf + 64)
                    if n >= 4:
                        pe.wait_ge(S("w_sb"), n - 3)
                    pe.matmul(ps[:, SCORE_BANK[n % 4], 0:512], AQ[r, cc, P * qb:P * (qb + 1)], AK[r, cc // 4, :],
                              start=True, stop=True).then_inc(S("w_s"), 1)

                def turn(n):
                    pe.wait_ge(S("w_pn"), n + 1)
                    if n >= 2:
                        pe.wait_ge(S("w_pt"), n - 1)
                    for t in range(4):
                        mm = pe.transpose(ps[:, 2 + n % 2, P * t:P * (t + 1)], pn[:, n % 2, P * t:P * (t + 1)], ident)
                    mm.then_inc(S("w_tr"), 1)

                def values(n):
                    cc, hf = n // 4, n // 2 % 2
                    pe.wait_ge(S("w_pt"), n + 1)
                    if hf == 0 and cc >= 2:
                        pe.wait_ge(S("gated"), c["hid"] + cc - 1)
                    r = slice(64 * hf, 64 * hf + 64)
                    for t in range(4):
                        v0 = P * (cc // 4) + 64 * hf
                        mm = pe.matmul(ps[r, 4 + cc % 2, 0:T], VV[:, t, v0:v0 + 64], PTw[:, hf, t, :],
                                       start=(t == 0), stop=(t == 3))
                    mm.then_inc(S("w_pv"), 1)

                scores(0)
                scores(1)
                for n in range(32):
                    if n + 2 < 32:
                        scores(n + 2)
                    turn(n)
                    if n % 2 == 0 and n:
                        values(n - 1)
                values(31)

            def pair_slot(h):
                return 2 * (h % 2) + h // 2

            def mix_pe(c):
                b, l = c["unit"], c["l"]

                def need(name, per, k):
                    pe.wait_ge(S(name), per * l + k)

                for n in range(N_IN):
                    if n >= 4:
                        need("m_evac", N_IN, n - 3)
                    in_unit(pe, b + n, 0, n % 4, T, h=c["h"] - DC if n == 0 else None)
                need("m_evac", N_IN, N_IN)
                need("m_sq1", 1, 1)
                for n in range(2):
                    pe.matmul(ps[:, 0, 0:T], ones, sqm[:, n, :], start=(n == 0), stop=(n == 1))
                pe.matmul(ps[:, 0, T:2 * T], ones, sqm[:, 2, :], start=True, stop=True)
                for n in range(2):
                    mm = pe.matmul(ps[:, 1 + n, :], bones64, sqm[:, 4 + 2 * n:6 + 2 * n, :].rearrange("p a t -> p (a t)"),
                                   start=True, stop=True)
                mm.then_inc(S("m_ss1"), 1)
                need("m_sqc", 1, 1)
                for n in range(2):
                    mm = pe.matmul(ps[:, 3, 0:T], ones, sqm[:, n, :], start=(n == 0), stop=(n == 1))
                mm.then_inc(S("m_ssc"), 1)

                pe.matmul(ps[:, 4, 0:T], bupt[:, l, :], Z[0:16, B_G, :], start=True, stop=True).then_inc(S("b_gate"), 1)
                for m in range(2):
                    for t in range(TT):
                        mm = pe.transpose(ps[:, 5, P * (2 * t + m):P * (2 * t + m + 1)], Z[:, B_V + m, P * t:P * (t + 1)],
                                          ident)
                mm.then_inc(S("b_vt"), 1)
                need("b_qk", 1, 1)
                for t in range(TT):
                    mm = pe.transpose(ps[:, 6, P * t:P * (t + 1)], KP[:, LEVELS, P * t:P * (t + 1)], ident)
                mm.then_inc(S("b_kt"), 1)
                need("b_vb", 2, 2)
                for k in range(3):
                    r = slice(64 * (k % 2), 64 * (k % 2) + 64)
                    mm = pe.matmul(ps[:, 7, 0:2 * P] if k == 0 else ps[:, 3 + k, 0:2 * P] if k == 1 else ps[:, 5, 0:2 * P],
                                   kdT[r, k // 2, :], VB[r, k // 2, :], start=True, stop=True)
                mm.then_inc(S("b_st"), 1)
                need("m_rt", 2, 2)
                for v in range(LEVELS + 1):
                    if v >= 1:
                        need("b_at", LEVELS + 1, v)
                    for h in range(4):
                        r = slice(32 * h, 32 * h + 32)
                        for t in range(TT):
                            kk = KP[r, v, P * t:P * (t + 1)] if v < LEVELS else Z[r, B_K, P * t:P * (t + 1)]
                            qq = QP[r, v, P * t:P * (t + 1)] if v < LEVELS else Z[r, B_Q, P * t:P * (t + 1)]
                            mm = pe.matmul(ps[:, h, P * t:P * (t + 1)], kk, qq, start=True, stop=True)
                    mm.then_inc(S("b_lv"), 1)
                need("b_at", LEVELS + 1, LEVELS + 1)
                need("b_s", 2, 2)
                for h in range(4):
                    for t in range(TT):
                        r = slice(64 * (h % 2), 64 * (h % 2) + 64)
                        pe.matmul(ps[r, 4, T * (h // 2) + P * t:T * (h // 2) + P * (t + 1)],
                                  VB[:, t, 64 * h:64 * h + 64], AT[:, h, P * t:P * (t + 1)], start=True, stop=True)
                for m in range(2):
                    for k in range(1, 4):
                        mm = pe.matmul(ps[:, 5, T * m + 64 * k:T * m + 64 * (k + 1)], ST[:, k - 1, P * m:P * (m + 1)],
                                       QP[:, LEVELS, 64 * k:64 * (k + 1)], start=True, stop=True)
                mm.then_inc(S("b_o"), 1)
                need("b_sq", 1, 1)
                pe.matmul(ps[:, 6, :], bones64, sqm[:, 0:2, :].rearrange("p a t -> p (a t)"), start=True,
                          stop=True).then_inc(S("b_ss"), 1)

                need("d_cn", 1, 1)
                pe.wait_ge(S("lo_ready"), b + N_IN + 1)
                for h in range(4):
                    for k in range(2):
                        mm = tile(pe, (b + N_IN) % RING, 4 * k + h, ps[:, h // 2, T * (h % 2):T * (h % 2 + 1)], cn_hi[:, k, :],
                                  cn_lo[:, k, :], k == 0, k == 1)
                mm.then_inc(S("unit_done"), 1)
                pe.wait_ge(S("lo_ready"), b + N_IN + 2)
                for h in range(4):
                    mm = tile(pe, (b + N_IN + 1) % RING, h, ps[:, 2 + h // 2, T * (h % 2):T * (h % 2 + 1)], cn_hi[:, 2, :],
                              cn_lo[:, 2, :], True, True)
                mm.then_inc(S("unit_done"), 1)
                need("d_sq", 1, 1)
                for n in range(4):
                    mm = pe.matmul(ps[0:96, n, :], ones[0:96, 0:96], sqm[0:96, 2 * n:2 * n + 2, :].rearrange("p a t -> p (a t)"),
                                   start=True, stop=True)
                mm.then_inc(S("d_ss"), 1)
                need("d_n", 2, 2)
                for n in range(4):
                    src = (DQ if n < 2 else DK)[0:96, 2 * (n % 2):2 * (n % 2) + 2, :].rearrange("p a t -> p (a t)")
                    mm = pe.matmul(ps[0:96, n, :], permD[0:96, 0:96], src, start=True, stop=True)
                mm.then_inc(S("d_perm"), 1)
                need("d_e", 4, 4)
                for t in range(TT):
                    for h in range(4):
                        mm = pe.transpose(ps[:, 4 + t, P * h:P * (h + 1)], DV[:, h, P * t:P * (t + 1)], ident)
                mm.then_inc(S("d_vt"), 1)

                def attend(slot, q, k, v, q0, qb):
                    kc = P * (qb + 1)
                    for h in range(4):
                        g = slot(h)
                        mm = pe.matmul(ps[:, g // 2, T * (g % 2):T * (g % 2) + kc], q(h)[:, P * qb:P * (qb + 1)],
                                       k(h)[:, 0:kc], start=True, stop=True)
                    mm.then_inc(S("s_s"), 1)
                    pe.wait_ge(S("s_p"), 4 * l + q0 + qb + 1)
                    for t in range(qb + 1):
                        for h in range(4):
                            mm = pe.transpose(ps[:, 2 + t, P * h:P * (h + 1)], PR[:, h, P * t:P * (t + 1)], ident)
                    mm.then_inc(S("s_tr"), 1)
                    pe.wait_ge(S("s_pt"), 4 * l + q0 + qb + 1)
                    for h in range(4):
                        r = slice(64 * (h % 2), 64 * (h % 2) + 64)
                        for t in range(qb + 1):
                            mm = pe.matmul(ps[r, 6, T * (h // 2) + P * qb:T * (h // 2) + P * (qb + 1)], v(t, h),
                                           PTm[:, t, slot(h), P * qb:P * (qb + 1)], start=(t == 0), stop=(t == qb))
                    mm.then_inc(S("s_pv"), 1)

                need("d_r", 2, 2)
                need("d_vt2", 2, 2)
                for qb in range(TT):
                    attend(lambda h: h, lambda h: DQ[0:96, h, :], lambda h: DK[0:96, h, :], lambda t, h: VT[:, t, h, 64:128], 0, qb)

                for t in range(TT):
                    mm = pe.transpose(ps[:, 7, 8 * t:8 * t + 8], Z[0:8, I_W, P * t:P * (t + 1)], ident[0:8, 0:8])
                mm.then_inc(S("i_wt"), 1)
                for m in range(2):
                    for t in range(TT):
                        mm = pe.transpose(ps[:, 5, P * (2 * t + m):P * (2 * t + m + 1)], Z[:, A_V + m, P * t:P * (t + 1)],
                                          ident)
                mm.then_inc(S("a_vt"), 1)
                for qb in range(TT):
                    kc = P * (qb + 1)
                    if qb == 1:
                        pass
                    for h in range(8):
                        r = slice(32 * (h % 4), 32 * (h % 4) + 32)
                        n = 8 * qb + h
                        if n >= 2:
                            need("i_r", 16, n - 1)
                        pe.matmul(ps[:, 2 + n % 2, 0:kc], Z[r, I_Q + h // 4, P * qb:P * (qb + 1)], Z[r, I_K, 0:kc],
                                  start=True, stop=True).then_inc(S("i_s"), 1)
                need("a_vt2", 1, 1)
                need("i_r", 16, 16)
                for qb in range(TT):
                    attend(pair_slot, lambda h: QA[64 * (h % 2):64 * (h % 2) + 64, h // 2, :],
                           lambda h: QA[64 * (h % 2):64 * (h % 2) + 64, 2 + h // 2, :],
                           lambda t, h: VT[:, t, h // 2, 64 * (h % 2):64 * (h % 2) + 64], 2, qb)

            pe.wait_ge(S("rbb_ready"), 1)
            for h in range(4):
                mm = pe.matmul(ps[:, 1 + pair_slot(h), 0:384], rbb[:, h, :], oh[:, :], start=True, stop=True)
            mm.then_inc(S("bias_rows"), 1)
            plan = list(PLAN)
            for n, (kind, c) in enumerate(plan):
                if kind == "mod":
                    mod_pe(c)
                elif kind == "gu_mod":
                    gu_mod_pe(c)
                elif kind == "pre" or kind == "pre2" and n == 0:
                    for t in range(DC):
                        stat(c, c.get("N", T), t)
                elif kind == "pre2" and c["update"] is None:
                    for t in range(DC):
                        stat(c, T, t)
                elif kind == "gu":
                    gu_pe(c)
                elif kind == "out":
                    out_pe(c, plan[n - 1][0], plan[n + 1] if n + 1 < len(plan) else ("add", None))
                elif kind == "conv":
                    conv_pe(c)
                elif kind == "attn":
                    attn_pe(c)
                elif kind == "mix":
                    mix_pe(c)

        @block.scalar
        def _(act):
            def root(c, N, scale):
                act.wait_ge(S("ss_done"), DC * (c["norm"] + 1))
                act.activation(rt[:, 0:N], ps[:, 4, 0:N], ACT.Sqrt, bias=epsc[:, 0:1],
                               scale=scale).then_inc(S("rt_ready"), 1)

            def square(c, N, n, src):
                if DC * c["norm"] + n - 1 > 0:
                    act.wait_ge(S("ss_done"), DC * c["norm"] + n - 1)
                act.activation(sq[:, n % 2, 0:N], src, ACT.Square).then_inc(S("sq_ready"), 1)

            def wait_x(c, t):
                if not c["x"]:
                    act.wait_ge(S("x_loaded"), 16)
                elif t < DC - POOL_X:
                    act.wait_ge(S("x_ready"), c["x"] - (DC - POOL_X) + t + 1)
                else:
                    act.wait_ge(S("xp_ready"), c["xp"] - DC + t + 1)

            def pre_act(c):
                N = c["N"]
                for n, t in enumerate(X_ORDER):
                    wait_x(c, t)
                    square(c, N, n, xT[:, t, 0:N])
                root(c, N, 1.0 / D)
                for t in range(DC):
                    act.wait_ge(S("tn_ready"), c["h"] + t + 1)
                    for v, r in halves(N):
                        a, s = coef(c["coef"], t, v)
                        ins = act.activation(hf[:, t, r], tn[:, t, r], ACT.Identity, bias=s, scale=a)
                    ins.then_inc(S("hf_ready"), 1)

            def pre2_act(c):
                for t in range(DC):
                    if c["update"] is None:
                        wait_x(c, t)
                    else:
                        act.wait_ge(S("x_ready"), c["x"] + t + 1)
                    square(c, T, t, xT[:, t, 0:T])
                    a, _ = coef(c["coef"], t, 0)
                    act.activation(h_hi[:, t, 0:T], xT[:, t, 0:T], ACT.Identity, scale=a).then_inc(S("h_hi_ready"), 1)
                root(c, T, 1.0 / D)

            def gu_act(c):
                N, b = c["N"], c["unit"]
                with act.Fori(0, FC // 2) as i:
                    for j in range(2):
                        split_hi(act, b + 2 * j + 2, i)
                        if c["late"]:
                            act.wait_ge(S("gate_scaled"), FC * c["fin"] + 2 * i + (j + 1))
                        else:
                            act.wait_ge(S("unit_done"), b + 2 * j + 1 + 4 * i)
                        act.activation(gt[:, j, 0:N], gt[:, j, 0:N] if c["late"] else ps[:, j, 0:N],
                                       ACT.Silu).then_inc(S("silu_done"), 1)
                        split_hi(act, b + 2 * j + 3, i)

            def gu_mod_act(c):
                N, b = c["N"], c["unit"]
                with act.Fori(0, FC // 2) as i:
                    for j in range(2):
                        split_hi(act, b + 4 * j + 2, i, 8)
                        act.wait_ge(S("unit_done"), b + 4 * j + 1 + 8 * i)
                        act.activation(gt[:, j, 0:N], ps[:, j, 0:N], ACT.Silu).then_inc(S("silu_done"), 1)
                        split_hi(act, b + 4 * j + 3, i, 8)
                        split_hi(act, b + 4 * j + 4, i, 8)
                        if j == 1:
                            mod_evacuate(act, b + 8 + 8 * i, 1, MB + i, bass.ds(512 * i, 512))
                        split_hi(act, b + 4 * j + 5, i, 8)

            def mod_act(c):
                b = c["unit"]
                with act.Fori(0, MB) as i:
                    for q in range(3):
                        split_hi(act, b + q + 2, i)
                    mod_evacuate(act, b + 4 + 4 * i, 0, i, bass.ds(512 * i, 512))
                    split_hi(act, b + 5, i)
                mod_reload(act, 0)

            def out_act(c):
                b, nk = c["unit"], c["nk"]
                full = (nk // 4) if b + nk + 2 <= UNITS else nk // 4 - 1
                with act.Fori(0, full) as i:
                    for j in range(4):
                        split_hi(act, b + 2 + j, i)
                for k in range(4 * full, nk):
                    split_hi(act, b + 2 + k)

            def post_act(c):
                N = c["N"]
                for t in range(DC):
                    wait_y(act, c, t)
                    square(c, N, t, ps[:, out_bank(t), 0:N])
                root(c, N, 1.0 / D)

            def conv_act(c):
                b = c["unit"]
                for n in range(DC):
                    first = b + 7 * n
                    split_hi(act, first + 2)
                    split_hi(act, first + 3)
                    act.wait_ge(S("unit_done"), first + (3 if n < MOD_CONV else 2))
                    if n >= 2:
                        act.wait_ge(S("cu_ready"), n - 1)
                    act.activation(gt[:, n % 2, :], ps[:, 3 * (n % 2) + 1, :], ACT.Copy).then_inc(S("cg_ready"), 1)
                    for q in range(4, 8 if n < MOD_CONV else 5):
                        split_hi(act, first + q)
                    act.wait_ge(S("cu_ready"), n + 1)
                    if n >= 2:
                        act.wait_ge(S("gated"), c["hid"] + n - 1)
                    w = VEC["convw"] + DC + n
                    act.activation(cy[:, n % 2, :, :], cu[:, n % 2, :, 1:T + 1], ACT.Copy,
                                   scale=vec[:, w:w + 1]).then_inc(S("cy_ready"), 1)
                    if n < MOD_CONV:
                        m = 2 * MB - MOD_CONV + n
                        mod_evacuate(act, first + 7, 1, m, slice(512 * (m - MB), 512 * (m - MB + 1)))
                        split_hi(act, first + 8)
                    if n == MOD_CONV - 1:
                        mod_reload(act, 1)

            def attn_act(c):
                b = c["unit"]
                act.wait_ge(S("unit_done"), b)
                act.dma_start(atab[:, :], attabs).then_inc(S("atab_loaded"), 16)
                for n in range(12):
                    split_hi(act, b + n + 2)
                    act.wait_ge(S("unit_done"), b + n + 1)
                    dst = AK[:, n, :] if n < 2 else AV[:, n - 2, :] if n < 4 else AQ[:, n - 4, :]
                    act.activation(dst, ps[:, n % 4, 0:2 * T if n < 4 else T], ACT.Copy).then_inc(S("w_evac"), 1)
                act.wait_ge(S("w_vt"), 1)
                for n in range(2):
                    act.activation(VV[:, :, P * n:P * (n + 1)],
                                   ps[:, 5 + n, :].rearrange("p (t v) -> p t v", t=4), ACT.Copy).then_inc(S("w_vv"), 1)

                def pt(n):
                    hf, qb = n // 2 % 2, n % 2
                    act.wait_ge(S("w_tr"), n + 1)
                    if n >= 4:
                        act.wait_ge(S("w_pv"), n // 2 - 1)
                    act.activation(PTw[:, hf, :, P * qb:P * (qb + 1)],
                                   ps[:, 2 + n % 2, :].rearrange("p (t q) -> p t q", t=4), ACT.Copy).then_inc(S("w_pt"), 1)

                for n in range(32):
                    head = 2 * (n // 4) + n // 2 % 2
                    sk = VEC["sink"] + head
                    act.wait_ge(S("w_nm"), n + 1)
                    if n >= 2:
                        act.wait_ge(S("w_pn"), n - 1)
                    act.activation(pw[:, n % 2, :], sw[:, n % 2, :], ACT.Exp, bias=aw[:, n % 2, 1:2],
                                   accum_out=aw[:, n % 2, 2:3]).then_inc(S("w_e"), 1)
                    act.activation(aw[:, n % 2, 3:4], vec[:, sk:sk + 1], ACT.Exp,
                                   bias=aw[:, n % 2, 1:2]).then_inc(S("w_e"), 1)
                    if n >= 1:
                        pt(n - 1)
                pt(31)


            def mix_act(c):
                b, l = c["unit"], c["l"]

                def need(name, per, k):
                    act.wait_ge(S(name), per * l + k)

                act.wait_ge(S("unit_done"), b)
                act.dma_start(mtab[:, :], mixtabs).then_inc(S("mtab_loaded"), 16)
                for n in range(N_IN):
                    split_hi(act, b + n + 2)
                    if n == C_G + 2:
                        need("m_evac", N_IN, C_G + 2)
                        act.activation(Z[:, C_G:C_G + 2, :], Z[:, C_G:C_G + 2, :], ACT.Sigmoid).then_inc(S("c_sig"), 1)
                need("m_evac", N_IN, N_IN)
                act.activation(sqm[:, :, :], Z[:, D_Q:D_Q + 8, :], ACT.Square).then_inc(S("m_sq1"), 1)
                need("m_ss1", 1, 1)
                act.activation(rm[:, 0:T], ps[:, 0, 0:T], ACT.Sqrt, bias=epsc[:, 0:1], scale=1 / 256)
                act.activation(rm[:, T:2 * T], ps[:, 0, T:2 * T], ACT.Sqrt, bias=epsc[:, 0:1], scale=1 / 128)
                act.activation(rm[:, 2 * T:6 * T], ps[:, 1:3, :].rearrange("p a t -> p (a t)"), ACT.Sqrt,
                               bias=epsc[:, 0:1], scale=1 / 64).then_inc(S("m_rt"), 1)
                need("c_tap", 2 * KTAPS, 2 * KTAPS)
                act.activation(sqm[:, 0:2, :], hc[:, :, :], ACT.Square).then_inc(S("m_sqc"), 1)
                need("m_ssc", 1, 1)
                act.activation(rm[:, 6 * T:7 * T], ps[:, 3, 0:T], ACT.Sqrt, bias=epsc[:, 0:1],
                               scale=1 / 256).then_inc(S("m_rt"), 1)
                need("c_n", 1, 1)
                act.activation(hc[:, :, :], hc[:, :, :], ACT.Silu).then_inc(S("c_silu"), 1)
                act.wait_ge(S("gated"), c["hid"] + 2)
                need("b_vt", 1, 1)
                act.activation(VB[:, :, :].rearrange("p a t -> p (a t)"), ps[:, 5, :], ACT.Copy).then_inc(S("b_vb"), 1)
                need("b_g", 1, 1)
                act.activation(G2, G1, ACT.Abs).then_inc(S("b_a"), 1)
                need("b_a", 3, 1)
                act.activation(G2, G2, ACT.Exp, scale=-1.0).then_inc(S("b_a"), 1)
                need("b_a", 3, 2)
                act.activation(G2, G2, ACT.Ln, bias=1.0).then_inc(S("b_a"), 1)
                need("b_e", 1, 1)
                act.activation(EB[:, :, :], EB[:, :, :], ACT.Exp, scale=1 / 16).then_inc(S("b_p"), 1)
                need("b_kt", 1, 1)
                act.activation(kdT[:, :, :].rearrange("p a t -> p (a t)"), ps[:, 6, 0:2 * P], ACT.Copy).then_inc(S("b_vb"), 1)
                need("b_o", 1, 1)
                act.activation(OB[:, :, :].rearrange("p a t -> p (a t)"), ps[:, 4, :], ACT.Copy).then_inc(S("b_oc"), 1)
                need("b_oi", 1, 1)
                act.activation(sqm[:, 0:2, :], OB[:, :, :], ACT.Square).then_inc(S("b_sq"), 1)
                need("b_ss", 1, 1)
                act.activation(rm[:, 0:2 * T], ps[:, 6, :], ACT.Sqrt, bias=epsc[:, 0:1], scale=1 / 64).then_inc(S("b_rt"), 1)
                act.activation(Z[:, B_R:B_R + 2, :], Z[:, B_R:B_R + 2, :], ACT.Silu).then_inc(S("b_silu"), 1)
                act.wait_ge(S("gated"), c["hid"] + 4)
                act.wait_ge(S("unit_done"), b + N_IN + 2)
                act.activation(DQ[:, :, :], ps[:, 0:2, :].rearrange("p a (b t) -> p (a b) t", b=2), ACT.Copy).then_inc(S("d_e"), 1)
                act.activation(DV[:, :, :], ps[:, 2:4, :].rearrange("p a (b t) -> p (a b) t", b=2), ACT.Copy).then_inc(S("d_e"), 1)
                act.activation(DK[0:64, :, :], ps[0:64, 2:4, :].rearrange("p a (b t) -> p (a b) t", b=2),
                               ACT.Copy).then_inc(S("d_e"), 1)
                act.activation(DK[64:96, :, :], Z[64:96, D_PE, :].unsqueeze(1).broadcast_to([32, 4, T]),
                               ACT.Copy).then_inc(S("d_e"), 1)
                split_hi(act, b + N_IN + 2)
                split_hi(act, b + N_IN + 3)
                need("d_e", 4, 4)
                act.activation(sqm[0:96, 0:4, :], DQ[0:96, :, :], ACT.Square)
                act.activation(sqm[0:96, 4:8, :], DK[0:96, :, :], ACT.Square).then_inc(S("d_sq"), 1)
                need("d_ss", 1, 1)
                act.activation(rm[0:96, :], ps[0:96, 0:4, :].rearrange("p a t -> p (a t)"), ACT.Sqrt,
                               bias=epsc[0:96, 0:1], scale=1 / 96).then_inc(S("d_rt"), 1)
                need("d_vt", 1, 1)
                for t in range(TT):
                    act.activation(VT[:, t, :, :], ps[:, 4 + t, :].rearrange("p (h v) -> p h v", h=4),
                                   ACT.Copy).then_inc(S("d_vt2"), 1)

                def attend(q0, qb):
                    kc, n = P * (qb + 1), 4 * l + q0 + qb + 1
                    act.wait_ge(S("s_nm"), n)
                    for h in range(4):
                        ins = act.activation(PR[:, h, 0:kc], LG[:, h, 0:kc], ACT.Exp, bias=am[:, 4 + h:5 + h],
                                             accum_out=am[:, 8 + h:9 + h])
                    ins.then_inc(S("s_e"), 1)
                    act.wait_ge(S("s_tr"), n)
                    for t in range(qb + 1):
                        ins = act.activation(PTm[:, t, :, P * qb:P * (qb + 1)],
                                             ps[:, 2 + t, :].rearrange("p (h q) -> p h q", h=4), ACT.Copy)
                    ins.then_inc(S("s_pt"), 1)

                for qb in range(TT):
                    attend(0, qb)
                need("i_wt", 1, 1)
                act.activation(iw[:, :, :].rearrange("p a t -> p (a t)"), ps[:, 7, 0:16], ACT.Copy,
                               scale=8 ** -0.5).then_inc(S("i_w"), 1)
                need("a_vt", 1, 1)
                act.activation(VT[:, :, 0:2, :].rearrange("p t a v -> p t (a v)"),
                               ps[:, 5, :].rearrange("p (t v) -> p t v", t=2), ACT.Copy).then_inc(S("a_vt2"), 1)
                for n in range(16):
                    kc = P * (n // 8 + 1)
                    need("i_s", 16, n + 1)
                    if n >= 2:
                        need("i_a", 16, n - 1)
                    act.activation(RI[:, n % 2, 0:kc], ps[:, 2 + n % 2, 0:kc], ACT.Relu,
                                   scale=32 ** -0.5).then_inc(S("i_r"), 1)
                for qb in range(TT):
                    attend(2, qb)

            act.dma_start(cv[:, :, :], cvec).then_inc(S("small_loaded"), 16)
            act.dma_start(vec[:, :], vecs).then_inc(S("small_loaded"), 16)
            act.dma_start(tabs[:, :], ctabs).then_inc(S("small_loaded"), 16)
            act.dma_start(bupt[:, :, :], bup).then_inc(S("small_loaded"), 16)
            act.dma_start(rl[:, :], relb).then_inc(S("small_loaded"), 16)
            act.dma_start(oh[:, :], onehot).then_inc(S("small_loaded"), 16)
            act.dma_start(xT[:, :, :], xin).then_inc(S("x_loaded"), 16)
            act.wait_ge(S("small_loaded"), 96)
            act.wait_ge(S("init"), 1)
            act.activation(cv[:, :, :], cv[:, :, :], ACT.Silu).then_inc(S("cv_ready"), 1)
            act.wait_ge(S("cv_ready"), 1)
            act.activation(cs[:, :, 0:2], cv[:, :, :], ACT.Copy).then_inc(S("cs_ready"), 1)
            act.wait_ge(S("bias_rows"), 1)
            act.activation(sqb[:, :, :], ps[:, 1:5, 0:384], ACT.Copy).then_inc(S("bias_copied"), 1)
            act.wait_ge(S("bias_copied"), 1)
            act.dma_start(skew, sqb[:, :, :]).then_inc(S("skew_stored"), 16)
            split_hi(act, 0)
            split_hi(act, 1)
            act.wait_ge(S("skew_stored"), 16)
            act.dma_start(biasA[:, :, :], skewed).then_inc(S("bias_loaded"), 16)
            for kind, c in PLAN:
                if kind == "mod":
                    mod_act(c)
                elif kind == "gu_mod":
                    gu_mod_act(c)
                elif kind == "pre":
                    pre_act(c)
                elif kind == "pre2":
                    pre2_act(c)
                elif kind == "gu":
                    gu_act(c)
                elif kind == "out":
                    out_act(c)
                elif kind == "post":
                    post_act(c)
                elif kind == "conv":
                    conv_act(c)
                elif kind == "attn":
                    attn_act(c)
                elif kind == "mix":
                    mix_act(c)

        @block.vector
        def _(dve):
            def recip(c, N):
                dve.wait_ge(S("rt_ready"), c["norm"] + 1)
                dve.reciprocal(rstd[:, 0:N], rt[:, 0:N]).then_inc(S("rstd_ready"), 1)
                dve.wait_ge(S("rstd_ready"), c["norm"] + 1)

            def pre_dve(c):
                N, h = c["N"], c["h"]
                recip(c, N)
                for t in range(DC + 2):
                    if t < DC:
                        dve.tensor_tensor(tn[:, t, 0:N], xT[:, t, 0:N], rstd[:, 0:N], ALU.mult).then_inc(S("tn_ready"), 1)
                    if t >= 2:
                        dve.wait_ge(S("h_hi_ready"), h + t - 1)
                        dve.tensor_tensor(h_lo[:, t - 2, 0:N], hf[:, t - 2, 0:N], h_hi[:, t - 2, 0:N],
                                          ALU.subtract).then_inc(S("h_ready"), 1)

            def pre2_dve(c):
                h = c["h"]
                for t in range(DC + 2):
                    if t < DC and c["update"] is not None:
                        wait_y(dve, c, t)
                        dve.scalar_tensor_tensor(xT[:, t, 0:T], ps[:, out_bank(t), 0:T], c["update"], xT[:, t, 0:T],
                                                 ALU.mult, ALU.add).then_inc(S("x_ready"), 1)
                    if t >= 2:
                        if c["update"] is None and t == DC - POOL_X + 2:
                            dve.wait_ge(S("xp_ready"), c["xp"])
                        dve.wait_ge(S("h_hi_ready"), h + t - 1)
                        a, _ = coef(c["coef"], t - 2, 0)
                        dve.scalar_tensor_tensor(h_lo[:, t - 2, 0:T], xT[:, t - 2, 0:T], a, h_hi[:, t - 2, 0:T],
                                                 ALU.mult, ALU.subtract).then_inc(S("h_ready"), 1)
                recip(c, T)

            def gu_late_dve(c):
                b, hid = c["unit"], c["hid"]
                with dve.Fori(0, FC // 2) as i:
                    for j in range(2):
                        split_lo(dve, b + 2 * j + 2, i)
                        dve.wait_ge(S("unit_done"), b + 2 * j + 1 + 4 * i)
                        dve.tensor_tensor(gt[:, j, 0:T], ps[:, j, 0:T], rstd[:, 0:T], ALU.mult).then_inc(S("gate_scaled"), 1)
                        split_lo(dve, b + 2 * j + 3, i)
                        dve.wait_ge(S("unit_done"), b + 2 * j + 2 + 4 * i)
                        dve.tensor_tensor(sq[:, j, 0:T], ps[:, 2 + j, 0:T], rstd[:, 0:T], ALU.mult).then_inc(S("up_scaled"), 1)
                        dve.wait_ge(S("up_scaled"), FC * c["fin"] + 2 * i + (j + 1))
                        dve.wait_ge(S("silu_done"), FC * c["ffn"] + 2 * i + (j + 1))
                        dve.wait_ge(S("ulo_ready"), hid + 2 * i + (j + 1))
                        dve.tensor_tensor(ut[:, j, 0:T], gt[:, j, 0:T], sq[:, j, 0:T], ALU.mult).then_inc(S("gated"), 1)

            def gu_dve(c):
                N, b, hid = c["N"], c["unit"], c["hid"]
                with dve.Fori(0, FC // 2) as i:
                    for j in range(2):
                        split_lo(dve, b + 2 * j + 2, i)
                        split_lo(dve, b + 2 * j + 3, i)
                        dve.wait_ge(S("silu_done"), FC * c["ffn"] + 2 * i + (j + 1))
                        dve.wait_ge(S("unit_done"), b + 2 * j + 2 + 4 * i)
                        dve.wait_ge(S("ulo_ready"), hid + 2 * i + (j + 1))
                        dve.tensor_tensor(ut[:, j, 0:N], gt[:, j, 0:N], ps[:, 2 + j, 0:N],
                                          ALU.mult).then_inc(S("gated"), 1)

            def gu_mod_dve(c):
                N, b, hid = c["N"], c["unit"], c["hid"]
                with dve.Fori(0, FC // 2) as i:
                    for j in range(2):
                        split_lo(dve, b + 4 * j + 2, i, 8)
                        split_lo(dve, b + 4 * j + 3, i, 8)
                        split_lo(dve, b + 4 * j + 4, i, 8)
                        dve.wait_ge(S("silu_done"), FC * c["ffn"] + 2 * i + (j + 1))
                        dve.wait_ge(S("unit_done"), b + 4 * j + 3 + 8 * i)
                        dve.wait_ge(S("ulo_ready"), hid + 2 * i + (j + 1))
                        dve.tensor_tensor(ut[:, j, 0:N], gt[:, j, 0:N], ps[:, 2 + j, 0:N],
                                          ALU.mult).then_inc(S("gated"), 1)
                        split_lo(dve, b + 4 * j + 5, i, 8)

            def out_dve(c):
                b, nk = c["unit"], c["nk"]
                full = (nk // 4) if b + nk + 2 <= UNITS else nk // 4 - 1
                with dve.Fori(0, full) as i:
                    for j in range(4):
                        split_lo(dve, b + 2 + j, i)
                for k in range(4 * full, nk):
                    split_lo(dve, b + 2 + k)

            def post_dve(c):
                N = c["N"]
                l, part = c["coef"]
                for t in range(DC):
                    dve.wait_ge(S("sq_ready"), DC * c["norm"] + t + 1)
                    for v, r in halves(N):
                        ins = dve.tensor_scalar(gy[:, t, r], ps[:, out_bank(t), r], CG[:, l, part, t, v:v + 1], None, ALU.mult)
                    ins.then_inc(S("gy_ready"), 1)
                recip(c, N)
                mine = DC - POOL_X
                for t in range(mine + 1):
                    if t < mine:
                        dve.wait_ge(S("gy_ready"), DC * c["post"] + t + 1)
                        dve.tensor_tensor(gy[:, t, 0:N], gy[:, t, 0:N], rstd[:, 0:N], ALU.mult).then_inc(S("yn_ready"), 1)
                    if t >= 1:
                        dve.wait_ge(S("yn_ready"), mine * c["post"] + t)
                        dve.tensor_tensor(xT[:, t - 1, 0:N], xT[:, t - 1, 0:N], gy[:, t - 1, 0:N],
                                          ALU.add).then_inc(S("x_ready"), 1)

            def add_dve(c):
                for t in range(DC):
                    wait_y(dve, c, t)
                    dve.scalar_tensor_tensor(xT[:, t, 0:T], ps[:, out_bank(t), 0:T], c["weight"], xT[:, t, 0:T],
                                             ALU.mult, ALU.add).then_inc(S("x_ready"), 1)

            def conv_dve(c):
                b, hid = c["unit"], c["hid"]
                for n in range(DC):
                    first = b + 7 * n
                    for m in range(2, 8 if n < MOD_CONV else 5):
                        split_lo(dve, first + m)
                    if n == 0:
                        dve.memset(cu[:, :, :, 0:1], 0.0)
                        dve.memset(cu[:, :, :, T + 1:T + 2], 0.0).then_inc(S("cu_zero"), 1)
                        dve.wait_ge(S("cu_zero"), 1)
                    dve.wait_ge(S("cg_ready"), n + 1)
                    dve.wait_ge(S("unit_done"), first + (5 if n < MOD_CONV else 3))
                    dve.tensor_tensor(cu[:, n % 2, :, 1:T + 1], gt[:, n % 2, :].rearrange("p (v t) -> p v t", v=2),
                                      ps[:, 3 * (n % 2) + 2, :].rearrange("p (v t) -> p v t", v=2),
                                      ALU.mult).then_inc(S("cu_ready"), 1)
                    dve.wait_ge(S("cy_ready"), n + 1)
                    dve.wait_ge(S("cu_ready"), n + 1)
                    for m, o in ((0, 0), (2, 2)):
                        w = VEC["convw"] + DC * m + n
                        dve.scalar_tensor_tensor(cy[:, n % 2, :, :], cu[:, n % 2, :, o:o + T], vec[:, w:w + 1],
                                                 cy[:, n % 2, :, :], ALU.mult, ALU.add).then_inc(S("cy_tap"), 1)
                        dve.wait_ge(S("cy_tap"), 2 * n + (1 if o == 0 else 2))
                    dve.wait_ge(S("ulo_ready"), hid + n + 1)
                    dve.tensor_tensor(ut[:, n % 2, :], cy[:, n % 2, :, :].rearrange("p v t -> p (v t)"),
                                      ps[:, 3 * (n % 2), :], ALU.mult).then_inc(S("gated"), 1)
                    if n < MOD_CONV:
                        split_lo(dve, first + 8)
                mod_finish(dve, 1)

            def attn_dve(c):
                b, hid = c["unit"], c["hid"]
                for n in range(12):
                    split_lo(dve, b + n + 2)
                dve.wait_ge(S("w_perm"), 1)
                dve.wait_ge(S("atab_loaded"), 16)
                for n in range(5):
                    dst = AK[:, :, 0:T] if n == 0 else AQ[:, 2 * n - 2:2 * n, :]
                    cs = ropeW[0 if n == 0 else 2].unsqueeze(1).broadcast_to([P, 2, T])
                    sn = ropeW[1 if n == 0 else 3].unsqueeze(1).broadcast_to([P, 2, T])
                    dve.tensor_tensor(rp1[:, n % 2], dst, cs, ALU.mult).then_inc(S("w_rp"), 1)
                    dve.tensor_tensor(rp2[:, n % 2], ps[:, n, :].rearrange("p (a t) -> p a t", a=2), sn,
                                      ALU.mult).then_inc(S("w_rp"), 1)
                    dve.wait_ge(S("w_rp"), 2 * n + 2)
                    dve.tensor_tensor(dst, rp1[:, n % 2], rp2[:, n % 2], ALU.add).then_inc(S("w_rope"), 1)

                def top(n):
                    qb = n % 2
                    sk = VEC["sink"] + 2 * (n // 4) + n // 2 % 2
                    dve.wait_ge(S("w_s"), n + 1)
                    if n >= 2:
                        dve.wait_ge(S("w_e"), 2 * (n - 1))
                    dve.tensor_tensor(sw[:, n % 2, :], ps[:, SCORE_BANK[n % 4], :], bandW[:, qb, :], ALU.add).then_inc(S("w_sb"), 1)
                    dve.wait_ge(S("w_sb"), n + 1)
                    dve.tensor_reduce(aw[:, n % 2, 0:1], sw[:, n % 2, :], AXX, ALU.max).then_inc(S("w_mx"), 1)
                    dve.wait_ge(S("w_mx"), n + 1)
                    dve.tensor_scalar(aw[:, n % 2, 1:2], aw[:, n % 2, 0:1], vec[:, sk:sk + 1], -1.0, ALU.max,
                                      ALU.mult).then_inc(S("w_nm"), 1)

                def norm(n):
                    dve.wait_ge(S("w_e"), 2 * n + 2)
                    dve.tensor_tensor(aw[:, n % 2, 4:5], aw[:, n % 2, 2:3], aw[:, n % 2, 3:4],
                                      ALU.add).then_inc(S("w_sum"), 1)
                    dve.wait_ge(S("w_sum"), n + 1)
                    dve.reciprocal(aw[:, n % 2, 5:6], aw[:, n % 2, 4:5]).then_inc(S("w_rec"), 1)
                    dve.wait_ge(S("w_rec"), n + 1)
                    if n >= 2:
                        dve.wait_ge(S("w_tr"), n - 1)
                    dve.tensor_scalar(pn[:, n % 2, :], pw[:, n % 2, :], aw[:, n % 2, 5:6], None,
                                      ALU.mult).then_inc(S("w_pn"), 1)

                def head_out(cc):
                    dve.wait_ge(S("w_pv"), 2 * cc + 2)
                    dve.wait_ge(S("ulo_ready"), hid + cc + 1)
                    dve.tensor_copy(ut[:, cc % 2, 0:T], ps[:, 4 + cc % 2, 0:T]).then_inc(S("gated"), 1)

                top(0)
                for n in range(32):
                    if n + 1 < 32:
                        top(n + 1)
                    norm(n)
                    if n % 4 == 2 and n > 4:
                        head_out(n // 4 - 1)
                head_out(7)


            def mix_dve(c):
                b, l, hid = c["unit"], c["l"], c["hid"]
                V = lambda name, i=0: vec[:, VEC[f"{name}{l}"] + i:VEC[f"{name}{l}"] + i + 1]

                def need(name, per, k):
                    dve.wait_ge(S(name), per * l + k)

                step = [S_STEP[0]]

                def then(ins):
                    ins.then_inc(S("dve_step"), 1)
                    step[0] += 1
                    dve.wait_ge(S("dve_step"), step[0])

                taps = [(k, ch) for k in range(1, KTAPS) for ch in range(2)]

                def tap():
                    k, ch = taps.pop(0)
                    n = 2 * k + ch
                    need("c_tap", 2 * KTAPS, n - 1)
                    dve.scalar_tensor_tensor(hc[:, ch, :], hp[:, ch, k:k + T], V("cw", n), hc[:, ch, :],
                                             ALU.mult, ALU.add).then_inc(S("c_tap"), 1)

                for n in range(N_IN):
                    split_lo(dve, b + n + 2)
                    dve.wait_ge(S("unit_done"), b + n + 1)
                    if n == B_Q:
                        dve.scalar_tensor_tensor(Z[:, n, :], ps[:, n % 4, 0:T], 32 ** -0.5, rstd[:, 0:T], ALU.mult,
                                                 ALU.mult).then_inc(S("m_evac"), 1)
                    else:
                        dve.tensor_tensor(Z[:, n, :], ps[:, n % 4, 0:T], rstd[:, 0:T], ALU.mult).then_inc(S("m_evac"), 1)
                    if n == 5:
                        need("c_sig", 1, 1)
                        dve.memset(hp[:, :, 0:KTAPS - 1], 0.0)
                        then(dve.tensor_tensor(hp[:, :, KTAPS - 1:], Z[:, C_A:C_A + 2, :], Z[:, C_G:C_G + 2, :], ALU.mult))
                        for ch in range(2):
                            dve.tensor_scalar(hc[:, ch, :], hp[:, ch, 0:T], V("cw", ch), V("cb", ch), ALU.mult,
                                              ALU.add).then_inc(S("c_tap"), 1)
                    if n > 5:
                        for _ in range(3):
                            tap()
                while len(taps) > 1:
                    tap()
                tap()
                need("c_tap", 2 * KTAPS, 2 * KTAPS)
                need("m_rt", 2, 1)
                then(dve.reciprocal(rm[:, 0:6 * T], rm[:, 0:6 * T]))
                for n in range(3):
                    r = rm[:, T:2 * T] if n == 2 else rm[:, 0:T]
                    g = V("dkva") if n == 2 else V("dqa", n)
                    ins = dve.scalar_tensor_tensor(cnf[:, n, :], Z[:, D_Q + n, :], g, r, ALU.mult, ALU.mult)
                then(ins)
                then(dve.tensor_copy(cn_hi[:, :, :], cnf[:, :, :]))
                dve.tensor_tensor(cn_lo[:, :, :], cnf[:, :, :], cn_hi[:, :, :], ALU.subtract).then_inc(S("d_cn"), 1)
                for n in range(2):
                    ins = dve.scalar_tensor_tensor(Z[:, A_Q + 2 * n:A_Q + 2 * n + 2, :], Z[:, A_Q + 2 * n:A_Q + 2 * n + 2, :],
                                                   V("ak") if n else V("aq"),
                                                   rm[:, (2 + 2 * n) * T:(4 + 2 * n) * T].rearrange("p (a t) -> p a t", a=2),
                                                   ALU.mult, ALU.mult)
                then(ins)

                def hand_over(k, src, name, wait_first=None):
                    dve.wait_ge(S("ulo_ready"), hid + k + 1)
                    return src

                need("m_rt", 2, 2)
                then(dve.reciprocal(rm[:, 6 * T:7 * T], rm[:, 6 * T:7 * T]))
                for ch in range(2):
                    ins = dve.scalar_tensor_tensor(hc[:, ch, :], hc[:, ch, :], V("cn", ch), rm[:, 6 * T:7 * T], ALU.mult,
                                                   ALU.mult)
                ins.then_inc(S("c_n"), 1)
                need("c_silu", 1, 1)
                for ch in range(2):
                    dve.wait_ge(S("ulo_ready"), hid + ch + 1)
                    dve.tensor_copy(ut[:, ch, 0:T], hc[:, ch, :]).then_inc(S("gated"), 1)
                dve.wait_ge(S("gated"), hid + 2)
                then(dve.memset(AT[:, :, :], 0.0))

                need("b_gate", 1, 1)
                dve.tensor_scalar(G1, ps[:, 4, 0:T], V("bg"), None, ALU.add).then_inc(S("b_g"), 1)
                need("b_g", 1, 1)
                need("b_a", 3, 3)
                then(dve.tensor_scalar(G1, G1, 0.0, None, ALU.min))
                then(dve.tensor_tensor(G1, G1, G2, ALU.subtract))
                dve.wait_ge(S("mtab_loaded"), 16 * (l + 1))
                bb = EB[:, LEVELS, :]
                then(dve.tensor_tensor_scan(bb, scanm, G1, 0.0, ALU.mult, ALU.add))
                for v in range(LEVELS):
                    s = 32 >> v
                    w = bb.rearrange("p (n a s) -> p n a s", a=2, s=s)
                    e = EB[:, v, :].rearrange("p (n a s) -> p n a s", a=2, s=s)
                    mid = w[:, :, 0, s - 1:s].broadcast_to([P, T // (2 * s), s])
                    dve.tensor_tensor(e[:, :, 0, :], mid, w[:, :, 0, :], ALU.subtract)
                    dve.tensor_tensor(e[:, :, 1, :], w[:, :, 1, :], mid, ALU.subtract)
                w = bb.rearrange("p (n s) -> p n s", s=64)
                dve.tensor_tensor(EB[:, LEVELS + 1, :].rearrange("p (n s) -> p n s", s=64),
                                  w[:, :, 63:64].broadcast_to([P, 4, 64]), w, ALU.subtract).then_inc(S("b_e"), 1)
                need("b_p", 1, 1)
                q6 = Z[:, B_Q:B_Q + 1, :].broadcast_to([P, LEVELS + 1, T])
                k6 = Z[:, B_K:B_K + 1, :].broadcast_to([P, LEVELS, T])
                dve.tensor_tensor(QP[:, :, :], q6, EB[:, 0:LEVELS + 1, :], ALU.mult)
                dve.tensor_tensor(KP[:, 0:LEVELS, :], k6, EB[:, 0:LEVELS, :], ALU.mult)
                dve.tensor_tensor(KP[:, LEVELS, :], Z[:, B_K, :], EB[:, LEVELS + 1, :], ALU.mult).then_inc(S("b_qk"), 1)
                need("b_st", 1, 1)
                for k in range(3):
                    src = ps[:, 7, 0:2 * P] if k == 0 else ps[:, 4, 0:2 * P] if k == 1 else ps[:, 5, 0:2 * P]
                    ins = dve.tensor_tensor(ST[:, k, :], src, bmask, ALU.mult)
                then(ins)
                for k in (1, 2):
                    e = EB[:, LEVELS, 64 * k + 63:64 * k + 64]
                    dve.scalar_tensor_tensor(ST[:, k, :], ST[:, k - 1, :], e, ST[:, k, :], ALU.mult,
                                             ALU.add).then_inc(S("b_s"), 1)
                    need("b_s", 2, k)
                for v in range(LEVELS + 1):
                    need("b_lv", LEVELS + 1, v + 1)
                    if v:
                        need("b_at", LEVELS + 1, v)
                    mask = levm[:, v:v + 1, :].bitcast(U32).broadcast_to([P, 4, T])
                    dve.copy_predicated(AT[:, :, :], mask, ps[:, 0:4, 0:T]).then_inc(S("b_at"), 1)
                need("b_oc", 1, 1)
                dve.tensor_tensor(OB[:, :, 64:T], OB[:, :, 64:T], ps[:, 5, :].rearrange("p (a t) -> p a t", a=2)[:, :, 64:T],
                                  ALU.add).then_inc(S("b_oi"), 1)
                need("b_rt", 1, 1)
                need("b_oi", 1, 1)
                then(dve.reciprocal(rm[:, 0:2 * T], rm[:, 0:2 * T]))
                then(dve.scalar_tensor_tensor(OB[:, :, :], OB[:, :, :], V("bo"),
                                              rm[:, 0:2 * T].rearrange("p (a t) -> p a t", a=2), ALU.mult, ALU.mult))
                need("b_silu", 1, 1)
                for ch in range(2):
                    dve.wait_ge(S("ulo_ready"), hid + 2 + ch + 1)
                    dve.tensor_tensor(ut[:, ch, 0:T], OB[:, ch, :], Z[:, B_R + ch, :], ALU.mult).then_inc(S("gated"), 1)
                dve.wait_ge(S("gated"), hid + 4)

                split_lo(dve, b + N_IN + 2)
                split_lo(dve, b + N_IN + 3)
                need("d_rt", 1, 1)
                then(dve.reciprocal(rm[0:96, :], rm[0:96, :]))
                for n, x in enumerate((DQ, DK)):
                    dve.scalar_tensor_tensor(x[0:96, :, :].rearrange("p a t -> p (a t)"),
                                             x[0:96, :, :].rearrange("p a t -> p (a t)"),
                                             (V("dk") if n else V("dq"))[0:96, :], rm[0:96, 4 * T * n:4 * T * (n + 1)],
                                             ALU.mult, ALU.mult).then_inc(S("d_n"), 1)
                need("d_n", 2, 2)
                need("d_perm", 1, 1)
                for n, x in enumerate((DQ, DK)):
                    then(dve.tensor_tensor(dt1[0:96, :, :], ps[0:96, 2 * n:2 * n + 2, :].rearrange("p a (b t) -> p (a b) t", b=2),
                                           SD[0:96, :].unsqueeze(1).broadcast_to([96, 4, T]), ALU.mult))
                    then(dve.tensor_tensor(x[0:96, :, :], x[0:96, :, :], CD[0:96, :].unsqueeze(1).broadcast_to([96, 4, T]),
                                           ALU.mult))
                    dve.tensor_tensor(x[0:96, :, :], x[0:96, :, :], dt1[0:96, :, :], ALU.add).then_inc(S("d_r"), 1)
                    need("d_r", 2, n + 1)

                def attend(q0, qb, scale, bias):
                    kc, n = P * (qb + 1), 4 * l + q0 + qb + 1
                    dve.wait_ge(S("s_s"), n)
                    src = ps[:, 0:2, :].rearrange("p a (b t) -> p (a b) t", b=2)[:, :, 0:kc]
                    if bias is None:
                        cz = (caus0[:, P * (1 - qb):P * (1 - qb) + kc] if qb == 0 else caus0[:, 0:kc])
                        then(dve.scalar_tensor_tensor(LG[:, :, 0:kc], src, scale, cz.unsqueeze(1).broadcast_to([P, 4, kc]),
                                                      ALU.mult, ALU.add))
                    else:
                        k0 = P if qb == 0 else 0
                        then(dve.scalar_tensor_tensor(LG[:, :, 0:kc], src, scale, biasA[:, :, k0:k0 + kc], ALU.mult, ALU.add))
                        then(dve.tensor_tensor(LG[:, :, 0:kc], LG[:, :, 0:kc], bias[:, 0:kc].unsqueeze(1).broadcast_to([P, 4, kc]),
                                               ALU.add))
                    then(dve.tensor_reduce(am[:, 0:4], LG[:, :, 0:kc], AXX, ALU.max))
                    dve.tensor_scalar(am[:, 4:8], am[:, 0:4], -1.0, None, ALU.mult).then_inc(S("s_nm"), 1)
                    dve.wait_ge(S("s_e"), n)
                    then(dve.reciprocal(am[:, 12:16], am[:, 8:12]))
                    for h in range(4):
                        ins = dve.tensor_scalar(PR[:, h, 0:kc], PR[:, h, 0:kc], am[:, 12 + h:13 + h], None, ALU.mult)
                    ins.then_inc(S("s_p"), 1)
                    dve.wait_ge(S("s_p"), n)

                def values_out(q0, k0):
                    dve.wait_ge(S("s_pv"), 4 * l + q0 + 2)
                    for ch in range(2):
                        dve.wait_ge(S("ulo_ready"), hid + k0 + ch + 1)
                        dve.tensor_copy(ut[:, ch, 0:T], ps[:, 6, T * ch:T * (ch + 1)]).then_inc(S("gated"), 1)
                    dve.wait_ge(S("gated"), hid + k0 + 2)

                for qb in range(TT):
                    attend(0, qb, 96 ** -0.5, None)
                values_out(0, 4)
                then(dve.tensor_copy(QA[:, :, :], Z[:, A_Q:A_Q + 4, :]))
                need("i_w", 1, 1)
                sel = []
                for qb in range(TT):
                    kc = P * (qb + 1)
                    acc = SCI[:, 0:kc]
                    for h in range(8):
                        n = 8 * qb + h
                        need("i_r", 16, n + 1)
                        wcol = iw[:, qb, h:h + 1]
                        if h == 0:
                            dve.tensor_scalar(acc, RI[:, n % 2, 0:kc], wcol, None, ALU.mult).then_inc(S("i_a"), 1)
                        else:
                            dve.scalar_tensor_tensor(acc, RI[:, n % 2, 0:kc], wcol, acc, ALU.mult, ALU.add).then_inc(S("i_a"), 1)
                        need("i_a", 16, n + 1)
                    k0 = P if qb == 0 else 0
                    then(dve.tensor_tensor(acc, acc, caus1[:, k0:k0 + kc], ALU.mult))
                    then(dve.tensor_tensor(WK[:, 0, 0:kc], acc, caus0[:, k0:k0 + kc], ALU.add))
                    cur = 0
                    for it in range(8):
                        then(dve.max(m8[:, it % 2, :], WK[:, cur, 0:kc]))
                        then(dve.match_replace(WK[:, 1 - cur, 0:kc], m8[:, it % 2, :], WK[:, cur, 0:kc], -3.3e38))
                        cur = 1 - cur
                    bias = sqm[:, qb, :]
                    then(dve.tensor_scalar(SEL[:, 0:kc], WK[:, cur, 0:kc], -3.3e38, None, ALU.is_equal))
                    then(dve.tensor_tensor(SEL[:, 0:kc], SEL[:, 0:kc], caus1[:, k0:k0 + kc], ALU.mult))
                    then(dve.tensor_scalar(bias[:, 0:kc], SEL[:, 0:kc], 1.0, -NEG, ALU.subtract, ALU.mult))
                for qb in range(TT):
                    attend(2, qb, 0.125, sqm[:, qb, :])
                values_out(2, 6)
                S_STEP[0] = step[0]

            dve.memset(epsc[:, :], EPS)
            dve.memset(zc[:, :], 0.0).then_inc(S("init"), 1)
            dve.wait_ge(S("small_loaded"), 96)
            dve.tensor_copy(rbb[:, :, :], rl[:, :].unsqueeze(2).broadcast_to([32, 4, P])).then_inc(S("rbb_ready"), 1)
            dve.wait_ge(S("cs_ready"), 1)
            dve.tensor_tensor(cs[:, :, 2:4], cv[:, :, :], cs[:, :, 0:2], ALU.subtract).then_inc(S("cs_ready"), 1)
            split_lo(dve, 0)
            split_lo(dve, 1)
            for kind, c in PLAN:
                if kind == "mod":
                    with dve.Fori(0, MB) as i:
                        for q in range(4):
                            split_lo(dve, c["unit"] + q + 2, i)
                    mod_finish(dve, 0)
                elif kind == "gu_mod":
                    gu_mod_dve(c)
                elif kind == "pre":
                    pre_dve(c)
                elif kind == "pre2":
                    pre2_dve(c)
                elif kind == "gu":
                    (gu_late_dve if c["late"] else gu_dve)(c)
                elif kind == "out":
                    out_dve(c)
                elif kind == "post":
                    post_dve(c)
                elif kind == "add":
                    add_dve(c)
                elif kind == "conv":
                    conv_dve(c)
                elif kind == "attn":
                    attn_dve(c)
                elif kind == "mix":
                    mix_dve(c)

        @block.gpsimd
        def _(pool):
            pool.memset(stepper[:, 2:3], 0.0).then_inc(S("mod_evac"), 1)
            pool.memset(stepper[:, 3:4], 0.0).then_inc(S("mod_stored"), 1)
            pool.memset(stepper[:, 0:1], 0.0).then_inc(S("ulo_ready"), 1)
            pool.memset(stepper[:, 1:2], 0.0).then_inc(S("ulo_ready"), 1)

            def pre_pool(c):
                N, h = c["N"], c["h"]
                for t in range(DC):
                    pool.wait_ge(S("hf_ready"), h + t + 1)
                    pool.tensor_scalar(h_hi[:, t, 0:N], hf[:, t, 0:N], 1.0, None, ALU.mult).then_inc(S("h_hi_ready"), 1)

            def post_pool(c):
                N = c["N"]
                pool.wait_ge(S("rstd_ready"), c["norm"] + 1)
                for n in range(POOL_X):
                    t = DC - POOL_X + n
                    pool.wait_ge(S("gy_ready"), DC * c["post"] + t + 1)
                    pool.tensor_tensor(gy[:, t, 0:N], gy[:, t, 0:N], rstd[:, 0:N], ALU.mult).then_inc(S("yp_ready"), 1)
                    pool.wait_ge(S("yp_ready"), POOL_X * c["post"] + n + 1)
                    pool.tensor_tensor(xT[:, t, 0:N], xT[:, t, 0:N], gy[:, t, 0:N], ALU.add).then_inc(S("xp_ready"), 1)

            def split_hidden(c, k, par, N, hi, lo):
                pool.wait_ge(S("gated"), c["hid"] + k + 1)
                pool.tensor_copy(hi[:, k, 0:N], ut[:, par, 0:N]).then_inc(S("uhi_ready"), 1)
                pool.wait_ge(S("uhi_ready"), c["hid"] + k + 1)
                pool.tensor_tensor(lo[:, k, 0:N], ut[:, par, 0:N], hi[:, k, 0:N],
                                   ALU.subtract).then_inc(S("ulo_ready"), 1)

            for kind, c in PLAN:
                if kind == "pre":
                    pre_pool(c)
                elif kind == "post":
                    post_pool(c)
                elif kind in ("gu", "gu_mod"):
                    with pool.Fori(0, FC // 2) as i:
                        for j in range(2):
                            split_hidden(c, 2 * i + j, j, c["N"], u_hi, u_lo)
                elif kind == "conv":
                    for k in range(DC):
                        split_hidden(c, k, k % 2, c["N"], u_hi, u_lo)
                elif kind == "attn":
                    for k in range(DC):
                        split_hidden(c, k, k % 2, T, h_hi, h_lo)
                elif kind == "mix":
                    for k in range(DC):
                        split_hidden(c, k, k % 2, T, h_hi, h_lo)


def cols(v):
    v = np.asarray(v)
    return np.ascontiguousarray(v.reshape(-1, P).T)


def in_units(w, heads=None):
    k, n = w.shape
    return w.reshape(k // P, P, n // P, P).transpose(2, 1, 0, 3).reshape(n // P, P, k)


def out_units(w):
    return w.reshape(-1, P, D)


def head_of(chunk, half):
    return (2 * (chunk // 4) + half) * 4 + chunk % 4


def weight_stream(a):
    units = []
    HD = 64

    def ffn(gu, down):
        g, u = in_units(gu[:, :DFF]), in_units(gu[:, DFF:])
        units.extend([np.stack([g, u], 1).reshape(2 * FC, P, D), out_units(down)])

    def ffn3(gate, up, down):
        units.extend([np.stack([in_units(gate), in_units(up)], 1).reshape(2 * FC, P, D), out_units(down)])

    def mod_blocks(l):
        return a["w_mod"][l].reshape(4, 2, P, MB, 512).transpose(3, 0, 2, 1, 4).reshape(MB, 4, P, D)

    mod1 = mod_blocks(1)
    units.append(mod_blocks(0).reshape(-1, P, D))
    for l in range(2):
        if l == 0:
            w = a["ffn_w_gu"][0, 0]
            gu = np.stack([in_units(w[:, :DFF]), in_units(w[:, DFF:])], 1).reshape(FC // 2, 4, P, D)
            units.extend([np.stack([gu, mod1[:FC // 2]], 2).reshape(-1, P, D), out_units(a["ffn_w_down"][0, 0])])
            w = in_units(a["conv_w_in"][0]).reshape(3, DC, P, D).transpose(1, 0, 2, 3)
            for n in range(DC):
                if n < MOD_CONV:
                    m = mod1[FC // 2 + n]
                    units.append(np.stack([w[n][0], m[0], w[n][1], m[1], w[n][2], m[2], m[3]]))
                else:
                    units.append(w[n])
            units.append(out_units(a["conv_w_out"][0]))
        else:
            ffn(a["ffn_w_gu"][l, 0], a["ffn_w_down"][l, 0])
            w = a["attn_w_qkv"][0]
            order = [head_of(c, h) for c in range(8) for h in range(2)]
            q = w[:, :1024].reshape(D, 16, HD)[:, order].reshape(D, 1024)
            wo = a["attn_w_o"][0].reshape(16, HD, D)[order].reshape(1024, D)
            units.extend([in_units(w[:, 1024:]), in_units(q), out_units(wo)])
        ffn(a["ffn_w_gu"][l, 1], a["ffn_w_down"][l, 1])
    for l in range(2):
        ffn3(a["ffn1_gate_2"][l], a["ffn1_up_2"][l], a["ffn1_down_2"][l])
        w = a["w_in_2"][l]
        z = np.zeros((D, P), w.dtype)

        def put(at, first, width, n=1):
            m = z.copy()
            for j in range(n):
                m[:, at + j * width:at + (j + 1) * width] = w[:, first:first + width]
            return m

        parts = [w[:, 1848:2360], w[:, 1064:1576], put(0, 1576, 16), w[:, 1592:1848], w[:, 2360:2744],
                 put(64, 2744, 32), w[:, 0:1024], put(0, 1024, 32, 4), put(0, 1056, 8)]
        units.append(in_units(np.concatenate(parts, 1)))
        uq = np.zeros((2, P, 4, P), w.dtype)
        uq[..., :96] = a["d_uq_2"][l].reshape(2, P, 4, 96)
        units.append(uq.transpose(1, 0, 2, 3).reshape(1, P, D))
        ukv = np.zeros((P, D), w.dtype)
        ukv[:, :512] = a["d_ukv_2"][l]
        units.append(ukv[None])
        units.append(out_units(a["w_out_2"][l].reshape(4, 256, D)[ORDER].reshape(1024, D)))
        ffn3(a["ffn2_gate_2"][l], a["ffn2_up_2"][l], a["ffn2_down_2"][l])
    return np.concatenate(units, 0)


ORDER = [2, 1, 3, 0]


def vectors(a):
    v = np.zeros((P, NVEC), np.float32)

    def put(name, m):
        v[:, VEC[name]:VEC[name] + m.shape[1]] = m

    put("g1", cols(a["norm_g"]))
    put("g2", cols(np.stack([a["ffn1_norm_2"], a["mix_norm_2"], a["ffn2_norm_2"]], 1)))
    put("convw", cols(a["conv_w"][0]))
    put("bmod", cols(a["b_mod"]))
    put("sink", np.broadcast_to(a["attn_sink"][0][[head_of(c, h) for c in range(8) for h in range(2)]], (P, 16)))
    for l in range(2):
        put(f"aq{l}", np.tile(a["a_q_norm_2"][l], 2)[:, None])
        put(f"ak{l}", np.tile(a["a_k_norm_2"][l], 2)[:, None])
        put(f"bg{l}", a["b_gate_bias_2"][l][:, None])
        put(f"bo{l}", np.tile(a["b_out_norm_2"][l], 2)[:, None])
        put(f"cw{l}", cols(a["c_dw_w_2"][l][:, 0]))
        put(f"cb{l}", cols(a["c_dw_b_2"][l]))
        put(f"cn{l}", cols(a["c_norm_2"][l]))
        put(f"dqa{l}", cols(a["d_qa_norm_2"][l]))
        put(f"dkva{l}", cols(a["d_kva_norm_2"][l]))
        for n in "qk":
            v[:96, VEC[f"d{n}{l}"]] = a[f"d_{n}_norm_2"][l]
    return v


def rotation(first, n, half):
    r = np.zeros((P, P), np.float32)
    for g in range(n):
        for i in range(half):
            p = first + 2 * half * g + i
            r[p + half, p] = -1.0
            r[p, p + half] = 1.0
    return r


def tables():
    f = np.float32
    one = np.ones((P, P), f)
    p = np.arange(P)
    b64 = (p[:, None] // 64 == p[None] // 64).astype(f)
    o96 = np.zeros((P, P), f)
    o96[:96] = 1.0
    k = np.arange(T)
    caus = ((p[:, None] + P) >= k[None]).astype(f)
    bmask = (p[:, None] // 32 == k[None] // 64).astype(f)
    ctabs = np.concatenate([one, np.eye(P, dtype=f), b64, o96, rotation(0, 4, 16), rotation(64, 1, 16),
                            caus, ((caus - 1) * f(3e38)).astype(f), bmask], 1)
    band = np.zeros((P, 2, 2 * T), f)
    for b in range(2):
        band[:, b, :T] = np.where(np.abs(P * b + p[:, None] - k[None]) <= 128, f(0), f(NEG))
    tok = np.arange(T)
    inv = (f(10000.0) ** (-np.arange(16, dtype=f) / f(16))).astype(f)
    ang = np.stack([(tok // 64).astype(f)[:, None] * inv, (tok % 64).astype(f)[:, None] * inv], 0)
    ang = ang[(p // 32) % 2, :, p % 16]
    C, Sn = np.cos(ang).astype(f), np.sin(ang).astype(f)
    att = np.concatenate([band.reshape(P, -1), C, Sn, C * f(0.125), Sn * f(0.125)], 1)
    ang = tok.astype(f)[None] * inv[p % 16][:, None]
    on = ((p >= 64) & (p < 96))[:, None]
    CD, SD = np.where(on, np.cos(ang), 1).astype(f), np.where(on, np.sin(ang), 0).astype(f)
    lev = []
    j, i = p[:, None], (k % P)[None]
    for s in (32, 16, 8, 4, 2, 1):
        lev.append((j // (2 * s) == i // (2 * s)) & (j // s % 2 == 0) & (i // s % 2 == 1))
    lev.append(j == i)
    lev = np.stack(lev, 1).astype(f).reshape(P, -1)
    scan = np.broadcast_to((k % 64 != 0).astype(f), (P, T))
    mix = np.concatenate([CD, SD, scan, lev], 1)
    dist = np.maximum(255 - np.arange(384), 0)
    large = 16 + (np.log(np.maximum(dist, 1).astype(f) / f(16)) / f(np.log(8.0)) * f(16)).astype(np.int32)
    buck = np.where(dist < 16, dist, np.minimum(large, 31))
    onehot = (np.arange(32)[:, None] == buck[None]).astype(f)
    return [np.ascontiguousarray(m.astype(f)) for m in (ctabs, att, mix, onehot)]


def chunked(x):
    return x.T.reshape(DC, P, -1).transpose(1, 0, 2)


def host(a):
    a = {k: np.asarray(v) for k, v in a.items()}
    ctabs, att, mix, onehot = tables()
    return dict(
        xin=np.ascontiguousarray(np.concatenate([chunked(a["x"][0]), chunked(a["ctx"][0])], 2)),
        wst=weight_stream(a),
        cvec=np.ascontiguousarray(np.stack([cols(a["c"]), cols(a["c_ctx"])], 2)),
        vecs=vectors(a), ctabs=ctabs, attabs=att, mixtabs=mix,
        bup=np.ascontiguousarray(a["b_gate_up_2"].transpose(1, 0, 2)), relb=a["rel_bias_2"], onehot=onehot)


def kernel(**inputs):
    from concourse import bacc
    from concourse.bass_utils import run_bass_kernel_spmd

    arrays = host(inputs)
    nc = bacc.Bacc("TRN2", target_bir_lowering=False, num_devices=1)
    args = [nc.dram_tensor(n, v.shape, mybir.dt.from_np(v.dtype), kind="ExternalInput").ap() for n, v in arrays.items()]
    out = nc.dram_tensor("out", (P, DC, T), F32, kind="ExternalOutput").ap()
    build(nc, *args, out)
    r = run_bass_kernel_spmd(nc, [arrays], core_ids=[0]).results[0]["out"]
    return np.ascontiguousarray(r.transpose(1, 0, 2).reshape(D, T).T)[None]
```

```python
from contextlib import ExitStack

import numpy as np
import concourse.bass as bass
from concourse import mybir

F32 = mybir.dt.float32
F32R = mybir.dt.float32r
U32 = mybir.dt.uint32
ACT = mybir.ActivationFunctionType
ALU = mybir.AluOpType
AXX = mybir.AxisListType.X

P = 128
D = 1024
DC = D // P
T = 256
TT = T // P
DFF = 2816
FC = DFF // P
RING = 4
EPS = 1e-6
HI = ("act", "pool", "dve", "act", "pool", "act", "pool", "dve")
LAG = 4
NMOD = 9
NEG = -1.0e30


def out_bank(d):
    return (d + 4) % 8

C_A, C_G = 0, 2
B_Q, B_K, B_V, B_G, B_R = 4, 5, 6, 8, 9
D_Q, D_KV, D_PE = 11, 13, 14
A_Q, A_K, A_V, I_Q, I_K, I_W = 15, 17, 19, 21, 23, 24
N_IN = 25
KTAPS = 31
PER_CHUNK = 3
SCORE_BANK = (0, 1, 6, 7)
LEVELS = 6

POOL_X = 2
X_ORDER = [0, 1, 6, 2, 3, 7, 4, 5]
MB = NMOD * D // 512
MOD_LOOP = FC // 2
MOD_FIRST = MB - MOD_LOOP
MOD_PARTS = [(4 * a, 4 * b, subs) for a, b, subs in [
    (0, MOD_FIRST, [(0, 0)]), (MOD_FIRST, MB, [(0, 1), (0, 2)]),
    (MB, MB + MOD_FIRST, [(1, 0)]), (MB + MOD_FIRST, 2 * MB, [(1, 1), (1, 2)])]]

def make_plan():
    plan = []
    c = dict(unit=0, mod=0, norm=0, pre=0, pre2=0, x=0, xp=0, out=0, post=0, ffn=0, fin=0, hid=0, h=0)

    def add(kind, **k):
        plan.append((kind, dict(c) | k))

    def pre(N, coef):
        add("pre", N=N, coef=coef)
        c["pre"] += 1
        c["norm"] += 1
        c["h"] += DC

    def gu(N, late=False):
        add("gu", N=N, late=late)
        c["unit"] += 2 * FC
        c["ffn"] += 1
        c["fin"] += late
        c["hid"] += FC

    def out(N, nk):
        add("out", N=N, nk=nk)
        c["unit"] += nk
        c["out"] += 1

    def post(N, coef):
        add("post", N=N, coef=coef)
        c["norm"] += 1
        c["post"] += 1
        c["x"] += DC - POOL_X
        c["xp"] += POOL_X

    add("mod")
    c["unit"] += 4 * MOD_FIRST
    c["mod"] += MOD_FIRST
    for l in range(2):
        for part in range(3):
            N = T if (l, part) == (1, 2) else 2 * T
            pre(2 * T if (l, part) == (1, 1) else N, (l, part))
            if l == 0 and part != 1:
                add("gu_mod", N=N)
                c["mod"] += MOD_LOOP
                c["unit"] += 4 * FC
                c["ffn"] += 1
                c["hid"] += FC
                out(N, FC)
            elif part != 1:
                gu(N)
                out(N, FC)
            elif l == 0:
                add("conv", N=N)
                c["mod"] += MOD_FIRST
                c["unit"] += 3 * DC + 4 * MOD_FIRST
                c["hid"] += DC
                out(N, DC)
            else:
                add("attn", N=N)
                c["unit"] += 12
                c["hid"] += DC
                out(T, DC)
                N = T
            post(N, (l, part))
    for l in range(2):
        for part in range(3):
            if (l, part) == (0, 0):
                add("pre2", coef=(2, 0), update=None)
                c["pre2"] += 1
                c["norm"] += 1
                c["h"] += DC
            if part != 1:
                gu(T, late=True)
                out(T, FC)
            else:
                add("mix", l=l)
                c["unit"] += N_IN + 2
                c["hid"] += DC
                out(T, DC)
            weight = 1.0 if part == 1 else 0.5
            if (l, part) == (1, 2):
                add("add", weight=weight)
                c["x"] += DC
            else:
                add("pre2", coef=(2 + l + (part == 2), (part + 1) % 3), update=weight)
                c["x"] += DC
                c["norm"] += 1
                c["pre2"] += 1
                c["h"] += DC
    return plan, c["unit"], c["x"]


PLAN, UNITS, NX = make_plan()

VEC = {}


def vec_columns():
    at = 0
    for name, n in [("g1", 12 * DC), ("g2", 6 * DC), ("convw", 3 * DC), ("bmod", 2 * NMOD * DC), ("sink", 16)] + [
            (f"{name}{l}", n) for l in range(2) for name, n in
            [("aq", 1), ("ak", 1), ("bg", 1), ("bo", 1), ("cw", 62), ("cb", 2), ("cn", 2), ("dqa", 2), ("dkva", 1),
             ("dq", 1), ("dk", 1)]]:
        VEC[name] = at
        at += n
    return at


NVEC = vec_columns()


def build(nc, xin, wst, cvec, vecs, ctabs, attabs, mixtabs, bup, relb, onehot, out):
    es = ExitStack()
    with es:
        def sb(name, shape, dt=F32, ctx=es):
            return ctx.enter_context(nc.sbuf_tensor(name, shape, dt))

        sems = {}

        def S(name):
            if name not in sems:
                sems[name] = es.enter_context(nc.semaphore(name))
            return sems[name]

        xT = sb("xT", [P, DC, 2 * T])
        with ExitStack() as c1:
            z_hi = sb("z_hi", [P, DC, 2 * T], F32, c1)
            z_lo = sb("z_lo", [P, DC, 2 * T], F32, c1)
        h_hi = sb("h_hi", [P, DC, 2 * T], F32R)
        h_lo = sb("h_lo", [P, DC, 2 * T], F32R)
        w_hi = sb("w_hi", [P, RING, D], F32R)
        gt = sb("gt", [P, 2, 2 * T])
        ut = sb("ut", [P, 2, 2 * T])
        sq = sb("sq", [P, 2, 2 * T])
        modb = sb("modb", [4, 512])
        rt = sb("rt", [P, 2 * T])
        rstd = sb("rstd", [P, 2 * T])
        tabs = sb("tabs", [P, 6 * P + 3 * T + 7 * 32])
        vec = sb("vec", [P, vecs.shape[1]])
        cv = sb("cv", [P, DC, 2])
        cs = sb("cs", [P, DC, 4], F32R)
        MOD = sb("MOD", [P, 2, NMOD * DC, 2])
        CA = sb("CA", [P, 2, 3, DC, 2])
        CG = sb("CG", [P, 2, 3, DC, 2])
        epsc = sb("epsc", [P, 1])
        zc = sb("zc", [P, 1])
        spare = sb("spare", [P, 1])
        stepper = sb("stepper", [P, 4])

        ones, ident, bones64, ones96, permW, permD = (tabs[:, P * i:P * (i + 1)] for i in range(6))
        caus1, caus0, bmask = (tabs[:, 6 * P + T * i:6 * P + T * (i + 1)] for i in range(3))

        with ExitStack() as c1:
            raw = sb("raw", [P, RING, D], F32, c1)
        w_lo = sb("w_lo", [P, RING, D], F32R)

        esel = tabs[:, 6 * P + 3 * T:]
        xz = lambda k: xT[:, k, T:2 * T]
        RI = lambda n: xz(n % 2)
        SCI = lambda qb: xz(2 + qb)
        WK = lambda k: xz(4 + k)
        SEL = xz(0)
        BI = lambda qb: xz(6 + qb)
        hp = gt[:, :, 0:KTAPS - 1 + T]
        hc = sq[:, :, T:2 * T]
        tap = lambda n: xz(4 + n % 4)
        m8 = sb("m8", [P, 2, 8])
        iw = sb("iw", [P, TT, 8])
        biasA = sb("biasA", [P, 4, T])
        bupt = sb("bupt", [16, 2, P])

        with ExitStack() as c1:
            u_hi = sb("u_hi", [P, FC, 2 * T], F32R, c1)
            u_lo = sb("u_lo", [P, FC, 2 * T], F32R, c1)
        with ExitStack() as c1:
            sb("norm_pad", [P, DC, 2 * T], F32, c1)
            gy = sb("gy", [P, DC, 2 * T], F32, c1)
            tn = sb("tn", [P, DC, 2 * T], F32, c1)
            hf = sb("hf", [P, DC, 2 * T], F32, c1)
        with ExitStack() as c1:
            sqb = sb("sqb", [P, 4, 384], F32, c1)
            rbb = sb("rbb", [32, 4, P], F32, c1)
            oh = sb("oh", [32, 384], F32, c1)
            rl = sb("rl", [32, 4], F32, c1)
        with ExitStack() as c1:
            sb("conv_pad", [P, DC, 2 * T], F32, c1)
            cu = sb("cu", [P, 2, 2, T + 2], F32, c1)
            cy = sb("cy", [P, 2, 2, T], F32, c1)
        with ExitStack() as c1:
            AK = sb("AK", [P, 2, 2 * T], F32, c1)
            AV = sb("AV", [P, 2, 2 * T], F32, c1)
            AQ = sb("AQ", [P, DC, T], F32, c1)
            VV = sb("VV", [P, 4, 2 * P], F32, c1)
            atab = sb("atab", [P, attabs.shape[1]], F32, c1)
            rp1 = sb("rp1", [P, 2, 2, T], F32, c1)
            rp2 = sb("rp2", [P, 2, 2, T], F32, c1)
            sw = sb("sw", [P, 2, 2 * T], F32, c1)
            pw = sb("pw", [P, 2, 2 * T], F32, c1)
            pn = sb("pn", [P, 2, 2 * T], F32, c1)
            PTw = sb("PTw", [P, 2, 4, T], F32, c1)
            aw = sb("aw", [P, 2, 8], F32, c1)
        with ExitStack() as c1:
            Z = sb("Z", [P, N_IN, T], F32, c1)
            mtab = sb("mtab", [P, mixtabs.shape[1]], F32, c1)
            sqm = sb("sqm", [P, 8, T], F32, c1)
            rm = sb("rm", [P, 8 * T], F32, c1)
            cnf = sb("cnf", [P, 3, T], F32, c1)
            cn_hi = sb("cn_hi", [P, 3, T], F32R, c1)
            cn_lo = sb("cn_lo", [P, 3, T], F32R, c1)
            with ExitStack() as c2:
                OB = sb("OB", [P, 2, T], F32, c2)
                G1, G2 = OB[:, 0, :], OB[:, 1, :]
                EB = sb("EB", [P, LEVELS + 2, T], F32, c2)
                QP = sb("QP", [P, LEVELS + 1, T], F32, c2)
                KP = sb("KP", [P, LEVELS + 1, T], F32, c2)
                AT = sb("AT", [P, 4, T], F32, c2)
                kdT = sb("kdT", [P, TT, P], F32, c2)
                VB = sb("VB", [P, TT, 2 * P], F32, c2)
                ST = Z[:, C_A:C_A + 3, :]
            with ExitStack() as c2:
                DQ, DK, DV, dt1 = z_hi[:, 0:4, T:], z_hi[:, 4:8, T:], z_lo[:, 0:4, T:], z_lo[:, 4:8, T:]
                sb("past_OB", [P, 2, T], F32, c2)
                VA = sb("VA", [P, TT, 2, P], F32, c2)
                VT = sb("VT", [P, TT, 4, P], F32, c2)
                LG = lambda k: sqm[:, 0:4, :] if k % 2 else dt1
                PR = lambda k: sqm[:, 4:8, :] if k % 2 else DV
                PTm = sb("PTm", [P, TT, 4, T], F32, c2)
                am = sb("am", [P, 2, 16], F32, c2)
        CD, SD, scanm = (mtab[:, T * i:T * (i + 1)] for i in range(3))
        levm = mtab[:, 3 * T:(3 + LEVELS + 1) * T].rearrange("p (l k) -> p l k", l=LEVELS + 1)
        bandW = atab[:, 0:4 * T].rearrange("p (b k) -> p b k", b=2)
        skew = nc.dram_tensor("skew", (P, 4, 384), F32).ap()
        mod_rows = nc.dram_tensor("mod_rows", (4, 2 * NMOD * D), F32).ap()
        skewed = bass.AP(skew.tensor, 127, [[4 * 384 - 1, P], [384, 4], [1, T]])
        ropeW = [atab[:, 4 * T + T * i:4 * T + T * (i + 1)] for i in range(4)]

        ps = es.enter_context(nc.psum_tensor("ps", [P, 8, 512], F32))

        def unit(b, i, step=4):
            return b + step * i, b % 4, 16 * (b // 4 + 1) + 4 * step * i

        def split_hi(act, b, i=0, step=4):
            if isinstance(i, int) and b + step * i >= UNITS:
                return
            u, s, landed = unit(b, i, step)
            act.wait_ge(S(f"raw_landed{s}"), landed)
            act.activation(w_hi[:, s, :], raw[:, s, :], ACT.Copy).then_inc(S("hi_ready"), 1)

        def split_lo(dve, b, i=0, step=4):
            if isinstance(i, int) and b + step * i >= UNITS:
                return
            u, s, _ = unit(b, i, step)
            dve.wait_ge(S("hi_ready"), u + 1)
            dve.tensor_tensor(w_lo[:, s, :], raw[:, s, :], w_hi[:, s, :],
                              ALU.subtract).then_inc(S("lo_ready"), 1)

        def tile(pe, s, k, psum, hi, lo, start, stop):
            wh, wl = w_hi[:, s, P * k:P * (k + 1)], w_lo[:, s, P * k:P * (k + 1)]
            pe.matmul(psum, wh, hi, start=start, stop=False)
            pe.matmul(psum, wh, lo, start=False, stop=False)
            return pe.matmul(psum, wl, hi, start=False, stop=stop)

        def mod_unit(pe, b, i, step, q, m):
            u, s, _ = unit(b, i, step)
            if q == 0:
                pe.wait_ge(S("mod_evac"), m + 1)
            pe.wait_ge(S("lo_ready"), u + 1)
            for k in range(2):
                for part, w in enumerate((w_hi, w_lo)):
                    mm = pe.matmul(ps[0:4, 6, :], cs[:, 2 * q + k, :], w[:, s, 512 * k:512 * (k + 1)],
                                   start=(q + k + part == 0), stop=(q == 3 and k == 1 and part == 1))
            mm.then_inc(S("unit_done"), 1)

        def mod_evacuate(act, done, m):
            act.wait_ge(S("unit_done"), done)
            act.wait_ge(S("mod_stored"), 16 * m + 1)
            act.activation(modb[:, :], ps[0:4, 6, :], ACT.Copy).then_inc(S("mod_evac"), 1)
            act.wait_ge(S("mod_evac"), m + 2)
            act.dma_start(mod_rows[:, bass.ds(512 * m, 512)], modb[:, :]).then_inc(S("mod_stored"), 16)

        def mod_reload(act, f):
            n0, n1, _ = MOD_PARTS[f]
            act.wait_ge(S("mod_stored"), 16 * (n1 // 4) + 1)
            act.dma_start(rstd[0:n1 - n0, :].rearrange("n (r p) -> n r p", r=4),
                          mod_rows[:, P * n0:P * n1].rearrange("r (n p) -> n r p", p=P)).then_inc(S("mod_loaded"), 16)

        def mod_transpose(pe, f):
            n = MOD_PARTS[f][1] - MOD_PARTS[f][0]
            pe.wait_ge(S("mod_loaded"), 16 * (f + 1))
            pe.wait_ge(S("small_loaded"), 80)
            for r in range(4):
                mm = pe.transpose(ps[:, 7, n * r:n * (r + 1)], rstd[0:n, P * r:P * (r + 1)], ident[0:n, 0:n])
            mm.then_inc(S("mod_turned"), 1)

        def mod_finish(dve, f):
            n0, n1, sublayers = MOD_PARTS[f]
            n = n1 - n0
            dve.wait_ge(S("mod_turned"), f + 1)
            by_part = ps[:, 7, 0:4 * n].rearrange("p (r n) -> p n r", r=4)
            bm = vec[:, VEC["bmod"] + n0:VEC["bmod"] + n1].unsqueeze(2).broadcast_to([P, n, 2])
            m = MOD[:, :, :, :].rearrange("p l n v -> p (l n) v")[:, n0:n1, :]
            dve.tensor_tensor(m, by_part[:, :, 0:2], bm, ALU.add).then_inc(S("mod_ready"), 1)
            dve.wait_ge(S("mod_ready"), 2 * f + 1)
            dve.tensor_tensor(m, m, by_part[:, :, 2:4], ALU.add).then_inc(S("mod_ready"), 1)
            dve.wait_ge(S("mod_ready"), 2 * f + 2)
            for l, part in sublayers:
                for v in range(2):
                    g = VEC["g1"] + (l * 6 + 2 * part) * DC
                    m = 3 * part * DC
                    dve.scalar_tensor_tensor(CA[:, l, part, :, v], MOD[:, l, m + DC:m + 2 * DC, v], 1.0,
                                             vec[:, g:g + DC], ALU.add, ALU.mult)
                    ins = dve.scalar_tensor_tensor(CG[:, l, part, :, v], MOD[:, l, m + 2 * DC:m + 3 * DC, v],
                                                   1.0 if part == 1 else 0.5, vec[:, g + DC:g + 2 * DC],
                                                   ALU.mult, ALU.mult)
            ins.then_inc(S("coef_ready"), 1)
            dve.wait_ge(S("coef_ready"), f + 1)

        def in_unit(pe, b, i, bank, N, step=4, h=None, hi=h_hi, lo=h_lo):
            u, s, _ = unit(b, i, step)
            pe.wait_ge(S("lo_ready"), u + 1)
            for k in range(DC):
                if h is not None:
                    pe.wait_ge(S("h_ready"), h + k + 1)
                mm = tile(pe, s, k, ps[:, bank, 0:N], hi[:, k, 0:N], lo[:, k, 0:N], k == 0, k == DC - 1)
            mm.then_inc(S("unit_done"), 1)

        def wait_y(eng, c, t):
            if t < DC - 1:
                eng.wait_ge(S("y_done"), (DC - 1) * (c["out"] - 1) + t + 1)
            else:
                eng.wait_ge(S("unit_done"), c["unit"])

        def hi_count(c, t):
            return HI.count(HI[t]) * c["pre"] + HI[:t + 1].count(HI[t])

        def halves(N):
            return [(v, slice(T * v, T * (v + 1))) for v in range(N // T)]

        def coef(c, t, v):
            l, part = c
            if l < 2:
                return CA[:, l, part, t, v:v + 1], MOD[:, l, 3 * part * DC + t, v:v + 1]
            at = VEC["g2"] + ((l - 2) * 3 + part) * DC + t
            return vec[:, at:at + 1], zc[:, 0:1]

        steps_before = [0]
        block = es.enter_context(nc.Block())

        @block.sync
        def _(sp):
            for s in range(RING):
                sp.dma_start(raw[:, s, :], wst[s]).then_inc(S(f"raw_landed{s}"), 16)
            with sp.Fori(1, UNITS // 4) as i:
                for s in range(RING):
                    sp.wait_ge(S("unit_done"), 4 * i + (s - 3))
                    sp.dma_start(raw[:, s, :], wst[4 * i + s]).then_inc(S(f"raw_landed{s}"), 16)
            for u in range(UNITS // 4 * 4, UNITS):
                sp.wait_ge(S("unit_done"), u - 3)
                sp.dma_start(raw[:, u % 4, :], wst[u]).then_inc(S(f"raw_landed{u % 4}"), 16)
            sp.wait_ge(S("x_ready"), NX)
            sp.dma_start(out, xT[:, :, 0:T]).then_inc(S("stored"), 16)
            sp.wait_ge(S("stored"), 16)

        @block.tensor
        def _(pe):
            def mod_pe(c):
                pe.wait_ge(S("cs_ready"), 2)
                with pe.Fori(0, MOD_FIRST) as i:
                    for q in range(4):
                        mod_unit(pe, c["unit"] + q, i, 4, q, i)
                mod_transpose(pe, 0)

            def stat(c, N, n):
                pe.wait_ge(S("sq_ready"), DC * c["norm"] + n + 1)
                pe.matmul(ps[:, 4, 0:N], ones, sq[:, n % 2, 0:N], start=(n == 0),
                          stop=(n == DC - 1)).then_inc(S("ss_done"), 1)

            def gu_pe(c):
                N, b = c["N"], c["unit"]
                with pe.Fori(0, FC // 2) as i:
                    for j in range(2):
                        in_unit(pe, b + 2 * j, i, j, N, h=c["h"] - DC if j == 0 else None)
                        in_unit(pe, b + 2 * j + 1, i, 2 + j, N)

            def gu_mod_pe(c):
                N, b = c["N"], c["unit"]
                with pe.Fori(0, FC // 2) as i:
                    for j in range(2):
                        for q in range(2):
                            in_unit(pe, b + 4 * j + 2 * q, i, 2 * q + j, N, 8, c["h"] - DC if j + q == 0 else None)
                            mod_unit(pe, b + 4 * j + 2 * q + 1, i, 8, 2 * j + q, c["mod"] + i)

            def out_pe(c, kind, follower):
                N, b, nk = c["N"], c["unit"], c["nk"]
                hi, lo = (h_hi, h_lo) if kind in ("attn", "mix") else (u_hi, u_lo)

                def one(j, i, k, start, stop):
                    u, s, _ = unit(b + j, i)
                    pe.wait_ge(S("lo_ready"), u + 1)
                    pe.wait_ge(S("ulo_ready"), c["hid"] - nk + k + 3)
                    for d in range(DC):
                        if start and d == 4:
                            pe.wait_ge(S("gated"), c["hid"])
                        mm = tile(pe, s, d, ps[:, out_bank(d), 0:N], hi[:, k, 0:N], lo[:, k, 0:N], start, stop)
                        if stop:
                            mm.then_inc(S("unit_done" if d == DC - 1 else "y_done"), 1)
                            if d == 2 and follower[0] == "post":
                                pe.wait_ge(S("gy_ready"), DC * follower[1]["post"] + 1)
                            elif d == 2 and follower[0] == "pre2":
                                pe.wait_ge(S("x_ready"), follower[1]["x"] + 1)
                            if d >= 2 and follower[0] != "add":
                                stat(follower[1], N, d - 2)
                    if stop and follower[0] != "add":
                        stat(follower[1], N, DC - 2)
                        stat(follower[1], N, DC - 1)
                    if not stop:
                        mm.then_inc(S("unit_done"), 1)

                if kind == "gu_mod":
                    mod_transpose(pe, 1 if c["mod"] == MB else 3)
                if kind in ("gu_mod", "conv"):
                    f = {MB: 1, MB + MOD_FIRST: 2, 2 * MB: 3}[c["mod"]]
                    pe.wait_ge(S("mod_ready"), 2 * f + 2)
                    pe.wait_ge(S("mod_evac"), c["mod"] + 1)
                if kind not in ("gu", "gu_mod"):
                    pe.wait_ge(S("gated"), c["hid"])
                for k in range(2):
                    one(k, 0, k, k == 0, False)
                if nk == FC:
                    with pe.Fori(0, (nk - 4) // 4) as i:
                        for j in range(4):
                            one(2 + j, i, 4 * i + (2 + j), False, False)
                    first = 2 + (nk - 4) // 4 * 4
                else:
                    first = 2
                for k in range(first, nk):
                    one(k, 0, k, False, k == nk - 1)

            def conv_pe(c):
                N, b = c["N"], c["unit"]
                for n in range(DC):
                    if n >= 2:
                        pe.wait_ge(S("gated"), c["hid"] + n - 1)
                    for m in range(3):
                        in_unit(pe, b + 7 * n + (2 * m if n < MOD_FIRST else m), 0, 3 * (n % 2) + m, N,
                                h=c["h"] - DC if n + m == 0 else None)
                        if n < MOD_FIRST:
                            for q in ((0,), (1,), (2, 3))[m]:
                                mod_unit(pe, b + 7 * n + m + 1 + q, 0, 4, q, c["mod"] + n)
                mod_transpose(pe, 2)

            def attn_pe(c):
                b = c["unit"]
                for n in range(12):
                    if n >= 4:
                        pe.wait_ge(S("w_evac"), n - 3)
                    in_unit(pe, b + n, 0, n % 4, 2 * T if n < 4 else T, h=c["h"] - DC if n == 0 else None)
                pe.wait_ge(S("w_evac"), 12)
                for n in range(10):
                    src = AK[:, n, 0:T] if n < 2 else AQ[:, n - 2, :]
                    mm = pe.matmul(ps[:, n // 2, T * (n % 2):T * (n % 2 + 1)], permW, src, start=True, stop=True)
                mm.then_inc(S("w_perm"), 1)
                for n in range(2):
                    for t in range(4):
                        mm = pe.transpose(ps[:, 5 + n, P * t:P * (t + 1)], AV[:, n, P * t:P * (t + 1)], ident)
                mm.then_inc(S("w_vt"), 1)
                pe.wait_ge(S("w_rope"), 5)
                pe.wait_ge(S("w_vv"), 2)

                def scores(n):
                    cc, hf, qb = n // 4, n // 2 % 2, n % 2
                    r = slice(64 * hf, 64 * hf + 64)
                    if n >= 4:
                        pe.wait_ge(S("w_sb"), n - 3)
                    pe.matmul(ps[:, SCORE_BANK[n % 4], 0:512], AQ[r, cc, P * qb:P * (qb + 1)], AK[r, cc // 4, :],
                              start=True, stop=True).then_inc(S("w_s"), 1)

                def turn(n):
                    pe.wait_ge(S("w_pn"), n + 1)
                    if n >= 2:
                        pe.wait_ge(S("w_pt"), n - 1)
                    for t in range(4):
                        mm = pe.transpose(ps[:, 2 + n % 2, P * t:P * (t + 1)], pn[:, n % 2, P * t:P * (t + 1)], ident)
                    mm.then_inc(S("w_tr"), 1)

                def values(n):
                    cc, hf = n // 4, n // 2 % 2
                    pe.wait_ge(S("w_pt"), n + 1)
                    if hf == 0 and cc >= 2:
                        pe.wait_ge(S("gated"), c["hid"] + cc - 1)
                    r = slice(64 * hf, 64 * hf + 64)
                    for t in range(4):
                        v0 = P * (cc // 4) + 64 * hf
                        mm = pe.matmul(ps[r, 4 + cc % 2, 0:T], VV[:, t, v0:v0 + 64], PTw[:, hf, t, :],
                                       start=(t == 0), stop=(t == 3))
                    mm.then_inc(S("w_pv"), 1)

                scores(0)
                scores(1)
                for n in range(32):
                    if n + 2 < 32:
                        scores(n + 2)
                    turn(n)
                    if n % 2 == 0 and n:
                        values(n - 1)
                values(31)

            def pair_slot(h):
                return 2 * (h % 2) + h // 2

            def mix_pe(c):
                b, l = c["unit"], c["l"]

                def need(name, per, k):
                    pe.wait_ge(S(name), per * l + k)

                for n in range(N_IN):
                    if n >= 4:
                        need("m_evac", N_IN, n - 3)
                    in_unit(pe, b + n, 0, n % 4, T, h=c["h"] - DC if n == 0 else None)
                    if n == B_G + 2:
                        need("m_evac", N_IN, B_G + 1)
                        pe.matmul(ps[:, 4, 0:T], bupt[:, l, :], Z[0:16, B_G, :], start=True, stop=True).then_inc(S("b_gate"), 1)
                        for m in range(2):
                            for t in range(TT):
                                mm = pe.transpose(ps[:, 5, P * (2 * t + m):P * (2 * t + m + 1)],
                                                  Z[:, B_V + m, P * t:P * (t + 1)], ident)
                        mm.then_inc(S("b_vt"), 1)
                    elif n == D_KV + 3:
                        need("m_sq1", 1, 1)
                        for m in range(2):
                            pe.matmul(ps[:, 6, 0:T], ones, sqm[:, m, :], start=(m == 0), stop=(m == 1))
                        pe.matmul(ps[:, 6, T:2 * T], ones, sqm[:, 2, :], start=True, stop=True).then_inc(S("m_ss1"), 1)
                    elif n == A_K + 4:
                        need("m_sqa", 1, 1)
                        need("b_g", 1, 1)
                        need("b_vb", 2, 1)
                        for m in range(2):
                            mm = pe.matmul(ps[:, 4 + m, :], bones64,
                                           sqm[:, 4 + 2 * m:6 + 2 * m, :].rearrange("p a t -> p (a t)"),
                                           start=True, stop=True)
                        mm.then_inc(S("m_ssa"), 1)
                need("d_cn", 1, 1)
                pe.wait_ge(S("lo_ready"), b + N_IN + 1)
                need("m_rta", 1, 1)
                need("m_rt", 1, 1)
                for h in range(4):
                    for k in range(2):
                        mm = tile(pe, (b + N_IN) % RING, 4 * k + h, ps[:, 4 + h // 2, T * (h % 2):T * (h % 2 + 1)], cn_hi[:, k, :],
                                  cn_lo[:, k, :], k == 0, k == 1)
                mm.then_inc(S("unit_done"), 1)
                pe.wait_ge(S("lo_ready"), b + N_IN + 2)
                for h in range(4):
                    mm = tile(pe, (b + N_IN + 1) % RING, h, ps[:, 6 + h // 2, T * (h % 2):T * (h % 2 + 1)], cn_hi[:, 2, :],
                              cn_lo[:, 2, :], True, True)
                mm.then_inc(S("unit_done"), 1)
                def index_head(n):
                    qb, h = n // 8, n % 8
                    r = slice(32 * (h % 4), 32 * (h % 4) + 32)
                    if n == 0:
                        need("b_vb", 2, 2)
                        need("i_w", 1, 1)
                    if n >= 2:
                        need("i_r", 16, n - 1)
                    pe.matmul(ps[:, 6 + n % 2, 0:P * (qb + 1)], Z[r, I_Q + h // 4, P * qb:P * (qb + 1)],
                              Z[r, I_K, 0:P * (qb + 1)], start=True, stop=True).then_inc(S("i_s"), 1)

                need("m_evac", N_IN, N_IN)
                need("b_qk", 1, 1)
                for v in range(LEVELS + 1):
                    if v >= 1:
                        need("b_at", LEVELS + 1, v)
                    for h in range(4):
                        r = slice(32 * h, 32 * h + 32)
                        for t in range(TT):
                            kk = KP[r, v, P * t:P * (t + 1)] if v < LEVELS else Z[r, B_K, P * t:P * (t + 1)]
                            qq = QP[r, v, P * t:P * (t + 1)] if v < LEVELS else Z[r, B_Q, P * t:P * (t + 1)]
                            mm = pe.matmul(ps[:, h, P * t:P * (t + 1)], kk, qq, start=True, stop=True)
                            if (h, t) == (3, TT - 1):
                                mm.then_inc(S("b_lv"), 1)
                            if 1 <= v <= TT:
                                index_head(8 * (v - 1) + TT * h + t)
                    if v == 0:
                        need("d_e", 4, 3)
                        for t in range(TT):
                            mm = pe.transpose(ps[:, 7, 8 * t:8 * t + 8], Z[0:8, I_W, P * t:P * (t + 1)], ident[0:8, 0:8])
                        mm.then_inc(S("i_wt"), 1)
                        for t in range(TT):
                            mm = pe.transpose(ps[:, 6, P * t:P * (t + 1)], KP[:, LEVELS, P * t:P * (t + 1)], ident)
                        mm.then_inc(S("b_kt"), 1)
                    elif v == LEVELS - 1:
                        need("d_sq", 1, 1)
                        need("c_rt", 1, 1)
                        for h in range(4):
                            mm = pe.matmul(ps[:, 6, :].rearrange("p (a t) -> p a t", a=2), esel[0:96, 96 - 32 * h:224 - 32 * h],
                                           sqm[0:96, :, :].rearrange("p (a h) t -> p h a t", a=2)[:, h], start=(h == 0),
                                           stop=(h == 3))
                        mm.then_inc(S("d_ss"), 1)
                    elif v == TT + 1:
                        need("i_r", 16, 16)
                        need("m_sqc", 1, 1)
                        for n in range(2):
                            mm = pe.matmul(ps[:, 6, 0:T], ones, sqm[:, n, :], start=(n == 0), stop=(n == 1))
                        mm.then_inc(S("m_ssc"), 1)
                        need("m_rta", 1, 1)
                        for k in range(3):
                            r = slice(64 * (k % 2), 64 * (k % 2) + 64)
                            mm = pe.matmul(ps[:, (7, 4, 5)[k], 0:2 * P], kdT[r, k // 2, :], VB[r, k // 2, :],
                                           start=True, stop=True)
                        mm.then_inc(S("b_st"), 1)
                need("b_at", LEVELS + 1, LEVELS + 1)
                need("b_s", 2, 2)
                for h in range(4):
                    for t in range(TT):
                        r = slice(64 * (h % 2), 64 * (h % 2) + 64)
                        pe.matmul(ps[r, 4, T * (h // 2) + P * t:T * (h // 2) + P * (t + 1)],
                                  VB[:, t, 64 * h:64 * h + 64], AT[:, h, P * t:P * (t + 1)], start=True, stop=True)
                for m in range(2):
                    for k in range(1, 4):
                        mm = pe.matmul(ps[:, 5, T * m + 64 * k:T * m + 64 * (k + 1)], ST[:, k - 1, P * m:P * (m + 1)],
                                       QP[:, LEVELS, 64 * k:64 * (k + 1)], start=True, stop=True)
                mm.then_inc(S("b_o"), 1)
                need("d_rr", 1, 1)
                for h in range(4):
                    mm = pe.matmul(ps[0:96, h, :], ones[32 * h:32 * h + 1, 0:96], rm[32 * h:32 * h + 1, 0:2 * T],
                                   start=True, stop=True)
                mm.then_inc(S("d_rb"), 1)
                need("b_sq", 1, 1)
                need("d_rt", 1, 1)
                pe.matmul(ps[:, 6, :], bones64, sqm[:, 0:2, :].rearrange("p a t -> p (a t)"), start=True,
                          stop=True).then_inc(S("b_ss"), 1)

                need("d_n", 2, 2)
                for n in range(4):
                    src = (DQ if n < 2 else DK)[0:96, 2 * (n % 2):2 * (n % 2) + 2, :]
                    mm = pe.matmul(ps[0:96, n, :].rearrange("p (a t) -> p a t", a=2), permD[0:96, 0:96], src, start=True, stop=True)
                mm.then_inc(S("d_perm"), 1)
                need("d_e", 4, 4)
                for t in range(TT):
                    for h in range(4):
                        mm = pe.transpose(ps[:, 4 + t, P * h:P * (h + 1)], DV[:, h, P * t:P * (t + 1)], ident)
                mm.then_inc(S("d_vt"), 1)

                for m in range(2):
                    for t in range(TT):
                        mm = pe.transpose(ps[:, 7, P * (2 * t + m):P * (2 * t + m + 1)], Z[:, A_V + m, P * t:P * (t + 1)],
                                          ident)
                mm.then_inc(S("a_vt"), 1)

                def scores(k):
                    qb = k % TT
                    kc = P * (qb + 1)
                    if k >= 2:
                        need("s_nm", 4, k - 1)
                        need("a_n", 2, 2)
                    for h in range(4):
                        if k < TT:
                            g, qq, kk = h, DQ[0:96, h, :], DK[0:96, h, :]
                        else:
                            r = slice(64 * (h % 2), 64 * (h % 2) + 64)
                            g, qq, kk = pair_slot(h), Z[r, A_Q + h // 2, :], Z[r, A_K + h // 2, :]
                        mm = pe.matmul(ps[:, 4 * (k % 2) + g // 2, T * (g % 2):T * (g % 2) + kc],
                                       qq[:, P * qb:P * (qb + 1)], kk[:, 0:kc], start=True, stop=True)
                    mm.then_inc(S("s_s"), 1)

                def turn(k):
                    need("s_p", 4, k + 1)
                    if k >= 1:
                        need("s_pt", 4, k)
                    for t in range(k % TT + 1):
                        for h in range(4):
                            mm = pe.transpose(ps[:, 2 + t, P * h:P * (h + 1)], PR(k)[:, h, P * t:P * (t + 1)], ident)
                    mm.then_inc(S("s_tr"), 1)

                def values(k):
                    qb = k % TT
                    need("s_pt", 4, k + 1)
                    for h in range(4):
                        r = slice(64 * (h % 2), 64 * (h % 2) + 64)
                        for t in range(qb + 1):
                            vv, g = (VT[:, t, h, 64:128], h) if k < TT else (VA[:, t, h // 2, r], pair_slot(h))
                            mm = pe.matmul(ps[r, 6 + k // TT, T * (h // 2) + P * qb:T * (h // 2) + P * (qb + 1)], vv,
                                           PTm[:, t, g, P * qb:P * (qb + 1)], start=(t == 0), stop=(t == qb))
                    mm.then_inc(S("s_pv"), 1)

                need("d_r", 2, 2)
                need("b_rt", 1, 1)
                scores(0)
                need("d_vt2", 2, 2)
                scores(1)
                turn(0)
                scores(2)
                turn(1)
                values(0)
                scores(3)
                turn(2)
                values(1)
                turn(3)
                need("a_vt2", 1, 1)
                values(2)
                values(3)

            def bias_rows():
                pe.wait_ge(S("rbb_ready"), 1)
                pe.wait_ge(S("rt_ready"), 1)
                for h in range(4):
                    mm = pe.matmul(ps[:, 1 + pair_slot(h), 0:384], rbb[:, h, :], oh[:, :], start=True, stop=True)
                mm.then_inc(S("bias_rows"), 1)
                pe.wait_ge(S("bias_copied"), 1)

            plan = list(PLAN)
            for n, (kind, c) in enumerate(plan):
                if kind == "mod":
                    mod_pe(c)
                elif kind == "gu_mod":
                    gu_mod_pe(c)
                elif kind == "pre":
                    for t in range(DC):
                        stat(c, c["N"], t)
                    if c["norm"] == 0:
                        bias_rows()
                elif kind == "pre2" and c["update"] is None:
                    for t in range(DC):
                        stat(c, T, t)
                elif kind == "gu":
                    gu_pe(c)
                elif kind == "out":
                    out_pe(c, plan[n - 1][0], plan[n + 1] if n + 1 < len(plan) else ("add", None))
                elif kind == "conv":
                    conv_pe(c)
                elif kind == "attn":
                    attn_pe(c)
                elif kind == "mix":
                    mix_pe(c)

        @block.scalar
        def _(act):
            def root(c, N, scale):
                act.wait_ge(S("ss_done"), DC * (c["norm"] + 1))
                act.activation(rt[:, 0:N], ps[:, 4, 0:N], ACT.Sqrt, bias=epsc[:, 0:1],
                               scale=scale).then_inc(S("rt_ready"), 1)

            def load_root():
                act.activation(spare[:, 0:1], epsc[:, 0:1], ACT.Sqrt)

            def square(c, N, n, src):
                if DC * c["norm"] + n - 1 > 0:
                    act.wait_ge(S("ss_done"), DC * c["norm"] + n - 1)
                act.activation(sq[:, n % 2, 0:N], src, ACT.Square).then_inc(S("sq_ready"), 1)

            def wait_x(c, t):
                if not c["x"]:
                    act.wait_ge(S("x_loaded"), 16)
                elif t < DC - POOL_X:
                    act.wait_ge(S("x_ready"), c["x"] - (DC - POOL_X) + t + 1)
                else:
                    act.wait_ge(S("xp_ready"), c["xp"] - DC + t + 1)

            def pre_act(c):
                N = c["N"]
                for n, t in enumerate(X_ORDER):
                    wait_x(c, t)
                    square(c, N, n, xT[:, t, 0:N])
                root(c, N, 1.0 / D)
                if c["norm"] == 0:
                    act.wait_ge(S("bias_rows"), 1)
                    act.activation(sqb[:, :, :], ps[:, 1:5, 0:384], ACT.Copy).then_inc(S("bias_copied"), 1)
                    act.wait_ge(S("bias_copied"), 1)
                    act.dma_start(skew, sqb[:, :, :]).then_inc(S("skew_stored"), 16)
                for t in range(DC):
                    act.wait_ge(S("tn_ready"), DC * c["pre"] + t + 1)
                    for v, r in halves(N):
                        a, s = coef(c["coef"], t, v)
                        ins = act.activation(hf[:, t, r], tn[:, t, r], ACT.Identity, bias=s, scale=a)
                    ins.then_inc(S("hf_ready"), 1)
                    if HI[t] == "act":
                        act.wait_ge(S("hf_ready"), DC * c["pre"] + t + 1)
                        act.activation(h_hi[:, t, 0:N], hf[:, t, 0:N], ACT.Identity).then_inc(S("hi_by_act"), 1)

            def pre2_act(c):
                load_root()
                for t in range(DC):
                    if c["update"] is None:
                        wait_x(c, t)
                    else:
                        act.wait_ge(S("x_ready"), c["x"] + t + 1)
                    square(c, T, t, xT[:, t, 0:T])
                    a, _ = coef(c["coef"], t, 0)
                    act.activation(h_hi[:, t, 0:T], xT[:, t, 0:T], ACT.Identity, scale=a).then_inc(S("h_hi_ready"), 1)
                root(c, T, 1.0 / D)

            def gu_act(c):
                N, b = c["N"], c["unit"]
                with act.Fori(0, FC // 2) as i:
                    for j in range(2):
                        split_hi(act, b + 2 * j + 2, i)
                        if c["late"]:
                            act.wait_ge(S("gate_scaled"), FC * c["fin"] + 2 * i + (j + 1))
                        else:
                            act.wait_ge(S("unit_done"), b + 2 * j + 1 + 4 * i)
                        act.activation(gt[:, j, 0:N], gt[:, j, 0:N] if c["late"] else ps[:, j, 0:N],
                                       ACT.Silu).then_inc(S("silu_done"), 1)
                        split_hi(act, b + 2 * j + 3, i)

            def gu_mod_act(c):
                N, b = c["N"], c["unit"]
                with act.Fori(0, FC // 2) as i:
                    for j in range(2):
                        split_hi(act, b + 4 * j + 2, i, 8)
                        act.wait_ge(S("unit_done"), b + 4 * j + 1 + 8 * i)
                        act.activation(gt[:, j, 0:N], ps[:, j, 0:N], ACT.Silu).then_inc(S("silu_done"), 1)
                        split_hi(act, b + 4 * j + 3, i, 8)
                        split_hi(act, b + 4 * j + 4, i, 8)
                        if j == 1:
                            mod_evacuate(act, b + 8 + 8 * i, c["mod"] + i)
                        split_hi(act, b + 4 * j + 5, i, 8)

            def mod_act(c):
                b = c["unit"]
                with act.Fori(0, MOD_FIRST) as i:
                    for q in range(3):
                        split_hi(act, b + q + 2, i)
                    mod_evacuate(act, b + 4 + 4 * i, i)
                    split_hi(act, b + 5, i)
                mod_reload(act, 0)

            def out_act(c):
                b, nk = c["unit"], c["nk"]
                full = (nk // 4) if b + nk + 2 <= UNITS else nk // 4 - 1
                with act.Fori(0, full) as i:
                    for j in range(4):
                        split_hi(act, b + 2 + j, i)
                for k in range(4 * full, nk):
                    split_hi(act, b + 2 + k)

            def post_act(c):
                N = c["N"]
                load_root()
                for t in range(DC):
                    wait_y(act, c, t)
                    square(c, N, t, ps[:, out_bank(t), 0:N])
                root(c, N, 1.0 / D)

            def conv_act(c):
                b = c["unit"]
                for n in range(DC):
                    first = b + 7 * n
                    split_hi(act, first + 2)
                    split_hi(act, first + 3)
                    act.wait_ge(S("unit_done"), first + (3 if n < MOD_FIRST else 2))
                    if n >= 2:
                        act.wait_ge(S("cu_ready"), n - 1)
                    act.activation(gt[:, n % 2, :], ps[:, 3 * (n % 2) + 1, :], ACT.Copy).then_inc(S("cg_ready"), 1)
                    for q in range(4, 8 if n < MOD_FIRST else 5):
                        split_hi(act, first + q)
                    act.wait_ge(S("cu_ready"), n + 1)
                    if n >= 2:
                        act.wait_ge(S("gated"), c["hid"] + n - 1)
                    w = VEC["convw"] + DC + n
                    act.activation(cy[:, n % 2, :, :], cu[:, n % 2, :, 1:T + 1], ACT.Copy,
                                   scale=vec[:, w:w + 1]).then_inc(S("cy_ready"), 1)
                    if n < MOD_FIRST:
                        mod_evacuate(act, first + 7, c["mod"] + n)
                        split_hi(act, first + 8)
                    if n == MOD_FIRST - 1:
                        mod_reload(act, 2)

            def attn_act(c):
                b = c["unit"]
                act.wait_ge(S("unit_done"), b)
                act.dma_start(atab[:, :], attabs).then_inc(S("atab_loaded"), 16)
                for n in range(12):
                    split_hi(act, b + n + 2)
                    act.wait_ge(S("unit_done"), b + n + 1)
                    dst = AK[:, n, :] if n < 2 else AV[:, n - 2, :] if n < 4 else AQ[:, n - 4, :]
                    act.activation(dst, ps[:, n % 4, 0:2 * T if n < 4 else T], ACT.Copy).then_inc(S("w_evac"), 1)
                act.wait_ge(S("w_vt"), 1)
                for n in range(2):
                    act.activation(VV[:, :, P * n:P * (n + 1)],
                                   ps[:, 5 + n, :].rearrange("p (t v) -> p t v", t=4), ACT.Copy).then_inc(S("w_vv"), 1)

                def pt(n):
                    hf, qb = n // 2 % 2, n % 2
                    act.wait_ge(S("w_tr"), n + 1)
                    if n >= 4:
                        act.wait_ge(S("w_pv"), n // 2 - 1)
                    act.activation(PTw[:, hf, :, P * qb:P * (qb + 1)],
                                   ps[:, 2 + n % 2, :].rearrange("p (t q) -> p t q", t=4), ACT.Copy).then_inc(S("w_pt"), 1)

                for n in range(32):
                    head = 2 * (n // 4) + n // 2 % 2
                    sk = VEC["sink"] + head
                    act.wait_ge(S("w_nm"), n + 1)
                    if n >= 2:
                        act.wait_ge(S("w_pn"), n - 1)
                    act.activation(pw[:, n % 2, :], sw[:, n % 2, :], ACT.Exp, bias=aw[:, n % 2, 1:2],
                                   accum_out=aw[:, n % 2, 2:3]).then_inc(S("w_e"), 1)
                    act.activation(aw[:, n % 2, 3:4], vec[:, sk:sk + 1], ACT.Exp,
                                   bias=aw[:, n % 2, 1:2]).then_inc(S("w_e"), 1)
                    if n >= 1:
                        pt(n - 1)
                pt(31)


            def mix_act(c):
                b, l = c["unit"], c["l"]

                def need(name, per, k):
                    act.wait_ge(S(name), per * l + k)

                act.wait_ge(S("unit_done"), b)
                act.dma_start(mtab[:, :], mixtabs).then_inc(S("mtab_loaded"), 16)
                for n in range(N_IN):
                    split_hi(act, b + n + 2)
                    if n >= 6:
                        if n == 6:
                            need("hp_ready", 1, 1)
                        first = PER_CHUNK * (n - 6) + 2
                        for q in range(first, first + PER_CHUNK if n < N_IN - 1 else 2 * KTAPS):
                            need("c_tap", 2 * KTAPS, max(q - 3, 2))
                            act.activation(tap(q), hp[:, q % 2, q // 2:q // 2 + T], ACT.Copy,
                                           scale=vec[:, VEC[f"cw{l}"] + q:VEC[f"cw{l}"] + q + 1]).then_inc(S("c_prod"), 1)
                    if n == C_G + 2:
                        need("m_evac", N_IN, C_G + 2)
                        act.activation(Z[:, C_G:C_G + 2, :], Z[:, C_G:C_G + 2, :], ACT.Sigmoid).then_inc(S("c_sig"), 1)
                    elif n == 11:
                        need("b_vt", 1, 1)
                        act.activation(VB[:, :, :].rearrange("p a t -> p (a t)"), ps[:, 5, :], ACT.Copy).then_inc(S("b_vb"), 1)
                    elif n == 12:
                        need("b_g", 1, 1)
                        act.activation(G2, G1, ACT.Abs).then_inc(S("b_a"), 1)
                        need("b_a", 3, 1)
                        act.activation(G2, G2, ACT.Exp, scale=-1.0).then_inc(S("b_a"), 1)
                    elif n == 13:
                        need("b_a", 3, 2)
                        act.activation(G2, G2, ACT.Ln, bias=1.0).then_inc(S("b_a"), 1)
                    elif n == 15:
                        need("m_evac", N_IN, D_KV + 1)
                        act.activation(sqm[:, 0:3, :], Z[:, D_Q:D_Q + 3, :], ACT.Square).then_inc(S("m_sq1"), 1)
                    elif n == 16:
                        need("b_e", 1, 1)
                        act.activation(EB[:, :, :], EB[:, :, :], ACT.Exp, scale=1 / 16).then_inc(S("b_p"), 1)
                    elif n == 18:
                        need("m_ss1", 1, 1)
                        act.activation(rm[:, 0:T], ps[:, 6, 0:T], ACT.Sqrt, bias=epsc[:, 0:1], scale=1 / 256)
                        act.activation(rm[:, T:2 * T], ps[:, 6, T:2 * T], ACT.Sqrt, bias=epsc[:, 0:1],
                                       scale=1 / 128).then_inc(S("m_rt"), 1)
                    elif n == 20:
                        need("m_evac", N_IN, A_K + 2)
                        act.activation(sqm[:, 4:8, :], Z[:, A_Q:A_Q + 4, :], ACT.Square).then_inc(S("m_sqa"), 1)
                    elif n == 23:
                        need("m_ssa", 1, 1)
                        act.activation(rm[:, 2 * T:6 * T], ps[:, 4:6, :].rearrange("p a t -> p (a t)"), ACT.Sqrt,
                                       bias=epsc[:, 0:1], scale=1 / 64).then_inc(S("m_rta"), 1)
                act.wait_ge(S("unit_done"), b + N_IN + 2)
                act.activation(DQ[:, :, :], ps[:, 4:6, :].rearrange("p a (b t) -> p (a b) t", b=2), ACT.Copy).then_inc(S("d_e"), 1)
                act.activation(DV[:, :, :], ps[:, 6:8, :].rearrange("p a (b t) -> p (a b) t", b=2), ACT.Copy).then_inc(S("d_e"), 1)
                act.activation(DK[0:64, :, :], ps[0:64, 6:8, :].rearrange("p a (b t) -> p (a b) t", b=2),
                               ACT.Copy).then_inc(S("d_e"), 1)
                act.activation(DK[64:96, :, :], Z[64:96, D_PE, :].unsqueeze(1).broadcast_to([32, 4, T]),
                               ACT.Copy).then_inc(S("d_e"), 1)
                split_hi(act, b + N_IN + 2)
                split_hi(act, b + N_IN + 3)
                need("i_wt", 1, 1)
                act.activation(iw[:, :, :].rearrange("p a t -> p (a t)"), ps[:, 7, 0:16], ACT.Copy,
                               scale=8 ** -0.5).then_inc(S("i_w"), 1)
                need("b_kt", 1, 1)
                act.activation(kdT[:, :, :].rearrange("p a t -> p (a t)"), ps[:, 6, 0:2 * P], ACT.Copy).then_inc(S("b_vb"), 1)
                for n in range(16):
                    kc = P * (n // 8 + 1)
                    need("i_s", 16, n + 1)
                    if n >= 2:
                        need("i_a", 16, n - 1)
                    act.activation(RI(n)[:, 0:kc], ps[:, 6 + n % 2, 0:kc], ACT.Relu, scale=32 ** -0.5).then_inc(S("i_r"), 1)
                need("c_tap", 2 * KTAPS, 2 * KTAPS)
                act.activation(sqm[:, 0:2, :], hc[:, :, :], ACT.Square).then_inc(S("m_sqc"), 1)
                need("m_ssc", 1, 1)
                act.activation(rm[:, 6 * T:7 * T], ps[:, 6, 0:T], ACT.Sqrt, bias=epsc[:, 0:1],
                               scale=1 / 256).then_inc(S("c_rt"), 1)
                need("c_n", 1, 1)
                act.activation(hc[:, :, :], hc[:, :, :], ACT.Silu).then_inc(S("c_silu"), 1)
                need("d_e", 4, 4)
                act.activation(sqm[0:96, 0:4, :], DQ[0:96, :, :], ACT.Square)
                act.activation(sqm[0:96, 4:8, :], DK[0:96, :, :], ACT.Square).then_inc(S("d_sq"), 1)
                need("d_ss", 1, 1)
                act.activation(rm[:, 0:2 * T], ps[:, 6, :], ACT.Sqrt, bias=epsc[:, 0:1], scale=1 / 96).then_inc(S("d_rt"), 1)
                need("b_o", 1, 1)
                act.activation(OB[:, :, :].rearrange("p a t -> p (a t)"), ps[:, 4, :], ACT.Copy).then_inc(S("b_oc"), 1)
                need("b_oi", 1, 1)
                act.activation(sqm[:, 0:2, :], OB[:, :, :], ACT.Square).then_inc(S("b_sq"), 1)
                need("b_ss", 1, 1)
                act.activation(rm[:, 6 * T:8 * T], ps[:, 6, :], ACT.Sqrt, bias=epsc[:, 0:1], scale=1 / 64).then_inc(S("b_rt"), 1)
                act.activation(Z[:, B_R:B_R + 2, :], Z[:, B_R:B_R + 2, :], ACT.Silu).then_inc(S("b_silu"), 1)
                need("d_vt", 1, 1)
                for t in range(TT):
                    act.activation(VT[:, t, :, :], ps[:, 4 + t, :].rearrange("p (h v) -> p h v", h=4),
                                   ACT.Copy).then_inc(S("d_vt2"), 1)

                need("a_vt", 1, 1)
                act.activation(VA[:, :, :, :].rearrange("p t a v -> p (t a v)"), ps[:, 7, :], ACT.Copy).then_inc(S("a_vt2"), 1)

                def exponentials(k):
                    kc = P * (k % TT + 1)
                    m = am[:, k % 2, :]
                    need("s_nm", 4, k + 1)
                    for h in range(4):
                        ins = act.activation(PR(k)[:, h, 0:kc], LG(k)[:, h, 0:kc], ACT.Exp, bias=m[:, 4 + h:5 + h],
                                             accum_out=m[:, 8 + h:9 + h])
                    ins.then_inc(S("s_e"), 1)

                def turned(k):
                    qb = k % TT
                    need("s_tr", 4, k + 1)
                    if k >= 2:
                        need("s_pv", 4, k - 1)
                    for t in range(qb + 1):
                        ins = act.activation(PTm[:, t, :, P * qb:P * (qb + 1)],
                                             ps[:, 2 + t, :].rearrange("p (h q) -> p h q", h=4), ACT.Copy)
                    ins.then_inc(S("s_pt"), 1)

                exponentials(0)
                for k in range(1, 4):
                    exponentials(k)
                    turned(k - 1)
                turned(3)

            act.dma_start(cv[:, :, :], cvec).then_inc(S("c_loaded"), 16)
            act.dma_start(vec[:, :], vecs).then_inc(S("small_loaded"), 16)
            act.dma_start(tabs[:, :], ctabs).then_inc(S("small_loaded"), 16)
            act.dma_start(bupt[:, :, :], bup).then_inc(S("small_loaded"), 16)
            act.dma_start(rl[:, :], relb).then_inc(S("small_loaded"), 16)
            act.dma_start(oh[:, :], onehot).then_inc(S("small_loaded"), 16)
            act.dma_start(xT[:, :, :], xin).then_inc(S("x_loaded"), 16)
            act.wait_ge(S("c_loaded"), 16)
            act.wait_ge(S("init"), 1)
            act.activation(cv[:, :, :], cv[:, :, :], ACT.Silu).then_inc(S("cv_ready"), 1)
            act.wait_ge(S("cv_ready"), 1)
            act.activation(cs[:, :, 0:2], cv[:, :, :], ACT.Copy).then_inc(S("cs_ready"), 1)
            split_hi(act, 0)
            split_hi(act, 1)
            for kind, c in PLAN:
                if kind == "mod":
                    mod_act(c)
                elif kind == "gu_mod":
                    gu_mod_act(c)
                    mod_reload(act, 1 if c["mod"] < MB else 3)
                    if c["mod"] < MB:
                        act.wait_ge(S("skew_stored"), 16)
                        act.dma_start(biasA[:, :, :], skewed).then_inc(S("bias_loaded"), 16)
                elif kind == "pre":
                    pre_act(c)
                elif kind == "pre2":
                    pre2_act(c)
                elif kind == "gu":
                    gu_act(c)
                elif kind == "out":
                    out_act(c)
                elif kind == "post":
                    post_act(c)
                elif kind == "conv":
                    conv_act(c)
                elif kind == "attn":
                    attn_act(c)
                elif kind == "mix":
                    mix_act(c)

        @block.vector
        def _(dve):
            def recip(c, N):
                dve.wait_ge(S("rt_ready"), c["norm"] + 1)
                dve.reciprocal(rstd[:, 0:N], rt[:, 0:N]).then_inc(S("rstd_ready"), 1)
                dve.wait_ge(S("rstd_ready"), c["norm"] + 1)

            def pre_dve(c):
                N, h = c["N"], c["h"]
                recip(c, N)
                for t in range(DC + LAG):
                    if t < DC:
                        dve.tensor_tensor(tn[:, t, 0:N], xT[:, t, 0:N], rstd[:, 0:N], ALU.mult).then_inc(S("tn_ready"), 1)
                    if t >= LAG:
                        k = t - LAG
                        if HI[k] == "dve":
                            dve.wait_ge(S("hf_ready"), DC * c["pre"] + k + 1)
                            dve.tensor_copy(h_hi[:, k, 0:N], hf[:, k, 0:N]).then_inc(S("hi_by_dve"), 1)
                        dve.wait_ge(S("hi_by_" + HI[k]), hi_count(c, k))
                        dve.tensor_tensor(h_lo[:, k, 0:N], hf[:, k, 0:N], h_hi[:, k, 0:N],
                                          ALU.subtract).then_inc(S("h_ready"), 1)

            def pre2_dve(c):
                h = c["h"]
                for t in range(DC + 2):
                    if t < DC and c["update"] is not None:
                        wait_y(dve, c, t)
                        dve.scalar_tensor_tensor(xT[:, t, 0:T], ps[:, out_bank(t), 0:T], c["update"], xT[:, t, 0:T],
                                                 ALU.mult, ALU.add).then_inc(S("x_ready"), 1)
                    if t >= 2:
                        if c["update"] is None and t == DC - POOL_X + 2:
                            dve.wait_ge(S("xp_ready"), c["xp"])
                        dve.wait_ge(S("h_hi_ready"), DC * c["pre2"] + t - 1)
                        a, _ = coef(c["coef"], t - 2, 0)
                        dve.scalar_tensor_tensor(h_lo[:, t - 2, 0:T], xT[:, t - 2, 0:T], a, h_hi[:, t - 2, 0:T],
                                                 ALU.mult, ALU.subtract).then_inc(S("h_ready"), 1)
                recip(c, T)

            def gu_late_dve(c):
                b, hid = c["unit"], c["hid"]
                with dve.Fori(0, FC // 2) as i:
                    for j in range(2):
                        split_lo(dve, b + 2 * j + 2, i)
                        dve.wait_ge(S("unit_done"), b + 2 * j + 1 + 4 * i)
                        dve.tensor_tensor(gt[:, j, 0:T], ps[:, j, 0:T], rstd[:, 0:T], ALU.mult).then_inc(S("gate_scaled"), 1)
                        split_lo(dve, b + 2 * j + 3, i)
                        dve.wait_ge(S("unit_done"), b + 2 * j + 2 + 4 * i)
                        dve.tensor_tensor(sq[:, j, 0:T], ps[:, 2 + j, 0:T], rstd[:, 0:T], ALU.mult).then_inc(S("up_scaled"), 1)
                        dve.wait_ge(S("up_scaled"), FC * c["fin"] + 2 * i + (j + 1))
                        dve.wait_ge(S("silu_done"), FC * c["ffn"] + 2 * i + (j + 1))
                        dve.wait_ge(S("ulo_ready"), hid + 2 * i + (j + 1))
                        dve.tensor_tensor(ut[:, j, 0:T], gt[:, j, 0:T], sq[:, j, 0:T], ALU.mult).then_inc(S("gated"), 1)

            def gu_dve(c):
                N, b, hid = c["N"], c["unit"], c["hid"]
                with dve.Fori(0, FC // 2) as i:
                    for j in range(2):
                        split_lo(dve, b + 2 * j + 2, i)
                        split_lo(dve, b + 2 * j + 3, i)
                        dve.wait_ge(S("silu_done"), FC * c["ffn"] + 2 * i + (j + 1))
                        dve.wait_ge(S("unit_done"), b + 2 * j + 2 + 4 * i)
                        dve.wait_ge(S("ulo_ready"), hid + 2 * i + (j + 1))
                        dve.tensor_tensor(ut[:, j, 0:N], gt[:, j, 0:N], ps[:, 2 + j, 0:N],
                                          ALU.mult).then_inc(S("gated"), 1)

            def gu_mod_dve(c):
                N, b, hid = c["N"], c["unit"], c["hid"]
                with dve.Fori(0, FC // 2) as i:
                    for j in range(2):
                        split_lo(dve, b + 4 * j + 2, i, 8)
                        split_lo(dve, b + 4 * j + 3, i, 8)
                        split_lo(dve, b + 4 * j + 4, i, 8)
                        dve.wait_ge(S("silu_done"), FC * c["ffn"] + 2 * i + (j + 1))
                        dve.wait_ge(S("unit_done"), b + 4 * j + 3 + 8 * i)
                        dve.wait_ge(S("ulo_ready"), hid + 2 * i + (j + 1))
                        dve.tensor_tensor(ut[:, j, 0:N], gt[:, j, 0:N], ps[:, 2 + j, 0:N],
                                          ALU.mult).then_inc(S("gated"), 1)
                        split_lo(dve, b + 4 * j + 5, i, 8)

            def out_dve(c):
                b, nk = c["unit"], c["nk"]
                full = (nk // 4) if b + nk + 2 <= UNITS else nk // 4 - 1
                with dve.Fori(0, full) as i:
                    for j in range(4):
                        split_lo(dve, b + 2 + j, i)
                for k in range(4 * full, nk):
                    split_lo(dve, b + 2 + k)

            def post_dve(c):
                N = c["N"]
                l, part = c["coef"]
                for t in range(DC):
                    dve.wait_ge(S("sq_ready"), DC * c["norm"] + t + 1)
                    for v, r in halves(N):
                        ins = dve.tensor_scalar(gy[:, t, r], ps[:, out_bank(t), r], CG[:, l, part, t, v:v + 1], None, ALU.mult)
                    ins.then_inc(S("gy_ready"), 1)
                recip(c, N)
                mine = DC - POOL_X
                for t in range(mine + 1):
                    if t < mine:
                        dve.wait_ge(S("gy_ready"), DC * c["post"] + t + 1)
                        dve.tensor_tensor(gy[:, t, 0:N], gy[:, t, 0:N], rstd[:, 0:N], ALU.mult).then_inc(S("yn_ready"), 1)
                    if t >= 1:
                        dve.wait_ge(S("yn_ready"), mine * c["post"] + t)
                        dve.tensor_tensor(xT[:, t - 1, 0:N], xT[:, t - 1, 0:N], gy[:, t - 1, 0:N],
                                          ALU.add).then_inc(S("x_ready"), 1)

            def add_dve(c):
                for t in range(DC):
                    wait_y(dve, c, t)
                    dve.scalar_tensor_tensor(xT[:, t, 0:T], ps[:, out_bank(t), 0:T], c["weight"], xT[:, t, 0:T],
                                             ALU.mult, ALU.add).then_inc(S("x_ready"), 1)

            def conv_dve(c):
                b, hid = c["unit"], c["hid"]
                for n in range(DC):
                    first = b + 7 * n
                    for m in range(2, 8 if n < MOD_FIRST else 5):
                        split_lo(dve, first + m)
                    if n == 0:
                        dve.memset(cu[:, :, :, 0:1], 0.0)
                        dve.memset(cu[:, :, :, T + 1:T + 2], 0.0).then_inc(S("cu_zero"), 1)
                        dve.wait_ge(S("cu_zero"), 1)
                    dve.wait_ge(S("cg_ready"), n + 1)
                    dve.wait_ge(S("unit_done"), first + (5 if n < MOD_FIRST else 3))
                    dve.tensor_tensor(cu[:, n % 2, :, 1:T + 1], gt[:, n % 2, :].rearrange("p (v t) -> p v t", v=2),
                                      ps[:, 3 * (n % 2) + 2, :].rearrange("p (v t) -> p v t", v=2),
                                      ALU.mult).then_inc(S("cu_ready"), 1)
                    dve.wait_ge(S("cy_ready"), n + 1)
                    dve.wait_ge(S("cu_ready"), n + 1)
                    for m, o in ((0, 0), (2, 2)):
                        w = VEC["convw"] + DC * m + n
                        dve.scalar_tensor_tensor(cy[:, n % 2, :, :], cu[:, n % 2, :, o:o + T], vec[:, w:w + 1],
                                                 cy[:, n % 2, :, :], ALU.mult, ALU.add).then_inc(S("cy_tap"), 1)
                        dve.wait_ge(S("cy_tap"), 2 * n + (1 if o == 0 else 2))
                    dve.wait_ge(S("ulo_ready"), hid + n + 1)
                    dve.tensor_tensor(ut[:, n % 2, :], cy[:, n % 2, :, :].rearrange("p v t -> p (v t)"),
                                      ps[:, 3 * (n % 2), :], ALU.mult).then_inc(S("gated"), 1)
                    if n < MOD_FIRST:
                        split_lo(dve, first + 8)
                mod_finish(dve, 2)

            def attn_dve(c):
                b, hid = c["unit"], c["hid"]
                for n in range(12):
                    split_lo(dve, b + n + 2)
                dve.wait_ge(S("w_perm"), 1)
                dve.wait_ge(S("atab_loaded"), 16)
                for n in range(5):
                    dst = AK[:, :, 0:T] if n == 0 else AQ[:, 2 * n - 2:2 * n, :]
                    cs = ropeW[0 if n == 0 else 2].unsqueeze(1).broadcast_to([P, 2, T])
                    sn = ropeW[1 if n == 0 else 3].unsqueeze(1).broadcast_to([P, 2, T])
                    dve.tensor_tensor(rp1[:, n % 2], dst, cs, ALU.mult).then_inc(S("w_rp"), 1)
                    dve.tensor_tensor(rp2[:, n % 2], ps[:, n, :].rearrange("p (a t) -> p a t", a=2), sn,
                                      ALU.mult).then_inc(S("w_rp"), 1)
                    dve.wait_ge(S("w_rp"), 2 * n + 2)
                    dve.tensor_tensor(dst, rp1[:, n % 2], rp2[:, n % 2], ALU.add).then_inc(S("w_rope"), 1)

                def top(n):
                    qb = n % 2
                    sk = VEC["sink"] + 2 * (n // 4) + n // 2 % 2
                    dve.wait_ge(S("w_s"), n + 1)
                    if n >= 2:
                        dve.wait_ge(S("w_e"), 2 * (n - 1))
                    dve.tensor_tensor(sw[:, n % 2, :], ps[:, SCORE_BANK[n % 4], :], bandW[:, qb, :], ALU.add).then_inc(S("w_sb"), 1)
                    dve.wait_ge(S("w_sb"), n + 1)
                    dve.tensor_reduce(aw[:, n % 2, 0:1], sw[:, n % 2, :], AXX, ALU.max).then_inc(S("w_mx"), 1)
                    dve.wait_ge(S("w_mx"), n + 1)
                    dve.tensor_scalar(aw[:, n % 2, 1:2], aw[:, n % 2, 0:1], vec[:, sk:sk + 1], -1.0, ALU.max,
                                      ALU.mult).then_inc(S("w_nm"), 1)

                def norm(n):
                    dve.wait_ge(S("w_e"), 2 * n + 2)
                    dve.tensor_tensor(aw[:, n % 2, 4:5], aw[:, n % 2, 2:3], aw[:, n % 2, 3:4],
                                      ALU.add).then_inc(S("w_sum"), 1)
                    dve.wait_ge(S("w_sum"), n + 1)
                    dve.reciprocal(aw[:, n % 2, 5:6], aw[:, n % 2, 4:5]).then_inc(S("w_rec"), 1)
                    dve.wait_ge(S("w_rec"), n + 1)
                    if n >= 2:
                        dve.wait_ge(S("w_tr"), n - 1)
                    dve.tensor_scalar(pn[:, n % 2, :], pw[:, n % 2, :], aw[:, n % 2, 5:6], None,
                                      ALU.mult).then_inc(S("w_pn"), 1)

                def head_out(cc):
                    dve.wait_ge(S("w_pv"), 2 * cc + 2)
                    dve.wait_ge(S("ulo_ready"), hid + cc + 1)
                    dve.tensor_copy(ut[:, cc % 2, 0:T], ps[:, 4 + cc % 2, 0:T]).then_inc(S("gated"), 1)

                top(0)
                for n in range(32):
                    if n + 1 < 32:
                        top(n + 1)
                    norm(n)
                    if n % 4 == 2 and n > 4:
                        head_out(n // 4 - 1)
                head_out(7)


            def mix_dve(c):
                b, l, hid = c["unit"], c["l"], c["hid"]
                V = lambda name, i=0: vec[:, VEC[f"{name}{l}"] + i:VEC[f"{name}{l}"] + i + 1]

                def need(name, per, k):
                    dve.wait_ge(S(name), per * l + k)

                step = [steps_before[0]]

                def then(ins):
                    ins.then_inc(S("dve_step"), 1)
                    step[0] += 1
                    dve.wait_ge(S("dve_step"), step[0])

                bb = EB[:, LEVELS, :]
                for n in range(N_IN):
                    split_lo(dve, b + n + 2)
                    dve.wait_ge(S("unit_done"), b + n + 1)
                    if n == B_Q:
                        dve.scalar_tensor_tensor(Z[:, n, :], ps[:, n % 4, 0:T], 32 ** -0.5, rstd[:, 0:T], ALU.mult,
                                                 ALU.mult).then_inc(S("m_evac"), 1)
                    else:
                        dve.tensor_tensor(Z[:, n, :], ps[:, n % 4, 0:T], rstd[:, 0:T], ALU.mult).then_inc(S("m_evac"), 1)
                    if n == 5:
                        need("c_sig", 1, 1)
                        dve.memset(hp[:, :, 0:KTAPS - 1], 0.0)
                        dve.tensor_tensor(hp[:, :, KTAPS - 1:], Z[:, C_A:C_A + 2, :], Z[:, C_G:C_G + 2, :],
                                          ALU.mult).then_inc(S("hp_ready"), 1)
                    elif n == 11:
                        need("b_gate", 1, 1)
                        dve.tensor_scalar(G1, ps[:, 4, 0:T], V("bg"), None, ALU.add).then_inc(S("b_g"), 1)
                        need("b_g", 1, 1)
                        dve.memset(AT[:, :, :], 0.0).then_inc(S("b_zero"), 1)
                    elif n == 14:
                        need("b_a", 3, 3)
                        then(dve.tensor_scalar(G1, G1, 0.0, None, ALU.min))
                        then(dve.tensor_tensor(G1, G1, G2, ALU.subtract))
                        dve.wait_ge(S("mtab_loaded"), 16 * (l + 1))
                        then(dve.tensor_tensor_scan(bb, scanm, G1, 0.0, ALU.mult, ALU.add))
                    elif n == 15:
                        for v in range(LEVELS):
                            s = 32 >> v
                            w = bb.rearrange("p (n a s) -> p n a s", a=2, s=s)
                            e = EB[:, v, :].rearrange("p (n a s) -> p n a s", a=2, s=s)
                            mid = w[:, :, 0, s - 1:s].broadcast_to([P, T // (2 * s), s])
                            dve.tensor_tensor(e[:, :, 0, :], mid, w[:, :, 0, :], ALU.subtract)
                            dve.tensor_tensor(e[:, :, 1, :], w[:, :, 1, :], mid, ALU.subtract)
                        w = bb.rearrange("p (n s) -> p n s", s=64)
                        dve.tensor_tensor(EB[:, LEVELS + 1, :].rearrange("p (n s) -> p n s", s=64),
                                          w[:, :, 63:64].broadcast_to([P, 4, 64]), w, ALU.subtract).then_inc(S("b_e"), 1)
                    elif n == 17:
                        need("b_p", 1, 1)
                        dve.tensor_tensor(QP[:, :, :], Z[:, B_Q:B_Q + 1, :].broadcast_to([P, LEVELS + 1, T]),
                                          EB[:, 0:LEVELS + 1, :], ALU.mult)
                    elif n == 18:
                        dve.tensor_tensor(KP[:, 0:LEVELS, :], Z[:, B_K:B_K + 1, :].broadcast_to([P, LEVELS, T]),
                                          EB[:, 0:LEVELS, :], ALU.mult)
                        dve.tensor_tensor(KP[:, LEVELS, :], Z[:, B_K, :], EB[:, LEVELS + 1, :], ALU.mult).then_inc(S("b_qk"), 1)
                    elif n == 20:
                        need("m_rt", 1, 1)
                        then(dve.reciprocal(rm[:, 0:2 * T], rm[:, 0:2 * T]))
                    elif n == 21:
                        for m in range(3):
                            r = rm[:, T:2 * T] if m == 2 else rm[:, 0:T]
                            g = V("dkva") if m == 2 else V("dqa", m)
                            ins = dve.scalar_tensor_tensor(cnf[:, m, :], Z[:, D_Q + m, :], g, r, ALU.mult, ALU.mult)
                        then(ins)
                    elif n == 22:
                        then(dve.tensor_copy(cn_hi[:, :, :], cnf[:, :, :]))
                        dve.tensor_tensor(cn_lo[:, :, :], cnf[:, :, :], cn_hi[:, :, :], ALU.subtract).then_inc(S("d_cn"), 1)

                def index_add(n):
                    qb, h = n // 8, n % 8
                    kc = P * (qb + 1)
                    acc, wcol = SCI(qb)[:, 0:kc], iw[:, qb, h:h + 1]
                    need("i_r", 16, n + 1)
                    if h == 0:
                        dve.tensor_scalar(acc, RI(n)[:, 0:kc], wcol, None, ALU.mult).then_inc(S("i_a"), 1)
                    else:
                        dve.scalar_tensor_tensor(acc, RI(n)[:, 0:kc], wcol, acc, ALU.mult, ALU.add).then_inc(S("i_a"), 1)
                    need("i_a", 16, n + 1)

                def topk_rounds(qb, rounds):
                    kc = P * (qb + 1)
                    k0 = P if qb == 0 else 0
                    if rounds[0] == 0:
                        then(dve.tensor_tensor(SCI(qb)[:, 0:kc], SCI(qb)[:, 0:kc], caus1[:, k0:k0 + kc], ALU.mult))
                        then(dve.tensor_tensor(WK(0)[:, 0:kc], SCI(qb)[:, 0:kc], caus0[:, k0:k0 + kc], ALU.add))
                    for it in rounds:
                        then(dve.max(m8[:, it % 2, :], WK(it % 2)[:, 0:kc]))
                        then(dve.match_replace(WK(1 - it % 2)[:, 0:kc], m8[:, it % 2, :], WK(it % 2)[:, 0:kc], -3.3e38))

                def topk_bias(qb):
                    kc = P * (qb + 1)
                    k0 = P if qb == 0 else 0
                    then(dve.tensor_scalar(SEL[:, 0:kc], WK(0)[:, 0:kc], -3.3e38, None, ALU.is_equal))
                    then(dve.tensor_tensor(SEL[:, 0:kc], SEL[:, 0:kc], caus1[:, k0:k0 + kc], ALU.mult))
                    then(dve.tensor_scalar(BI(qb)[:, 0:kc], SEL[:, 0:kc], 1.0, -NEG, ALU.subtract, ALU.mult))

                def sparse_norm(n):
                    r = slice((2 + 2 * n) * T, (4 + 2 * n) * T)
                    then(dve.reciprocal(rm[:, r], rm[:, r]))
                    z = Z[:, A_Q + 2 * n:A_Q + 2 * n + 2, :]
                    dve.scalar_tensor_tensor(z, z, V("ak") if n else V("aq"), rm[:, r].rearrange("p (a t) -> p a t", a=2),
                                             ALU.mult, ALU.mult).then_inc(S("a_n"), 1)

                for v in range(LEVELS + 1):
                    if v == 0:
                        need("m_rta", 1, 1)
                        sparse_norm(0)
                    elif v <= TT:
                        need("i_w", 1, 1)
                        for n in range(8 * (v - 1), 8 * v):
                            index_add(n)
                    elif v == 3:
                        need("c_tap", 2 * KTAPS, 2 * KTAPS)
                        topk_rounds(0, range(0, 4))
                    elif v == 4:
                        need("b_st", 1, 1)
                        for k in range(3):
                            ins = dve.tensor_tensor(ST[:, k, :], ps[:, (7, 4, 5)[k], 0:2 * P], bmask, ALU.mult)
                        then(ins)
                        for k in (1, 2):
                            e = EB[:, LEVELS, 64 * k + 63:64 * k + 64]
                            dve.scalar_tensor_tensor(ST[:, k, :], ST[:, k - 1, :], e, ST[:, k, :], ALU.mult,
                                                     ALU.add).then_inc(S("b_s"), 1)
                            need("b_s", 2, k)
                        need("c_rt", 1, 1)
                        then(dve.reciprocal(rm[:, 6 * T:7 * T], rm[:, 6 * T:7 * T]))
                        for ch in range(2):
                            ins = dve.scalar_tensor_tensor(hc[:, ch, :], hc[:, ch, :], V("cn", ch), rm[:, 6 * T:7 * T],
                                                           ALU.mult, ALU.mult)
                        ins.then_inc(S("c_n"), 1)
                    elif v == 5:
                        topk_rounds(0, range(4, 8))
                        topk_bias(0)
                    elif v == 6:
                        topk_rounds(1, range(0, 4))
                    need("b_lv", LEVELS + 1, v + 1)
                    need("b_at", LEVELS + 1, v) if v else need("b_zero", 1, 1)
                    mask = levm[:, v:v + 1, :].bitcast(U32).broadcast_to([P, 4, T])
                    dve.copy_predicated(AT[:, :, :], mask, ps[:, 0:4, 0:T]).then_inc(S("b_at"), 1)
                need("d_rt", 1, 1)
                dve.reciprocal(rm[:, 0:2 * T], rm[:, 0:2 * T]).then_inc(S("d_rr"), 1)
                need("c_silu", 1, 1)
                for ch in range(2):
                    dve.wait_ge(S("ulo_ready"), hid + ch + 1)
                    dve.tensor_copy(ut[:, ch, 0:T], hc[:, ch, :]).then_inc(S("gated"), 1)
                need("b_oc", 1, 1)
                dve.tensor_tensor(OB[:, :, 64:T], OB[:, :, 64:T], ps[:, 5, :].rearrange("p (a t) -> p a t", a=2)[:, :, 64:T],
                                  ALU.add).then_inc(S("b_oi"), 1)
                need("d_rb", 1, 1)
                for n, x in enumerate((DQ, DK)):
                    dve.scalar_tensor_tensor(x[0:96, :, :], x[0:96, :, :], (V("dk") if n else V("dq"))[0:96, :],
                                             ps[0:96, 0:4, T * n:T * (n + 1)], ALU.mult, ALU.mult).then_inc(S("d_n"), 1)
                need("b_rt", 1, 1)
                need("b_oi", 1, 1)
                then(dve.reciprocal(rm[:, 6 * T:8 * T], rm[:, 6 * T:8 * T]))
                then(dve.scalar_tensor_tensor(OB[:, :, :], OB[:, :, :], V("bo"),
                                              rm[:, 6 * T:8 * T].rearrange("p (a t) -> p a t", a=2), ALU.mult, ALU.mult))
                need("b_silu", 1, 1)
                for ch in range(2):
                    dve.wait_ge(S("ulo_ready"), hid + 2 + ch + 1)
                    dve.tensor_tensor(ut[:, ch, 0:T], OB[:, ch, :], Z[:, B_R + ch, :], ALU.mult).then_inc(S("gated"), 1)
                dve.wait_ge(S("gated"), hid + 4)

                split_lo(dve, b + N_IN + 2)
                split_lo(dve, b + N_IN + 3)
                need("d_n", 2, 2)
                need("d_perm", 1, 1)
                for n, x in enumerate((DQ, DK)):
                    then(dve.tensor_tensor(dt1[0:96, :, :], ps[0:96, 2 * n:2 * n + 2, :].rearrange("p a (b t) -> p (a b) t", b=2),
                                           SD[0:96, :].unsqueeze(1).broadcast_to([96, 4, T]), ALU.mult))
                    then(dve.tensor_tensor(x[0:96, :, :], x[0:96, :, :], CD[0:96, :].unsqueeze(1).broadcast_to([96, 4, T]),
                                           ALU.mult))
                    dve.tensor_tensor(x[0:96, :, :], x[0:96, :, :], dt1[0:96, :, :], ALU.add).then_inc(S("d_r"), 1)
                    need("d_r", 2, n + 1)

                def top(k):
                    qb = k % TT
                    kc, k0 = P * (qb + 1), P * (1 - qb)
                    lg, m = LG(k)[:, :, 0:kc], am[:, k % 2, :]
                    need("s_s", 4, k + 1)
                    b0 = 4 * (k % 2)
                    src = ps[:, b0:b0 + 2, :].rearrange("p a (b t) -> p (a b) t", b=2)[:, :, 0:kc]
                    if k < TT:
                        then(dve.scalar_tensor_tensor(lg, src, 96 ** -0.5, caus0[:, k0:k0 + kc].unsqueeze(1).broadcast_to([P, 4, kc]),
                                                      ALU.mult, ALU.add))
                    else:
                        then(dve.scalar_tensor_tensor(lg, src, 0.125, biasA[:, :, k0:k0 + kc], ALU.mult, ALU.add))
                        then(dve.tensor_tensor(lg, lg, BI(qb)[:, 0:kc].unsqueeze(1).broadcast_to([P, 4, kc]), ALU.add))
                    then(dve.tensor_reduce(m[:, 0:4], lg, AXX, ALU.max))
                    dve.tensor_scalar(m[:, 4:8], m[:, 0:4], -1.0, None, ALU.mult).then_inc(S("s_nm"), 1)

                def normalise(k):
                    kc, m = P * (k % TT + 1), am[:, k % 2, :]
                    need("s_e", 4, k + 1)
                    then(dve.reciprocal(m[:, 12:16], m[:, 8:12]))
                    for h in range(4):
                        ins = dve.tensor_scalar(PR(k)[:, h, 0:kc], PR(k)[:, h, 0:kc], m[:, 12 + h:13 + h], None, ALU.mult)
                    ins.then_inc(S("s_p"), 1)

                def values_out(a):
                    need("s_pv", 4, 2 * a + 2)
                    for ch in range(2):
                        dve.wait_ge(S("ulo_ready"), hid + 4 + 2 * a + ch + 1)
                        dve.tensor_copy(ut[:, ch, 0:T], ps[:, 6 + a, T * ch:T * (ch + 1)]).then_inc(S("gated"), 1)

                dve.wait_ge(S("bias_loaded"), 16)
                top(0)
                sparse_norm(1)
                top(1)
                normalise(0)
                topk_rounds(1, range(4, 8))
                topk_bias(1)
                top(2)
                normalise(1)
                top(3)
                normalise(2)
                normalise(3)
                values_out(0)
                values_out(1)
                steps_before[0] = step[0]

            dve.memset(epsc[:, :], EPS)
            dve.memset(zc[:, :], 0.0).then_inc(S("init"), 1)
            dve.wait_ge(S("cs_ready"), 1)
            dve.tensor_tensor(cs[:, :, 2:4], cv[:, :, :], cs[:, :, 0:2], ALU.subtract).then_inc(S("cs_ready"), 1)
            split_lo(dve, 0)
            split_lo(dve, 1)
            for kind, c in PLAN:
                if kind == "mod":
                    with dve.Fori(0, MOD_FIRST) as i:
                        for q in range(4):
                            split_lo(dve, c["unit"] + q + 2, i)
                    dve.wait_ge(S("small_loaded"), 80)
                    dve.tensor_copy(rbb[:, :, :], rl[:, :].unsqueeze(2).broadcast_to([32, 4, P])).then_inc(S("rbb_ready"), 1)
                    mod_finish(dve, 0)
                elif kind == "gu_mod":
                    gu_mod_dve(c)
                    mod_finish(dve, 1 if c["mod"] < MB else 3)
                elif kind == "pre":
                    pre_dve(c)
                elif kind == "pre2":
                    pre2_dve(c)
                elif kind == "gu":
                    (gu_late_dve if c["late"] else gu_dve)(c)
                elif kind == "out":
                    out_dve(c)
                elif kind == "post":
                    post_dve(c)
                elif kind == "add":
                    add_dve(c)
                elif kind == "conv":
                    conv_dve(c)
                elif kind == "attn":
                    attn_dve(c)
                elif kind == "mix":
                    mix_dve(c)

        @block.gpsimd
        def _(pool):
            pool.memset(stepper[:, 2:3], 0.0).then_inc(S("mod_evac"), 1)
            pool.memset(stepper[:, 3:4], 0.0).then_inc(S("mod_stored"), 1)
            pool.memset(stepper[:, 0:1], 0.0).then_inc(S("ulo_ready"), 1)
            pool.memset(stepper[:, 1:2], 0.0).then_inc(S("ulo_ready"), 1)

            def pre_pool(c):
                N = c["N"]
                for t in range(DC):
                    if HI[t] == "pool":
                        pool.wait_ge(S("hf_ready"), DC * c["pre"] + t + 1)
                        pool.tensor_scalar(h_hi[:, t, 0:N], hf[:, t, 0:N], 1.0, None, ALU.mult).then_inc(S("hi_by_pool"), 1)

            def post_pool(c):
                N = c["N"]
                pool.wait_ge(S("rstd_ready"), c["norm"] + 1)
                for n in range(POOL_X):
                    t = DC - POOL_X + n
                    pool.wait_ge(S("gy_ready"), DC * c["post"] + t + 1)
                    pool.tensor_tensor(gy[:, t, 0:N], gy[:, t, 0:N], rstd[:, 0:N], ALU.mult).then_inc(S("yp_ready"), 1)
                    pool.wait_ge(S("yp_ready"), POOL_X * c["post"] + n + 1)
                    pool.tensor_tensor(xT[:, t, 0:N], xT[:, t, 0:N], gy[:, t, 0:N], ALU.add).then_inc(S("xp_ready"), 1)

            def depthwise(c):
                l = c["l"]
                cw, cb = VEC[f"cw{l}"], VEC[f"cb{l}"]
                pool.wait_ge(S("hp_ready"), l + 1)
                for ch in range(2):
                    pool.tensor_scalar(hc[:, ch, :], hp[:, ch, 0:T], vec[:, cw + ch:cw + ch + 1], vec[:, cb + ch:cb + ch + 1],
                                       ALU.mult, ALU.add).then_inc(S("c_tap"), 1)

                for n in range(2, 2 * KTAPS):
                    pool.wait_ge(S("c_prod"), 2 * (KTAPS - 1) * l + n - 1)
                    pool.wait_ge(S("c_tap"), 2 * KTAPS * l + n - 1)
                    pool.tensor_tensor(hc[:, n % 2, :], hc[:, n % 2, :], tap(n), ALU.add).then_inc(S("c_tap"), 1)

            def split_hidden(c, k, par, N, hi, lo):
                pool.wait_ge(S("gated"), c["hid"] + k + 1)
                pool.tensor_copy(hi[:, k, 0:N], ut[:, par, 0:N]).then_inc(S("uhi_ready"), 1)
                pool.wait_ge(S("uhi_ready"), c["hid"] + k + 1)
                pool.tensor_tensor(lo[:, k, 0:N], ut[:, par, 0:N], hi[:, k, 0:N],
                                   ALU.subtract).then_inc(S("ulo_ready"), 1)

            for kind, c in PLAN:
                if kind == "pre":
                    pre_pool(c)
                elif kind == "post":
                    post_pool(c)
                elif kind in ("gu", "gu_mod"):
                    pool.wait_ge(S("skew_stored"), 16)
                    with pool.Fori(0, FC // 2) as i:
                        for j in range(2):
                            split_hidden(c, 2 * i + j, j, c["N"], u_hi, u_lo)
                elif kind == "conv":
                    for k in range(DC):
                        split_hidden(c, k, k % 2, c["N"], u_hi, u_lo)
                elif kind == "attn":
                    for k in range(DC):
                        split_hidden(c, k, k % 2, T, h_hi, h_lo)
                elif kind == "mix":
                    depthwise(c)
                    for k in range(DC):
                        split_hidden(c, k, k % 2, T, h_hi, h_lo)


def cols(v):
    v = np.asarray(v)
    return np.ascontiguousarray(v.reshape(-1, P).T)


def in_units(w, heads=None):
    k, n = w.shape
    return w.reshape(k // P, P, n // P, P).transpose(2, 1, 0, 3).reshape(n // P, P, k)


def out_units(w):
    return w.reshape(-1, P, D)


def head_of(chunk, half):
    return (2 * (chunk // 4) + half) * 4 + chunk % 4


def weight_stream(a):
    units = []
    HD = 64

    def ffn(gu, down):
        g, u = in_units(gu[:, :DFF]), in_units(gu[:, DFF:])
        units.extend([np.stack([g, u], 1).reshape(2 * FC, P, D), out_units(down)])

    def ffn3(gate, up, down):
        units.extend([np.stack([in_units(gate), in_units(up)], 1).reshape(2 * FC, P, D), out_units(down)])

    def mod_blocks(l):
        return a["w_mod"][l].reshape(4, 2, P, MB, 512).transpose(3, 0, 2, 1, 4).reshape(MB, 4, P, D)

    def gu_mod(l, gu, down):
        gu = np.stack([in_units(gu[:, :DFF]), in_units(gu[:, DFF:])], 1).reshape(MOD_LOOP, 4, P, D)
        units.extend([np.stack([gu, mod_blocks(l)[MOD_FIRST:]], 2).reshape(-1, P, D), out_units(down)])

    units.append(mod_blocks(0)[:MOD_FIRST].reshape(-1, P, D))
    for l in range(2):
        if l == 0:
            gu_mod(0, a["ffn_w_gu"][0, 0], a["ffn_w_down"][0, 0])
            w = in_units(a["conv_w_in"][0]).reshape(3, DC, P, D).transpose(1, 0, 2, 3)
            for n in range(DC):
                if n < MOD_FIRST:
                    m = mod_blocks(1)[n]
                    units.append(np.stack([w[n][0], m[0], w[n][1], m[1], w[n][2], m[2], m[3]]))
                else:
                    units.append(w[n])
            units.append(out_units(a["conv_w_out"][0]))
            gu_mod(1, a["ffn_w_gu"][0, 1], a["ffn_w_down"][0, 1])
        else:
            ffn(a["ffn_w_gu"][l, 0], a["ffn_w_down"][l, 0])
            w = a["attn_w_qkv"][0]
            order = [head_of(c, h) for c in range(8) for h in range(2)]
            q = w[:, :1024].reshape(D, 16, HD)[:, order].reshape(D, 1024)
            wo = a["attn_w_o"][0].reshape(16, HD, D)[order].reshape(1024, D)
            units.extend([in_units(w[:, 1024:]), in_units(q), out_units(wo)])
            ffn(a["ffn_w_gu"][l, 1], a["ffn_w_down"][l, 1])
    for l in range(2):
        ffn3(a["ffn1_gate_2"][l], a["ffn1_up_2"][l], a["ffn1_down_2"][l])
        w = a["w_in_2"][l]
        z = np.zeros((D, P), w.dtype)

        def put(at, first, width, n=1):
            m = z.copy()
            for j in range(n):
                m[:, at + j * width:at + (j + 1) * width] = w[:, first:first + width]
            return m

        parts = [w[:, 1848:2360], w[:, 1064:1576], put(0, 1576, 16), w[:, 1592:1848], w[:, 2360:2744],
                 put(64, 2744, 32), w[:, 0:1024], put(0, 1024, 32, 4), put(0, 1056, 8)]
        units.append(in_units(np.concatenate(parts, 1)))
        uq = np.zeros((2, P, 4, P), w.dtype)
        uq[..., :96] = a["d_uq_2"][l].reshape(2, P, 4, 96)
        units.append(uq.transpose(1, 0, 2, 3).reshape(1, P, D))
        ukv = np.zeros((P, D), w.dtype)
        ukv[:, :512] = a["d_ukv_2"][l]
        units.append(ukv[None])
        units.append(out_units(a["w_out_2"][l].reshape(4, 256, D)[ORDER].reshape(1024, D)))
        ffn3(a["ffn2_gate_2"][l], a["ffn2_up_2"][l], a["ffn2_down_2"][l])
    return np.concatenate(units, 0)


ORDER = [2, 1, 3, 0]


def vectors(a):
    v = np.zeros((P, NVEC), np.float32)

    def put(name, m):
        v[:, VEC[name]:VEC[name] + m.shape[1]] = m

    put("g1", cols(a["norm_g"]))
    put("g2", cols(np.stack([a["ffn1_norm_2"], a["mix_norm_2"], a["ffn2_norm_2"]], 1)))
    put("convw", cols(a["conv_w"][0]))
    put("bmod", cols(a["b_mod"]))
    put("sink", np.broadcast_to(a["attn_sink"][0][[head_of(c, h) for c in range(8) for h in range(2)]], (P, 16)))
    for l in range(2):
        put(f"aq{l}", np.tile(a["a_q_norm_2"][l], 2)[:, None])
        put(f"ak{l}", np.tile(a["a_k_norm_2"][l], 2)[:, None])
        put(f"bg{l}", a["b_gate_bias_2"][l][:, None])
        put(f"bo{l}", np.tile(a["b_out_norm_2"][l], 2)[:, None])
        put(f"cw{l}", cols(a["c_dw_w_2"][l][:, 0]))
        put(f"cb{l}", cols(a["c_dw_b_2"][l]))
        put(f"cn{l}", cols(a["c_norm_2"][l]))
        put(f"dqa{l}", cols(a["d_qa_norm_2"][l]))
        put(f"dkva{l}", cols(a["d_kva_norm_2"][l]))
        for n in "qk":
            v[:96, VEC[f"d{n}{l}"]] = a[f"d_{n}_norm_2"][l]
    return v


def rotation(first, n, half):
    r = np.zeros((P, P), np.float32)
    for g in range(n):
        for i in range(half):
            p = first + 2 * half * g + i
            r[p + half, p] = -1.0
            r[p, p + half] = 1.0
    return r


def tables():
    f = np.float32
    one = np.ones((P, P), f)
    p = np.arange(P)
    b64 = (p[:, None] // 64 == p[None] // 64).astype(f)
    o96 = np.zeros((P, P), f)
    o96[:96] = 1.0
    k = np.arange(T)
    caus = ((p[:, None] + P) >= k[None]).astype(f)
    bmask = (p[:, None] // 32 == k[None] // 64).astype(f)
    ctabs = np.concatenate([one, np.eye(P, dtype=f), b64, o96, rotation(0, 4, 16), rotation(64, 1, 16),
                            caus, ((caus - 1) * f(3e38)).astype(f), bmask,
                            np.broadcast_to((np.arange(224) // 32 == 3).astype(f), (P, 224))], 1)
    band = np.zeros((P, 2, 2 * T), f)
    for b in range(2):
        band[:, b, :T] = np.where(np.abs(P * b + p[:, None] - k[None]) <= 128, f(0), f(NEG))
    tok = np.arange(T)
    inv = (f(10000.0) ** (-np.arange(16, dtype=f) / f(16))).astype(f)
    ang = np.stack([(tok // 64).astype(f)[:, None] * inv, (tok % 64).astype(f)[:, None] * inv], 0)
    ang = ang[(p // 32) % 2, :, p % 16]
    C, Sn = np.cos(ang).astype(f), np.sin(ang).astype(f)
    att = np.concatenate([band.reshape(P, -1), C, Sn, C * f(0.125), Sn * f(0.125)], 1)
    ang = tok.astype(f)[None] * inv[p % 16][:, None]
    on = ((p >= 64) & (p < 96))[:, None]
    CD, SD = np.where(on, np.cos(ang), 1).astype(f), np.where(on, np.sin(ang), 0).astype(f)
    lev = []
    j, i = p[:, None], (k % P)[None]
    for s in (32, 16, 8, 4, 2, 1):
        lev.append((j // (2 * s) == i // (2 * s)) & (j // s % 2 == 0) & (i // s % 2 == 1))
    lev.append(j == i)
    lev = np.stack(lev, 1).astype(f).reshape(P, -1)
    scan = np.broadcast_to((k % 64 != 0).astype(f), (P, T))
    mix = np.concatenate([CD, SD, scan, lev], 1)
    dist = np.maximum(255 - np.arange(384), 0)
    large = 16 + (np.log(np.maximum(dist, 1).astype(f) / f(16)) / f(np.log(8.0)) * f(16)).astype(np.int32)
    buck = np.where(dist < 16, dist, np.minimum(large, 31))
    onehot = (np.arange(32)[:, None] == buck[None]).astype(f)
    return [np.ascontiguousarray(m.astype(f)) for m in (ctabs, att, mix, onehot)]


def chunked(x):
    return x.T.reshape(DC, P, -1).transpose(1, 0, 2)


def host(a):
    a = {k: np.asarray(v) for k, v in a.items()}
    ctabs, att, mix, onehot = tables()
    return dict(
        xin=np.ascontiguousarray(np.concatenate([chunked(a["x"][0]), chunked(a["ctx"][0])], 2)),
        wst=weight_stream(a),
        cvec=np.ascontiguousarray(np.stack([cols(a["c"]), cols(a["c_ctx"])], 2)),
        vecs=vectors(a), ctabs=ctabs, attabs=att, mixtabs=mix,
        bup=np.ascontiguousarray(a["b_gate_up_2"].transpose(1, 0, 2)), relb=a["rel_bias_2"], onehot=onehot)


def kernel(**inputs):
    from concourse import bacc
    from concourse.bass_utils import run_bass_kernel_spmd

    arrays = host(inputs)
    nc = bacc.Bacc("TRN2", target_bir_lowering=False, num_devices=1)
    args = [nc.dram_tensor(n, v.shape, mybir.dt.from_np(v.dtype), kind="ExternalInput").ap() for n, v in arrays.items()]
    out = nc.dram_tensor("out", (P, DC, T), F32, kind="ExternalOutput").ap()
    build(nc, *args, out)
    r = run_bass_kernel_spmd(nc, [arrays], core_ids=[0]).results[0]["out"]
    return np.ascontiguousarray(r.transpose(1, 0, 2).reshape(D, T).T)[None]
```
